# Optimizing a Trainium2 kernel written in Bass

```python
import jax, jax.numpy as jnp
from jax import lax
import numpy as np

D_MODEL = 1024
BATCH = 1
SEQ = 512
DEPTH = 2

GRID_W = 64
D_GROUP = 256
N_GROUPS = 4
D_MIX = N_GROUPS * D_GROUP
HEAD_DIM = 64
CONV_A_WIDTH = 31
CONV_B_WIDTH = 3
SWA_Q_HEADS = D_GROUP // HEAD_DIM
SWA_KV_HEADS = 2
SWA_WINDOW = 128
SWA_BLOCK = 128
NA_HEADS = D_GROUP // HEAD_DIM
NA_KH_MAX = 8
NA_KW = 16
ROPE_THETA = 10000.0
EPS = 1e-6
NEG_INF = -1e30

SPLIT_SIZES = (
    D_GROUP, D_GROUP, D_GROUP,
    D_GROUP, D_GROUP, D_GROUP, D_GROUP,
    SWA_Q_HEADS * HEAD_DIM, SWA_KV_HEADS * HEAD_DIM,
    SWA_KV_HEADS * HEAD_DIM, D_GROUP,
    NA_HEADS * HEAD_DIM, NA_HEADS * HEAD_DIM,
    NA_HEADS * HEAD_DIM, D_GROUP,
)
D_IN = sum(SPLIT_SIZES)


def rmsnorm(x, g):
    x32 = x.astype(jnp.float32)
    y = x32 * lax.rsqrt(jnp.mean(x32 * x32, axis=-1, keepdims=True) + EPS)
    return y.astype(x.dtype) * g

def layernorm(x, g, b):
    x32 = x.astype(jnp.float32)
    mu = jnp.mean(x32, axis=-1, keepdims=True)
    xc = x32 - mu
    y = xc * lax.rsqrt(jnp.mean(xc * xc, axis=-1, keepdims=True) + EPS)
    return y.astype(x.dtype) * g + b

def depthwise_conv(x, w):
    width, ch = w.shape
    pad = (width - 1) // 2
    return lax.conv_general_dilated(
        x, w[:, None, :], window_strides=(1,), padding=[(pad, pad)],
        dimension_numbers=("NWC", "WIO", "NWC"), feature_group_count=ch)

def rope(x, pos):
    d = x.shape[-1]
    inv_freq = ROPE_THETA ** (-jnp.arange(0, d, 2, dtype=jnp.float32) / d)
    ang = pos[:, None] * inv_freq[None, :]
    cos = jnp.cos(ang)[None, :, None, :].astype(x.dtype)
    sin = jnp.sin(ang)[None, :, None, :].astype(x.dtype)
    x1, x2 = x[..., : d // 2], x[..., d // 2:]
    return jnp.concatenate([x1 * cos - x2 * sin, x2 * cos + x1 * sin], axis=-1)

def conformer_conv(u, v, conv_w, conv_b, ln_g, ln_b):
    h = u * jax.nn.sigmoid(v)
    h = depthwise_conv(h, conv_w) + conv_b
    h = layernorm(h, ln_g, ln_b)
    return jax.nn.silu(h)

def short_gated_conv(bg, cg, xv, conv_w):
    return bg * depthwise_conv(cg * xv, conv_w)

def window_gqa(q, k, v, sink):
    b, s, hq, d = q.shape
    hkv = k.shape[2]
    g = hq // hkv
    nb = s // SWA_BLOCK
    pos = jnp.arange(s, dtype=jnp.float32)
    q = rope(q, pos)
    k = rope(k, pos)
    qb = q.reshape(b, nb, SWA_BLOCK, hkv, g, d)
    pad = ((0, 0), (SWA_BLOCK, SWA_BLOCK), (0, 0), (0, 0))
    kp = jnp.pad(k, pad).reshape(b, nb + 2, SWA_BLOCK, hkv, d)
    vp = jnp.pad(v, pad).reshape(b, nb + 2, SWA_BLOCK, hkv, d)
    kw = jnp.concatenate([kp[:, :-2], kp[:, 1:-1], kp[:, 2:]], axis=2)
    vw = jnp.concatenate([vp[:, :-2], vp[:, 1:-1], vp[:, 2:]], axis=2)
    scores = jnp.einsum("bnqhgd,bnkhd->bnhgqk", qb, kw).astype(jnp.float32) * (d ** -0.5)
    blk = jnp.arange(nb)[:, None, None]
    qpos = blk * SWA_BLOCK + jnp.arange(SWA_BLOCK)[None, :, None]
    kpos = (blk - 1) * SWA_BLOCK + jnp.arange(3 * SWA_BLOCK)[None, None, :]
    valid = (jnp.abs(kpos - qpos) <= SWA_WINDOW) & (kpos >= 0) & (kpos < s)
    scores = jnp.where(valid[None, :, None, None], scores, NEG_INF)
    sink_col = jnp.broadcast_to(sink.astype(jnp.float32).reshape(1, 1, hkv, g, 1, 1),
                                scores.shape[:-1] + (1,))
    p = jax.nn.softmax(jnp.concatenate([scores, sink_col], axis=-1), axis=-1)[..., :-1]
    o = jnp.einsum("bnhgqk,bnkhd->bnqhgd", p.astype(v.dtype), vw)
    return o.reshape(b, s, hq * d)

def neighborhood_attn(q, k, v, rpb):
    b, s, h, d = q.shape
    rows = s // GRID_W
    kh = min(NA_KH_MAX, rows)
    r = jnp.arange(rows)
    r0 = jnp.clip(r - kh // 2, 0, rows - kh)
    row_idx = r0[:, None] + jnp.arange(kh)[None, :]
    qg = q.reshape(b, rows, GRID_W, h, d)
    kg = jnp.take(k.reshape(b, rows, GRID_W, h, d), row_idx, axis=1)
    vg = jnp.take(v.reshape(b, rows, GRID_W, h, d), row_idx, axis=1)
    scores = jnp.einsum("brqhd,brikhd->brhqik", qg, kg).astype(jnp.float32) * (d ** -0.5)
    c = jnp.arange(GRID_W)
    c0 = jnp.clip(c - NA_KW // 2, 0, GRID_W - NA_KW)
    col_ok = (c[None, :] >= c0[:, None]) & (c[None, :] < c0[:, None] + NA_KW)
    dr = row_idx - r[:, None] + (NA_KH_MAX - 1)
    dc = jnp.clip(c[None, :] - c[:, None], -(NA_KW - 1), NA_KW - 1) + (NA_KW - 1)
    bias = jnp.take(rpb[:, dr], dc, axis=-1)
    bias = bias.transpose(1, 0, 3, 2, 4).astype(jnp.float32)
    scores = jnp.where(col_ok[:, None, :], scores + bias[None], NEG_INF)
    p = jax.nn.softmax(scores.reshape(b, rows, h, GRID_W, kh * GRID_W), axis=-1)
    p = p.reshape(scores.shape).astype(v.dtype)
    o = jnp.einsum("brhqik,brikhd->brqhd", p, vg)
    return o.reshape(b, s, h * d)

def hybrid_layer(x, norm_g, w_in, w_out, conv_a_w, conv_a_b, ln_a_g, ln_a_b,
                 conv_b_w, swa_sink, na_rpb):
    b, s, _ = x.shape
    h = rmsnorm(x, norm_g)
    proj = jnp.einsum("bsd,de->bse", h, w_in)
    split_points = np.cumsum(SPLIT_SIZES)[:-1].tolist()
    (a_u, a_v, a_z,
     b_b, b_c, b_x, b_z,
     c_q, c_k, c_v, c_z,
     d_q, d_k, d_v, d_z) = jnp.split(proj, split_points, axis=-1)
    y_a = conformer_conv(a_u, a_v, conv_a_w, conv_a_b, ln_a_g, ln_a_b) * jax.nn.silu(a_z)
    y_b = short_gated_conv(b_b, b_c, b_x, conv_b_w) * jax.nn.silu(b_z)
    y_c = window_gqa(c_q.reshape(b, s, SWA_Q_HEADS, HEAD_DIM),
                     c_k.reshape(b, s, SWA_KV_HEADS, HEAD_DIM),
                     c_v.reshape(b, s, SWA_KV_HEADS, HEAD_DIM), swa_sink) * jax.nn.silu(c_z)
    y_d = neighborhood_attn(d_q.reshape(b, s, NA_HEADS, HEAD_DIM),
                            d_k.reshape(b, s, NA_HEADS, HEAD_DIM),
                            d_v.reshape(b, s, NA_HEADS, HEAD_DIM), na_rpb) * jax.nn.silu(d_z)
    y = jnp.concatenate([y_a, y_b, y_c, y_d], axis=-1)
    return x + jnp.einsum("bse,ed->bsd", y, w_out)

def first_inputs(seed: int = 0) -> dict:
    key = jax.random.key(seed)
    ks = jax.random.split(key, 12)
    f32 = jnp.float32
    x = jax.random.normal(ks[0], (BATCH, SEQ, D_MODEL), f32)
    norm_g = 1.0 + 0.05 * jax.random.normal(ks[1], (DEPTH, D_MODEL), f32)
    w_in = jax.random.normal(ks[2], (DEPTH, D_MODEL, D_IN), f32) * D_MODEL ** -0.5
    w_out = jax.random.normal(ks[3], (DEPTH, D_MIX, D_MODEL), f32) * D_MIX ** -0.5
    conv_a_w = jax.random.normal(ks[4], (DEPTH, CONV_A_WIDTH, D_GROUP), f32) * CONV_A_WIDTH ** -0.5
    conv_a_b = 0.02 * jax.random.normal(ks[5], (DEPTH, D_GROUP), f32)
    ln_a_g = 1.0 + 0.05 * jax.random.normal(ks[6], (DEPTH, D_GROUP), f32)
    ln_a_b = 0.02 * jax.random.normal(ks[7], (DEPTH, D_GROUP), f32)
    conv_b_w = jax.random.normal(ks[8], (DEPTH, CONV_B_WIDTH, D_GROUP), f32) * CONV_B_WIDTH ** -0.5
    swa_sink = jax.random.normal(ks[9], (DEPTH, SWA_Q_HEADS), f32)
    na_rpb = 0.1 * jax.random.normal(ks[10], (DEPTH, NA_HEADS, 2 * NA_KH_MAX - 1, 2 * NA_KW - 1), f32)
    final_norm_g = 1.0 + 0.05 * jax.random.normal(ks[11], (D_MODEL,), f32)
    return {"x": x, "norm_g": norm_g, "w_in": w_in, "w_out": w_out,
            "conv_a_w": conv_a_w, "conv_a_b": conv_a_b, "ln_a_g": ln_a_g, "ln_a_b": ln_a_b,
            "conv_b_w": conv_b_w, "swa_sink": swa_sink, "na_rpb": na_rpb,
            "final_norm_g": final_norm_g}

def first_block(x, norm_g, w_in, w_out, conv_a_w, conv_a_b, ln_a_g, ln_a_b,
              conv_b_w, swa_sink, na_rpb, final_norm_g):
    for l in range(DEPTH):
        x = hybrid_layer(x, norm_g[l], w_in[l], w_out[l], conv_a_w[l], conv_a_b[l],
                         ln_a_g[l], ln_a_b[l], conv_b_w[l], swa_sink[l], na_rpb[l])
    return rmsnorm(x, final_norm_g)


POOL_GROUPS = 4
POOL_GROUP_DIM = D_MODEL // 16
POOL_WIDTH = POOL_GROUPS * POOL_GROUP_DIM
POOL_WINDOWS = (2, 4, 8, 16)

MLA_HEADS = 8
MLA_NOPE_DIM = D_MODEL // 16
MLA_ROPE_DIM = D_MODEL // 32
MLA_V_DIM = D_MODEL // 16
MLA_Q_RANK = 3 * D_MODEL // 8
MLA_KV_RANK = D_MODEL // 4
MLA_QK_DIM = MLA_NOPE_DIM + MLA_ROPE_DIM
MLA_WIDTH = MLA_HEADS * MLA_V_DIM
Q_BLOCK = 128

LRU_WIDTH = D_MODEL // 4
LRU_HEADS = 4
LRU_HEAD_DIM = LRU_WIDTH // LRU_HEADS
CONV_WIDTH = 4
LRU_C = 8.0

N_BRANCH = 3
D_FF = 4 * D_MODEL

IN_POOL_END = POOL_WIDTH
IN_Q_END = IN_POOL_END + MLA_Q_RANK
IN_KV_END = IN_Q_END + MLA_KV_RANK + MLA_ROPE_DIM
IN_LRU_END = IN_KV_END + LRU_WIDTH
IN_COLS = IN_LRU_END + N_BRANCH * D_MODEL


def rms_norm(x, g):
    xf = x.astype(jnp.float32)
    y = xf * lax.rsqrt(jnp.mean(xf * xf, axis=-1, keepdims=True) + EPS)
    return (y * g.astype(jnp.float32)).astype(x.dtype)

def rope_tables(seq):
    pos = jnp.arange(seq, dtype=jnp.float32)
    inv = ROPE_THETA ** (-jnp.arange(0, MLA_ROPE_DIM, 2, dtype=jnp.float32) / MLA_ROPE_DIM)
    ang = pos[:, None] * inv[None, :]
    return jnp.cos(ang), jnp.sin(ang)

def apply_rope(x, cos, sin):
    x1, x2 = jnp.split(x.astype(jnp.float32), 2, axis=-1)
    shape = (cos.shape[0],) + (1,) * (x.ndim - 3) + (cos.shape[1],)
    c, s = cos.reshape(shape), sin.reshape(shape)
    return jnp.concatenate([x1 * c - x2 * s, x2 * c + x1 * s], axis=-1).astype(x.dtype)

def pool_mixer(u, w_grp, scale):
    B, S, _ = u.shape
    ug = u.reshape(B, S, POOL_GROUPS, POOL_GROUP_DIM)
    cs0 = jnp.pad(jnp.cumsum(ug.astype(jnp.float32), axis=1), ((0, 0), (1, 0), (0, 0), (0, 0)))
    t = jnp.arange(S, dtype=jnp.int32)[:, None]
    win = jnp.array(POOL_WINDOWS, dtype=jnp.int32)[None, :]
    start = jnp.maximum(t + 1 - win, 0)
    lagged = cs0[:, start, jnp.arange(POOL_GROUPS)[None, :], :]
    count = jnp.minimum(t + 1, win).astype(jnp.float32)[None, :, :, None]
    mixed = ((cs0[:, 1:] - lagged) / count - ug.astype(jnp.float32)).astype(u.dtype)
    y = jnp.einsum('bsgc,gcd->bsgd', mixed, w_grp)
    return y.reshape(B, S, POOL_WIDTH) * scale

def causal_attention(q, k, v):
    B, S, H, Dk = q.shape
    nb = S // Q_BLOCK
    scale = Dk ** -0.5
    qb = q.reshape(B, nb, Q_BLOCK, H, Dk).transpose(1, 0, 2, 3, 4)
    k_pos = jnp.arange(S, dtype=jnp.int32)

    def block(args):
        q_blk, i = args
        s = jnp.einsum('bqhd,bkhd->bhqk', q_blk, k, preferred_element_type=jnp.float32) * scale
        q_pos = i * Q_BLOCK + jnp.arange(Q_BLOCK, dtype=jnp.int32)
        s = jnp.where(k_pos[None, :] <= q_pos[:, None], s, -jnp.inf)
        p = jax.nn.softmax(s, axis=-1).astype(v.dtype)
        return jnp.einsum('bhqk,bkhd->bqhd', p, v)

    o = lax.map(block, (qb, jnp.arange(nb, dtype=jnp.int32)))
    return o.transpose(1, 0, 2, 3, 4).reshape(B, S, H, v.shape[-1])

def mla_mixer(q_lat, kv_lat, g_q, w_q_up, g_kv, w_kv_up, cos, sin):
    B, S, _ = q_lat.shape
    q = (rms_norm(q_lat, g_q) @ w_q_up).reshape(B, S, MLA_HEADS, MLA_QK_DIM)
    q_nope, q_rope = q[..., :MLA_NOPE_DIM], q[..., MLA_NOPE_DIM:]
    c_kv, k_rope = kv_lat[..., :MLA_KV_RANK], kv_lat[..., MLA_KV_RANK:]
    kv = (rms_norm(c_kv, g_kv) @ w_kv_up).reshape(B, S, MLA_HEADS, MLA_NOPE_DIM + MLA_V_DIM)
    k_nope, v = kv[..., :MLA_NOPE_DIM], kv[..., MLA_NOPE_DIM:]
    q_rope = apply_rope(q_rope, cos, sin)
    k_rope = apply_rope(k_rope, cos, sin)
    q = jnp.concatenate([q_nope, q_rope], axis=-1)
    k = jnp.concatenate([k_nope, jnp.broadcast_to(k_rope[:, :, None, :], (B, S, MLA_HEADS, MLA_ROPE_DIM))], axis=-1)
    o = causal_attention(q, k, v)
    return o.reshape(B, S, MLA_WIDTH)

def rg_lru_mixer(u, conv_w, conv_b, w_a, b_a, w_x, b_x, lam):
    B, S, C = u.shape
    u = lax.conv_general_dilated(u, conv_w[:, None, :], window_strides=(1,),
                                 padding=[(CONV_WIDTH - 1, 0)],
                                 dimension_numbers=('NWC', 'WIO', 'NWC'),
                                 feature_group_count=C) + conv_b
    ub = u.reshape(B, S, LRU_HEADS, LRU_HEAD_DIM)
    r = jax.nn.sigmoid(jnp.einsum('bshc,hcd->bshd', ub, w_a).reshape(B, S, C) + b_a)
    i = jax.nn.sigmoid(jnp.einsum('bshc,hcd->bshd', ub, w_x).reshape(B, S, C) + b_x)
    log_a = -LRU_C * r.astype(jnp.float32) * jax.nn.softplus(-lam.astype(jnp.float32))
    a = jnp.exp(log_a)
    b = jnp.sqrt(-jnp.expm1(2.0 * log_a)) * (i * u).astype(jnp.float32)

    def combine(left, right):
        a_l, b_l = left
        a_r, b_r = right
        return a_l * a_r, a_r * b_l + b_r

    _, h = lax.associative_scan(combine, (a, b), axis=1)
    return h.astype(u.dtype)

def second_inputs(seed: int = 0) -> dict:
    key = jax.random.key(seed)
    ks = jax.random.split(key, 26)
    f32 = jnp.float32

    def nrm(k, shape, fan_in):
        return jax.random.normal(k, shape, f32) * (fan_in ** -0.5)

    def gain(k, shape):
        return 1.0 + 0.05 * jax.random.normal(k, shape, f32)

    def small(k, shape):
        return 0.01 * jax.random.normal(k, shape, f32)

    a8 = jax.random.uniform(ks[17], (DEPTH, LRU_WIDTH), f32, minval=0.9, maxval=0.999)
    s = a8 ** (1.0 / LRU_C)
    lru_lambda = jnp.log(s) - jnp.log1p(-s)

    return {
        "x": jax.random.normal(ks[0], (BATCH, SEQ, D_MODEL), f32),
        "g_mix": gain(ks[1], (DEPTH, D_MODEL)),
        "w_in": nrm(ks[2], (DEPTH, D_MODEL, IN_COLS), D_MODEL),
        "w_pool_grp": nrm(ks[3], (DEPTH, POOL_GROUPS, POOL_GROUP_DIM, POOL_GROUP_DIM), POOL_GROUP_DIM),
        "pool_scale": 1.0 + 0.1 * jax.random.normal(ks[4], (DEPTH, POOL_WIDTH), f32),
        "w_pool_proj": nrm(ks[5], (DEPTH, POOL_WIDTH, D_MODEL), POOL_WIDTH),
        "g_q": gain(ks[6], (DEPTH, MLA_Q_RANK)),
        "w_q_up": nrm(ks[7], (DEPTH, MLA_Q_RANK, MLA_HEADS * MLA_QK_DIM), MLA_Q_RANK),
        "g_kv": gain(ks[8], (DEPTH, MLA_KV_RANK)),
        "w_kv_up": nrm(ks[9], (DEPTH, MLA_KV_RANK, MLA_HEADS * (MLA_NOPE_DIM + MLA_V_DIM)), MLA_KV_RANK),
        "w_mla_o": nrm(ks[10], (DEPTH, MLA_WIDTH, D_MODEL), MLA_WIDTH),
        "conv_w": nrm(ks[11], (DEPTH, CONV_WIDTH, LRU_WIDTH), CONV_WIDTH),
        "conv_b": small(ks[12], (DEPTH, LRU_WIDTH)),
        "w_lru_a": nrm(ks[13], (DEPTH, LRU_HEADS, LRU_HEAD_DIM, LRU_HEAD_DIM), LRU_HEAD_DIM),
        "b_lru_a": small(ks[14], (DEPTH, LRU_WIDTH)),
        "w_lru_x": nrm(ks[15], (DEPTH, LRU_HEADS, LRU_HEAD_DIM, LRU_HEAD_DIM), LRU_HEAD_DIM),
        "b_lru_x": small(ks[16], (DEPTH, LRU_WIDTH)),
        "lru_lambda": lru_lambda,
        "w_lru_proj": nrm(ks[18], (DEPTH, LRU_WIDTH, D_MODEL), LRU_WIDTH),
        "b_gate": small(ks[19], (DEPTH, N_BRANCH * D_MODEL)),
        "w_out": nrm(ks[20], (DEPTH, D_MODEL, D_MODEL), D_MODEL),
        "g_ffn": gain(ks[21], (DEPTH, D_MODEL)),
        "w_ff1": nrm(ks[22], (DEPTH, D_MODEL, D_FF), D_MODEL),
        "w_ff2": nrm(ks[23], (DEPTH, D_FF, D_MODEL), D_FF),
        "g_final": gain(ks[24], (D_MODEL,)),
    }

def second_block(x, g_mix, w_in, w_pool_grp, pool_scale, w_pool_proj, g_q, w_q_up, g_kv, w_kv_up,
              w_mla_o, conv_w, conv_b, w_lru_a, b_lru_a, w_lru_x, b_lru_x, lru_lambda, w_lru_proj,
              b_gate, w_out, g_ffn, w_ff1, w_ff2, g_final):
    B, S, D = x.shape
    cos, sin = rope_tables(S)
    for l in range(DEPTH):
        h = rms_norm(x, g_mix[l])
        proj = h @ w_in[l]
        u_pool, q_lat, kv_lat, u_lru, gate_logit = jnp.split(
            proj, [IN_POOL_END, IN_Q_END, IN_KV_END, IN_LRU_END], axis=-1)
        y_pool = pool_mixer(u_pool, w_pool_grp[l], pool_scale[l]) @ w_pool_proj[l]
        y_mla = mla_mixer(q_lat, kv_lat, g_q[l], w_q_up[l], g_kv[l], w_kv_up[l], cos, sin) @ w_mla_o[l]
        y_lru = rg_lru_mixer(u_lru, conv_w[l], conv_b[l], w_lru_a[l], b_lru_a[l],
                             w_lru_x[l], b_lru_x[l], lru_lambda[l]) @ w_lru_proj[l]
        gates = jax.nn.sigmoid(gate_logit + b_gate[l]).reshape(B, S, N_BRANCH, D)
        merged = gates[:, :, 0] * y_pool + gates[:, :, 1] * y_mla + gates[:, :, 2] * y_lru
        x = x + merged @ w_out[l]
        h = rms_norm(x, g_ffn[l])
        x = x + jnp.square(jax.nn.relu(h @ w_ff1[l])) @ w_ff2[l]
    return rms_norm(x, g_final)


def setup_inputs(seed=0):
    out = dict(first_inputs(seed))
    for name, value in second_inputs(seed + 1).items():
        if name != "x":
            out[name + "_2"] = value
    return out


def reference(
    x, norm_g, w_in, w_out, conv_a_w, conv_a_b, ln_a_g, ln_a_b, conv_b_w, swa_sink, na_rpb,
    final_norm_g, g_mix_2, w_in_2, w_pool_grp_2, pool_scale_2, w_pool_proj_2, g_q_2, w_q_up_2,
    g_kv_2, w_kv_up_2, w_mla_o_2, conv_w_2, conv_b_2, w_lru_a_2, b_lru_a_2, w_lru_x_2,
    b_lru_x_2, lru_lambda_2, w_lru_proj_2, b_gate_2, w_out_2, g_ffn_2, w_ff1_2, w_ff2_2,
    g_final_2,
):
    x = first_block(
        x, norm_g, w_in, w_out, conv_a_w, conv_a_b, ln_a_g, ln_a_b, conv_b_w, swa_sink, na_rpb,
        final_norm_g,
    )
    return second_block(
        x, g_mix_2, w_in_2, w_pool_grp_2, pool_scale_2, w_pool_proj_2, g_q_2, w_q_up_2, g_kv_2,
        w_kv_up_2, w_mla_o_2, conv_w_2, conv_b_2, w_lru_a_2, b_lru_a_2, w_lru_x_2, b_lru_x_2,
        lru_lambda_2, w_lru_proj_2, b_gate_2, w_out_2, g_ffn_2, w_ff1_2, w_ff2_2, g_final_2,
    )


_drawn_inputs = setup_inputs


def setup_inputs(seed=0):
    import zlib

    import numpy as np

    out = dict(_drawn_inputs(seed))
    spreads = {}
    factors = {'conv_a_b': 4.096,
     'ln_a_g': 3.239,
     'ln_a_b': 8.0,
     'swa_sink': 8.0,
     'na_rpb': 8.0,
     'g_q_2': 8.0,
     'g_kv_2': 6.788,
     'b_lru_a_2': 48.336,
     'b_lru_x_2': 23.309,
     'b_gate_2': 8.0}
    for name, (base, spread) in spreads.items():
        noise = np.random.default_rng([zlib.crc32(name.encode()), seed]).standard_normal(out[name].shape)
        drawn = base * np.exp(spread * noise) if base else spread * noise
        out[name] = __import__('jax').numpy.asarray(drawn.astype(out[name].dtype))
    for name, factor in factors.items():
        out[name] = (out[name] * factor).astype(out[name].dtype)
    return out
```

```python
from contextlib import ExitStack

import numpy as np

import concourse.bass as bass
from concourse import mybir

F32 = mybir.dt.float32
F32R = mybir.dt.float32r
ALU = mybir.AluOpType
ACT = mybir.ActivationFunctionType

P = 128
S = 512
D = 1024
KT = D // P
DEPTH = 2
EPS = 1e-6
NEG = -8e30
HD = 64
GRID = 64
CONV_A = 31
PAD_A = CONV_A // 2
POOLPAD = 16
U1 = 18
U2 = 62
UNITS = DEPTH * (U1 + U2)

P1 = {}
_n = 0
for _k, _w in (("norm_g", 8), ("conv_a_w", 2 * CONV_A), ("conv_a_b", 2), ("ln_g", 2), ("ln_b", 2),
               ("conv_b_w", 6), ("sink", 4)):
    P1[_k] = _n
    _n += _w
NP1 = _n
P2 = {}
_n = 0
for _k, _w in (("g_mix", 8), ("scale", 2), ("g_lat", 5), ("conv_w", 8), ("conv_b", 2), ("b_a", 2),
               ("b_x", 2), ("lam", 2), ("b_gate", 24), ("g_ffn", 8)):
    P2[_k] = _n
    _n += _w
NP2 = _n


COUNTS = []
SAFE = True


class Count:

    def __init__(self, sem, start, segments):
        self.sem, self.start, self.at_, off = sem, start, {}, 0
        for seg, reps, names in segments:
            for k, name in enumerate(names):
                assert (seg, name) not in self.at_, name
                self.at_[seg, name] = (off + k + 1, len(names))
            off += reps * len(names)
        self.total = off
        COUNTS.append(self)

    def at(self, l, name, seg="", i=0):
        k, step = self.at_[seg, name]
        return l * self.total + i * step + (self.start + k)

    def end(self):
        return self.start + DEPTH * self.total


class Own:

    def __init__(self, sem):
        self.sem, self.base, self.n, self.recent, self.outer = sem, 0, 0, [], []

    def step(self):
        self.n += 1
        self.recent.append((self.sem, self.base + self.n))
        return 1

    def reach(self, sem, value):
        self.recent.append((sem, value))
        return 1

    def event(self, count, l, name, seg="", i=0):
        return self.reach(count.sem, count.at(l, name, seg, i))

    def last(self, behind=0):
        if SAFE: behind = 0
        return self.recent[-1 - behind]

    def enter(self, i, per):
        self.outer.append((self.base, self.n, per))
        self.base, self.n = self.base + self.n + i * per, 0
        self.recent = 3 * [(self.sem, self.base)]

    def leave(self, times):
        base, n, per = self.outer.pop()
        assert self.n == per, f"the body counts {self.n}, not {per}"
        self.base, self.n = base, n + times * per
        self.recent = 3 * [(self.sem, self.base + self.n)]


B1_UNITS = ["dq", "dk", "dv", "dz", "av", "au", "bc", "bx", "cq", "ck", "cz", "bb", "bz", "az",
            "o0", "o1", "o2", "o3"]
B1_CHUNKS = [u + str(c) for u in B1_UNITS for c in range(2)]
B1_COLS = {"dq": 2560, "dk": 2816, "dv": 3072, "dz": 3328, "av": 256, "au": 0, "bc": 1024, "bx": 1280,
           "cq": 1792, "ck": 2048, "cz": 2304, "bb": 768, "bz": 1536, "az": 512}
N_CONST = 5
LN_STEP = 10
ACT_ORDER_1 = 33
ACT_ORDER_2 = 30
ACT_ORDER_H = 9
ACT_ORDER_M = 1
ACT_ORDER_F = 1
DVE_ORDER_1 = 212
DVE_ORDER_2 = 291
DVE_ORDER_H = 49
DVE_ORDER_M = 7
DVE_ORDER_F = 16
STEPS = 8
FILL = {0: "av0", 1: "av1", 2: "au0", 3: "au1", 4: "bc0", 5: "bc1", 6: "bx0", 7: "bx1",
        8: "bb0", 9: "bb1", 10: "bz0", 11: "bz1", 12: "az0", 13: "az1"}
TAPS = {4: 7, 5: 7, 6: 7, 7: 7, "cz0": 10, "cz1": 10, 8: 7, 9: 7}


def b1_splits():
    out = [f"n{k}" for k in range(KT)] + ["dq0", "dq1", "dk0", "dk1", "dv0", "dv1"]
    for i in range(2 * STEPS):
        if i == STEPS:
            out += ["cq0", "cq1", "ck0", "ck1", "ck2", "ck3", "cv"]
        out += [f"pt{i}a", f"pt{i}b"]
        fill = FILL.get(i, "")
        if fill[:2] in ("bz", "az"):
            out.append("y" + fill)
        out.append(f"y{i}")
    return out


def head_names(jj):
    out = [f"q{jj}0", f"k{jj}0", f"k{jj}1", f"v{jj}"]
    for s in range(4):
        out += [f"pt{jj}{s}{b}" for b in ("ab" if s % 2 else "a")]
        if s == 0:
            out.append(f"q{jj}1")
        out.append(f"y{jj}{s}")
    return out


def build(nc, dram):
    COUNTS.clear()
    with ExitStack() as ctx:
        _build(nc, dram, ctx)


def _build(nc, dram, ctx):
    def sem(name):
        return ctx.enter_context(nc.semaphore(name))

    def sb(name, shape, dt=F32, where=ctx):
        return where.enter_context(nc.sbuf_tensor(name, shape, dt))

    def two(name, shape, where=ctx):
        return (sb(name + "_hi", shape, F32R, where), sb(name + "_lo", shape, F32R, where))

    X = sb("X", [P, KT, S])
    H = two("H", [P, KT, S])
    Y = two("Y", [P, KT, S])
    W_raw = sb("W_raw", [P, 2, 2048])
    W = two("W", [P, 2, 2048])
    PRE = sb("PRE", [P, 2, S])
    TMP = sb("TMP", [P, 2, S])
    ident = sb("ident", [P, P])
    ones = sb("ones", [P, P])
    PR = sb("PR", [P, 2, S])
    SM = sb("SM", [P, 16])
    NR = sb("NR", [P, 4])
    spare = sb("spare", [P, 1])
    spare_a = sb("spare_a", [P, 1])
    spare_v = sb("spare_v", [P, 1])
    EPSC = sb("EPSC", [P, 1])
    PARF = sb("PARF", [P, 2 * KT])

    banks = [ctx.enter_context(nc.psum_tensor(f"bank{i}", [P, S], F32)) for i in range(8)]
    G, SC, TB, OB, NB = banks[0:2], banks[2:4], banks[4:6], banks[6], banks[7]

    w_raw = [sem("w_raw0"), sem("w_raw1")]
    w_hi = sem("w_hi")
    w_lo = sem("w_lo")
    consts_in = sem("consts_in")
    start = sem("start")
    par_in = sem("par_in")
    bias_in = [sem("bias_in0"), sem("bias_in1")]
    rope_in = sem("rope_in")
    x_out = sem("x_out")
    ln_in, ln_out, ls_ready = sem("ln_in"), sem("ln_out"), sem("ls_ready")
    act_step, dve_step, pool_step = sem("act_step"), sem("dve_step"), sem("pool_step")

    ACC_N = "acc"

    class Block:
        pass

    b1 = Block()
    b1.done = Count(sem("proj_done1"), 1, [("", 1, B1_CHUNKS)])
    split_names = b1_splits()
    b1.hi = Count(sem("split_hi1"), 0, [("", 1, split_names)])
    b1.lo = Count(sem("split_lo1"), 0, [("", 1, split_names)])
    b1.pre = Count(sem("pre1"), 0, [("", 1, [n for n in split_names if n[0] in "ny"
                                              or n in ("cq0", "cq1", "ck0")])])
    freed = [c for c in B1_CHUNKS if c[:2] not in ("dq", "dk", "dv", "av", "bc") and c != "ck1"]
    b1.free = Count(sem("proj_free1"), 1, [("", 1, freed)])
    b1.aux = Count(sem("act_aux1"), 0, [("", 1, ["dz0", "dz1", "av0", "av1", "bc0", "bc1", "cz0", "cz1",
                                                 "ln0", "ln1", "bz0", "bz1", "az0", "az1"])])
    steps = [str(i) for i in range(2 * STEPS)]
    b1.sc = Count(sem("scores1"), 0, [("", 1, steps)])
    b1.red = Count(sem("rowmax1"), 0, [("", 1, steps)])
    b1.ex = Count(sem("exp1"), 0, [("", 1, steps)])
    b1.pn = Count(sem("probs1"), 0, [("", 1, steps)])
    b1.tr = Count(sem("transposed1"), 0, [("", 1, steps)])
    b1.pv = Count(sem("attended1"), 1, [("", 1, steps)])
    norms1 = ["n", "mean", "var"]
    b1.acc = Count(sem("norm_acc1"), 0, [("", 1, norms1)])
    b1.ss = Count(sem("norm_sum1"), 0, [("", 1, norms1)])
    b1.rt = Count(sem("norm_root1"), 0, [("", 1, ["n", "var"])])
    b1.dg = Count(sem("norm_diag1"), 0, [("", 1, ["n", "var"])])
    b1.bc = Count(sem("norm_spread1"), 0, [("", 1, ["n", "var"])])
    b1.layer = Count(sem("layer1"), 1, [("", 1, ["end"])])

    b2 = Block()
    lats = ["q00", "q01", "q2", "kr", "kv0", "kv1"]
    pair_chunks = [f"{n}{jj}{s}" for jj in range(2) for n, s in
                   (("q", 0), ("k", 0), ("v", 0), ("q", 1), ("g", 0), ("g", 1), ("g", 2), ("g", 3))]
    mid = ["pl0", "pl1", "lr0", "lr1"]
    mrg_chunks = ["t0", "t1"]
    outs = [f"o{m}" for m in range(KT)]
    ffn_chunks = [f"u{m}" for m in range(KT)] + [f"d{m}" for m in range(KT)]
    b2.done = Count(sem("proj_done2"), 1, [("", 1, lats), ("h", 2, pair_chunks), ("mid", 1, mid),
                                            ("m", 4, mrg_chunks), ("out", 1, outs), ("f", 4, ffn_chunks)])
    sp = [("", 1, [f"n{k}" for k in range(KT)] + [f"l{k}" for k in range(5)] + ["kr"]),
          ("h", 2, head_names(0) + head_names(1)),
          ("mid", 1, ["pm0", "pm1", "py0", "py1", "uc0", "uc1", "lh0", "lh1"]),
          ("m", 4, ["b0", "b1"]),
          ("n2", 1, [f"e{k}" for k in range(KT)]),
          ("f", 4, [f"u{m}" for m in range(KT)])]
    b2.hi = Count(sem("split_hi2"), 0, sp)
    b2.lo = Count(sem("split_lo2"), 0, sp)
    qnames = [f"q{jj}{a}" for jj in range(2) for a in range(2)]
    b2.pre = Count(sem("pre2"), 0, [("", 1, [f"n{k}" for k in range(KT)] + [f"l{k}" for k in range(5)] + ["kr"]),
                                     ("h", 2, qnames),
                                     ("mid", 1, ["pm0", "pm1", "py0", "py1", "uc0", "uc1", "lh0", "lh1"]),
                                     ("m", 4, ["b0", "b1"]),
                                     ("n2", 1, [f"e{k}" for k in range(KT)]),
                                     ("f", 4, [f"u{m}" for m in range(KT)])])
    b2.free = Count(sem("proj_free2"), 2, [("", 1, lats), ("h", 2, qnames),
                                            ("mid", 1, mid), ("out", 1, outs),
                                            ("f", 4, [f"d{m}" for m in range(KT)])])
    b2.aux = Count(sem("act_aux2"), 2, [("h", 2, [c for c in pair_chunks if c[0] == "g"]),
                                         ("mid", 1, ["sp", "ra0", "rx0", "lt0", "la0", "sq0", "rt0",
                                                     "ra1", "rx1", "lt1", "la1", "sq1", "rt1"]),
                                         ("m", 4, mrg_chunks),
                                         ("f", 4, [f"u{m}" for m in range(KT)])])
    ps = [f"{jj}{s}" for jj in range(2) for s in range(4)]
    b2.sc = Count(sem("scores2"), 0, [("h", 2, ps)])
    b2.red = Count(sem("rowmax2"), 1, [("h", 2, ps)])
    b2.ex = Count(sem("exp2"), 0, [("h", 2, ps)])
    b2.pn = Count(sem("probs2"), 0, [("h", 2, ps)])
    b2.tr = Count(sem("transposed2"), 0, [("h", 2, ps)])
    b2.pv = Count(sem("attended2"), 1, [("h", 2, ps)])
    b2.sm = Count(sem("small2"), 0, [("", 1, ["p0", "p1", "a0", "x0", "a1", "x1"])])
    b2.br = Count(sem("branches2"), 1, [("m", 4, ["0", "1"])])
    b2.brf = Count(sem("merged2"), 2, [("m", 4, ["0", "1"])])
    b2.lru = Count(sem("lru_ready2"), 0, [("", 1, ["sp", "c0", "c1"])])
    norms2 = ["n", "q", "kv", "e"]
    b2.acc = Count(sem("norm_acc2"), 0, [("", 1, norms2)])
    b2.ss = Count(sem("norm_sum2"), 0, [("", 1, norms2)])
    b2.rt = Count(sem("norm_root2"), 0, [("", 1, norms2)])
    b2.dg = Count(sem("norm_diag2"), 0, [("", 1, norms2)])
    b2.bc = Count(sem("norm_spread2"), 0, [("", 1, norms2)])
    b2.layer = Count(sem("layer2"), 1, [("", 1, ["end"])])

    bf = Block()
    bf.acc, bf.ss, bf.rt, bf.dg, bf.bc = (Count(sem(f"norm_{n}F"), 0, [("", 1, ["n"])])
                                          for n in ("acc", "sum", "root", "diag", "spread"))
    final = Count(sem("final"), 0, [("", 1, [str(k) for k in range(KT)])])

    m1 = ExitStack()
    with m1:
        def t1(name, shape, dt=F32):
            return sb(name, shape, dt, m1)
        ACC1 = t1("ACC1", [P, S])
        PT1 = two("PT1", [P, 4, 256], m1)
        AQ, AK, AV = two("AQ", [P, 2, S], m1), two("AK", [P, 2, S], m1), two("AV", [P, 4, 256], m1)
        BT = t1("BT", [P, 2, 14, GRID])
        ROPE = BT[:, :, :, :].rearrange("p a b c -> p (a b c)")
        COS1, SIN1 = ROPE[:, 0:S], ROPE[:, S:2 * S]
        NM = t1("NM", [P, GRID])
        ZB = t1("ZB", [P, 2, S])
        HA = t1("HA", [P, 2, S + 2 * PAD_A])
        CA = t1("CA", [P, 2, S])
        CB = t1("CB", [P, 2, S])
        CX = t1("CX", [P, 2, S + 2])
        MS = t1("MS", [P, 640])
        PAR1 = t1("PAR1", [P, NP1])
    m2 = ExitStack()
    with m2:
        def t2(name, shape, dt=F32, where=m2):
            return sb(name, shape, dt, where)
        CS2 = t2("CS2", [P, S])
        PAR2 = t2("PAR2", [P, NP2])
        HB = t2("HB", [P, 28])
        LS = t2("LS", [P, 16])
        IC = t2("IC", [P, 2, POOLPAD])
        m2g = ExitStack()
        with m2g:
            GT = t2("GT", [P, 16, S], F32, m2g)
        MRG = two("MRG", [P, KT, S], m2)
        m2a = ExitStack()
        with m2a:
            PT2 = two("PT2", [P, 4, 256], m2a)
            LX = two("LX", [P, S], m2a)
            Q2, K2, V2 = (two("Q2", [P, S], m2a), two("K2", [P, 2, S], m2a), two("V2", [P, 4, P], m2a))
            MC = t2("MC", [P, 640], F32, m2a)
        m2b = ExitStack()
        with m2b:
            UP = t2("UP", [P, 4, S + POOLPAD], F32, m2b)
            L = t2("L", [P, 7, S], F32, m2b)
            MX = two("MX", [P, 2, S], m2b)
    block = ctx.enter_context(nc.Block())
    ACC2 = PR[:, 0, :]
    TH = TMP[:, 1, :]

    def lat(p, k):
        return LX[p][:, :] if k == 4 else Y[p][:, (0, 1, 6, 7)[k], :]

    def unit(b, l, k):
        return l * (U1 if b == 1 else U2) + (k if b == 1 else DEPTH * U1 + k)

    def unit_fill(b, l, k):
        per, first = (U1, 0) if b == 1 else (U2, DEPTH * U1)
        return l * (8 * per) + 16 * ((first + k) // 2 + 1)

    @block.sync
    def _(sp):
        with sp.Fori(0, UNITS // 2) as i:
            for s in range(2):
                sp.wait_ge(w_lo, 2 * i + s + 1)
                sp.dma_start(W_raw[:, s, :], dram["stream"][bass.ds(2 * i + s, 1)].rearrange(
                    "a p n -> p (a n)")).then_inc(w_raw[s], 16)
        sp.wait_ge(w_raw[0], 16 * (UNITS // 2))
        sp.sem_inc(w_raw[0], 16)
        for k in range(KT):
            sp.wait_ge(final.sem, final.at(0, str(k)))
            sp.dma_start(dram["out"][:, k, :], X[:, k, :]).then_inc(x_out, 16)
        sp.wait_ge(x_out, 16 * KT)

    @block.gpsimd
    def _(pool):
        nc.gpsimd.memset(ones[:], 1.0).then_inc(start, 1)
        n = 0
        for first, times in [(w_lo, 2)] + [(c.sem, c.start) for c in COUNTS if c.start]:
            for _ in range(times):
                if n:
                    pool.wait_ge(pool_step, n)
                nc.gpsimd.memset(spare[:], 0.0).then_inc(pool_step, 1)
                n += 1
                pool.wait_ge(pool_step, n)
                pool.sem_inc(first, 1)
        with pool.Fori(0, UNITS // 2) as i:
            for s in range(2):
                pool.wait_ge(w_hi, 2 * i + s + 1)
                nc.gpsimd.tensor_tensor(W[1][:, s, :], W_raw[:, s, :], W[0][:, s, :].bitcast(F32),
                                        ALU.subtract).then_inc(w_lo, 1)

    def w_tile(part, s, kt, lo, n):
        return W[part][:, s, kt * 256 + lo:kt * 256 + lo + n]

    def three(pe, out, pairs, skip=False):
        n = len(pairs)
        for k, (lhs, rhs) in enumerate(pairs):
            for a, b in ((0, 0), (0, 1), (1, 0)):
                mm = pe.matmul(out, lhs[a], rhs[b], start=(k == 0 and a == 0 and b == 0),
                               stop=(k == n - 1 and a == 1), skip_group_check=skip)
        return mm

    def tiles(src):
        return lambda p, k: src[p][:, k, :]

    def chunk_pairs(s, c, src, kts=range(KT), at=0):
        return [([w_tile(p, s, at + k, c * P, P) for p in range(2)],
                 [src[p][:, kt, :] for p in range(2)]) for k, kt in enumerate(kts)]

    def token_major(pe, out, s, c, src, kts=range(KT), at=0):
        for t in range(4):
            mm = three(pe, out[:, t * P:(t + 1) * P],
                       [([src(p, kt)[:, t * P:(t + 1) * P] for p in range(2)],
                         [w_tile(p, s, at + k, c * P, P) for p in range(2)]) for k, kt in enumerate(kts)],
                       skip=True)
        return mm

    def pe_norm(pe, b, l, name, acc):
        pe.wait_ge(b.acc.sem, b.acc.at(l, name))
        for t in range(4):
            mm = pe.matmul(NB[:, t:t + 1], acc[:, t * P:(t + 1) * P], ones[:, 0:1], start=True, stop=True,
                           skip_group_check=True)
        mm.then_inc(b.ss.sem, 1)
        pe.wait_ge(b.dg.sem, b.dg.at(l, name))
        for t in range(4):
            mm = pe.matmul(NB[:, t * P:(t + 1) * P], ones[:, :], TMP[:, 0, t * P:(t + 1) * P],
                           start=True, stop=True, skip_group_check=True)
        mm.then_inc(b.bc.sem, 1)

    def pe_transposes(pe, n_blocks):
        for n in range(n_blocks):
            for q in range(2):
                mm = pe.transpose(TB[n // 2][:, (n % 2) * 256 + q * P:(n % 2) * 256 + (q + 1) * P],
                                  PR[:, q, n * P:(n + 1) * P], ident[:, :])
        return mm

    NA_KEYS = (0, 1, 2, 3)

    def b1_keys(i):
        return NA_KEYS if i < STEPS else ((0, 1, 2), (1, 2, 3))[i % 2]

    @block.tensor
    def _(pe):
        pe.wait_ge(start, 1)
        pe.wait_ge(consts_in, 16 * N_CONST)

        def begin_unit(b, l, k):
            pe.wait_ge(w_lo, unit(b, l, k) + 3)

        with pe.Fori(0, DEPTH) as l:
            pe_norm(pe, b1, l, "n", ACC1)

            def free_bank(n):
                if n < 2:
                    pe.wait_ge(b1.free.sem, b1.free.at(l, "dz0") - 1)
                    return
                name = B1_CHUNKS[n - 2]
                if ("", name) in b1.free.at_:
                    pe.wait_ge(b1.free.sem, b1.free.at(l, name))
                else:
                    own = b1.aux if ("", name) in b1.aux.at_ else b1.lo
                    pe.wait_ge(own.sem, own.at(l, "cv" if name == "ck1" else name))

            def chunk(name):
                n = B1_CHUNKS.index(name)
                k, c = divmod(n, 2)
                if c == 0:
                    begin_unit(1, l, k)
                free_bank(n)
                out = G[c]
                if name in ("dv0", "dv1", "ck1"):
                    mm = token_major(pe, out, k % 2, c, tiles(H))
                elif name[0] == "o":
                    if name == "o00":
                        pe.wait_ge(b1.lo.sem, b1.lo.at(l, f"y{2 * STEPS - 1}"))
                    mm = three(pe, out[:, :], chunk_pairs(k % 2, c, Y))
                elif name == "dq0":
                    for kt in range(KT):
                        pe.wait_ge(b1.lo.sem, b1.lo.at(l, f"n{kt}"))
                        lhs = [w_tile(p, k % 2, kt, c * P, P) for p in range(2)]
                        for a, b in ((0, 0), (0, 1), (1, 0)):
                            mm = pe.matmul(out[:, :], lhs[a], H[b][:, kt, :],
                                           start=(kt == 0 and a == 0 and b == 0),
                                           stop=(kt == KT - 1 and a == 1))
                else:
                    mm = three(pe, out[:, :], chunk_pairs(k % 2, c, H))
                mm.then_inc(b1.done.sem, 1)

            def scores(i):
                if i in (0, STEPS):
                    pe.wait_ge(b1.lo.sem, b1.lo.at(l, "dk1" if i == 0 else "ck3"))
                if i >= 1:
                    pe.wait_ge(b1.red.sem, b1.red.at(l, str(i - 1)))
                h, half = (i % STEPS) // 2, i % 2
                kbs = b1_keys(i)
                lo, hi = kbs[0] * P, (kbs[-1] + 1) * P
                r = slice(HD * (h % 2), HD * (h % 2) + HD)
                for q in range(2):
                    qb = (2 * half + q) * P
                    mm = three(pe, SC[q][:, 0:hi - lo], [([AQ[p][r, h // 2, qb:qb + P] for p in range(2)],
                                                         [AK[p][r, h // 2, lo:hi] for p in range(2)])])
                mm.then_inc(b1.sc.sem, 1)

            def transposes(i):
                pe.wait_ge(b1.pn.sem, b1.pn.at(l, str(i)))
                if i >= 1:
                    pe.wait_ge(b1.lo.sem, b1.lo.at(l, f"pt{i - 1}b"))
                pe_transposes(pe, len(b1_keys(i))).then_inc(b1.tr.sem, 1)

            def attend(i):
                pe.wait_ge(b1.lo.sem, b1.lo.at(l, f"pt{i}b"))
                if i == 0:
                    pe.wait_ge(b1.lo.sem, b1.lo.at(l, "dv1"))
                if i == STEPS:
                    pe.wait_ge(b1.lo.sem, b1.lo.at(l, "cv"))
                if i >= 1:
                    pe.wait_ge(b1.pre.sem, b1.pre.at(l, f"y{i - 1}"))
                pair = (i // 4) % 2 if i < STEPS else 0
                three(pe, OB[:, 0:256], [([AV[p][:, kb, pair * P:(pair + 1) * P] for p in range(2)],
                                          [PT1[p][:, n, :] for p in range(2)])
                                         for n, kb in enumerate(b1_keys(i))]).then_inc(b1.pv.sem, 1)

            for name in ("dq0", "dq1", "dk0", "dk1", "dv0", "dv1"):
                chunk(name)
            scores(0)
            chunk("dz0")
            chunk("dz1")
            for i in range(2 * STEPS):
                if i == STEPS:
                    for name in ("cq0", "cq1", "ck0", "ck1", "cz0"):
                        chunk(name)
                    scores(i)
                    chunk("cz1")
                transposes(i)
                if i % STEPS < STEPS - 1:
                    scores(i + 1)
                if i == LN_STEP:
                    pe.wait_ge(b1.acc.sem, b1.acc.at(l, "mean"))
                    for c in range(2):
                        mm = pe.matmul(NB[:, :], ones[:, :], CA[:, c, :], start=(c == 0), stop=(c == 1))
                    mm.then_inc(b1.ss.sem, 1)
                    pe_norm(pe, b1, l, "var", ACC1)
                if i in FILL:
                    chunk(FILL[i])
                attend(i)
            for k in range(4):
                for c in range(2):
                    chunk(f"o{k}{c}")

        pe_norm(pe, bf, 0, "n", ACC1)

        with pe.Fori(0, DEPTH) as l:
            pe_norm(pe, b2, l, "n", ACC2)
            begin_unit(2, l, 0)

            for n, name in enumerate(lats):
                k, c = [(0, 0), (0, 1), (1, 0), (1, 1), (2, 0), (2, 1)][n]
                if c == 0 and k:
                    begin_unit(2, l, k)
                pe.wait_ge(b2.free.sem, b2.free.at(l, name) - 2)
                if n == 0:
                    for kt in range(KT):
                        pe.wait_ge(b2.lo.sem, b2.lo.at(l, f"n{kt}"))
                        lhs = [w_tile(p, 0, kt, 0, P) for p in range(2)]
                        for a, b in ((0, 0), (0, 1), (1, 0)):
                            mm = pe.matmul(G[0][:, :], lhs[a], H[b][:, kt, :],
                                           start=(kt == 0 and a == 0 and b == 0),
                                           stop=(kt == KT - 1 and a == 1))
                else:
                    mm = three(pe, G[c][:, :], chunk_pairs(k % 2, c, H))
                mm.then_inc(b2.done.sem, 1)
            pe_norm(pe, b2, l, "q", ACC2)
            pe_norm(pe, b2, l, "kv", ACC2)

            with pe.Fori(0, 2) as j:
                pe.wait_ge(b2.lo.sem, b2.lo.at(l, "kr"))
                for jj in range(2):
                    uk = 3 + 3 * jj
                    ju = unit(2, l, uk) + 6 * j
                    slot = uk % 2

                    pe.wait_ge(w_lo, ju + 3)

                    def bank(count, name, back=0):
                        pe.wait_ge(count.sem, count.at(l, name, "h", j) - back)

                    def q_chunk(a):
                        lhs = [([w_tile(p, slot, kt, a * P, P) for p in range(2)],
                                [lat(p, kt) for p in range(2)]) for kt in range(3)]
                        return three(pe, G[(0, 1)[a]][:, :], lhs)

                    bank(b2.aux, f"g{jj}0", 2)
                    bank(b2.free, f"q{jj}0", 1)
                    q_chunk(0).then_inc(b2.done.sem, 1)
                    bank(b2.aux, f"g{jj}0", 1)
                    three(pe, G[1][:, :], [([w_tile(p, slot, 3 + kt, 0, P) for p in range(2)],
                                            [lat(p, 3 + kt) for p in range(2)]) for kt in range(2)]
                          ).then_inc(b2.done.sem, 1)
                    bank(b2.free, f"q{jj}0")
                    token_major(pe, G[0], slot, 1, lat, (3, 4), 3).then_inc(b2.done.sem, 1)

                    def scores(s):
                        a, half = divmod(s, 2)
                        bank(b2.lo, f"q{jj}{a}")
                        if s == 0:
                            bank(b2.lo, f"k{jj}1")
                        bank(b2.red, f"{jj}{s}", 1)
                        for q in range(2):
                            qb = (2 * half + q) * P
                            w = (256, 512)[half]
                            mm = three(pe, SC[q][:, 0:w], [([Q2[p][0:96, qb:qb + P] for p in range(2)],
                                                           [K2[p][0:96, a, 0:w] for p in range(2)])])
                        mm.then_inc(b2.sc.sem, 1)

                    scores(0)
                    for s in range(4):
                        a, half = divmod(s, 2)
                        bank(b2.pn, f"{jj}{s}")
                        if s:
                            bank(b2.lo, f"pt{jj}{s - 1}" + ("b" if (s - 1) % 2 else "a"))
                        pe_transposes(pe, 4 if half else 2).then_inc(b2.tr.sem, 1)
                        if s == 0:
                            scores(1)
                            bank(b2.lo, f"k{jj}1")
                            q_chunk(1).then_inc(b2.done.sem, 1)
                        elif s < 3:
                            scores(s + 1)
                        gk = uk + 1 + s // 2
                        if s % 2 == 0:
                            pe.wait_ge(w_lo, unit(2, l, gk) + 6 * j + 3)
                        if s == 0:
                            bank(b2.lo, f"v{jj}")
                        elif s == 1:
                            bank(b2.free, f"q{jj}1")
                        else:
                            bank(b2.aux, f"g{jj}{s - 2}")
                        three(pe, G[s % 2][:, :], chunk_pairs(gk % 2, s % 2, H)).then_inc(b2.done.sem, 1)
                        bank(b2.lo, f"pt{jj}{s}" + ("b" if half else "a"))
                        if s:
                            bank(b2.lo, f"y{jj}{s - 1}")
                        three(pe, OB[:, 0:256], [([V2[p][:, kb, :] for p in range(2)],
                                                  [PT2[p][:, kb, :] for p in range(2)])
                                                 for kb in range(4 if half else 2)]).then_inc(b2.pv.sem, 1)

            for n, name in enumerate(mid):
                k, c = 15 + n // 2, n % 2
                if c == 0:
                    begin_unit(2, l, k)
                if n < 2:
                    pe.wait_ge(b2.aux.sem, b2.aux.at(l, f"g1{2 + n}", "h", 1))
                else:
                    pe.wait_ge(b2.free.sem, b2.free.at(l, mid[n - 2], "mid"))
                three(pe, G[c][:, :], chunk_pairs(k % 2, c, H)).then_inc(b2.done.sem, 1)
            begin_unit(2, l, 17)
            for n, (name, src) in enumerate((("p0", "pm0"), ("p1", "pm1"), ("a0", "uc0"), ("x0", "uc0"),
                                             ("a1", "uc1"), ("x1", "uc1"))):
                pe.wait_ge(b2.lo.sem, b2.lo.at(l, src, "mid"))
                col = {"p": 0, "a": 2, "x": 4}[name[0]] + int(name[1])
                out = {"p": SC, "a": TB, "x": (OB, NB)}[name[0]][int(name[1])]
                three(pe, out[:, :], [([w_tile(p, 1, col, 0, P) for p in range(2)],
                                       [MX[p][:, int(name[1]), :] for p in range(2)])]).then_inc(b2.sm.sem, 1)
            with pe.Fori(0, 4) as m:
                pe.wait_ge(b2.aux.sem, b2.aux.at(l, "rx1", "mid"))
                pe.wait_ge(b2.pre.sem, b2.pre.at(l, "py1", "mid"))
                pe.wait_ge(w_lo, unit(2, l, 18) + 2 * m + 3)
                for c in range(2):
                    if c == 0:
                        pe.wait_ge(b2.free.sem, b2.free.at(l, "lr1", "mid"))
                    pe.wait_ge(b2.aux.sem, b2.aux.at(l, f"t{c}", "m", m) - 2)
                    three(pe, G[c][:, :], chunk_pairs(0, c, H)).then_inc(b2.done.sem, 1)
                pe.wait_ge(w_lo, unit(2, l, 19) + 2 * m + 3)
                for c in range(2):
                    pe.wait_ge(b2.brf.sem, b2.brf.at(l, str(c), "m", m) - 2)
                    sets = ((SC[0], SC[1], TB[0]), (TB[1], OB, NB))[c]
                    pe.wait_ge(b2.lo.sem, b2.lo.at(l, "lh1", "mid"))
                    three(pe, sets[0][:, :], chunk_pairs(1, c, Y, (0, 1), 0))
                    three(pe, sets[1][:, :], chunk_pairs(1, c, Y, (2, 3, 4, 5), 2))
                    three(pe, sets[2][:, :], chunk_pairs(1, c, Y, (6, 7), 6)).then_inc(b2.br.sem, 1)
            pe.wait_ge(b2.lo.sem, b2.lo.at(l, "b1", "m", 3))
            for n in range(KT):
                k, c = 26 + n // 2, n % 2
                if c == 0:
                    begin_unit(2, l, k)
                if n < 2:
                    pe.wait_ge(b2.aux.sem, b2.aux.at(l, f"t{n}", "m", 3))
                else:
                    pe.wait_ge(b2.free.sem, b2.free.at(l, f"o{n - 2}", "out"))
                three(pe, G[c][:, :], chunk_pairs(k % 2, c, MRG)).then_inc(b2.done.sem, 1)
            pe_norm(pe, b2, l, "e", ACC2)
            with pe.Fori(0, 4) as f:
                for n in range(KT):
                    k, c = 30 + n // 2, n % 2
                    if c == 0:
                        pe.wait_ge(w_lo, unit(2, l, k) + 8 * f + 3)
                    if n < 2:
                        pe.wait_ge(b2.free.sem, b2.free.at(l, "d0", "f", f) - 2 + n)
                    else:
                        pe.wait_ge(b2.aux.sem, b2.aux.at(l, f"u{n - 2}", "f", f))
                    if n == 0:
                        for kt in range(KT):
                            pe.wait_ge(b2.lo.sem, b2.lo.at(l, f"e{kt}", "n2"))
                            lhs = [w_tile(p, 0, kt, 0, P) for p in range(2)]
                            for a, b in ((0, 0), (0, 1), (1, 0)):
                                mm = pe.matmul(G[0][:, :], lhs[a], H[b][:, kt, :],
                                               start=(kt == 0 and a == 0 and b == 0),
                                               stop=(kt == KT - 1 and a == 1))
                    else:
                        mm = three(pe, G[c][:, :], chunk_pairs(k % 2, c, H))
                    mm.then_inc(b2.done.sem, 1)
                for n in range(KT):
                    k, c = 34 + n // 2, n % 2
                    if c == 0:
                        pe.wait_ge(w_lo, unit(2, l, k) + 8 * f + 3)
                    if n < 2:
                        pe.wait_ge(b2.aux.sem, b2.aux.at(l, f"u{6 + n}", "f", f))
                    else:
                        pe.wait_ge(b2.free.sem, b2.free.at(l, f"d{n - 2}", "f", f))
                    if n == 0:
                        for kt in range(KT):
                            pe.wait_ge(b2.lo.sem, b2.lo.at(l, f"u{kt}", "f", f))
                            lhs = [w_tile(p, 0, kt, 0, P) for p in range(2)]
                            for a, b in ((0, 0), (0, 1), (1, 0)):
                                mm = pe.matmul(G[0][:, :], lhs[a], Y[b][:, kt, :],
                                               start=(kt == 0 and a == 0 and b == 0),
                                               stop=(kt == KT - 1 and a == 1))
                    else:
                        mm = three(pe, G[c][:, :], chunk_pairs(k % 2, c, Y))
                    mm.then_inc(b2.done.sem, 1)
        pe_norm(pe, bf, 1, "n", ACC2)

    @block.scalar
    def _(act):
        own = Own(act_step)

        def load(dst, src, sem_):
            act.dma_start(dst, src).then_inc(sem_, 16)

        for dst, src in ((X[:, :, :], "x"), (ident[:, :], "ident"), (MS[:, :], "window"), (NM[:, :], "columns"),
                         (PARF[:, :], "finals"), ):
            load(dst, dram[src], consts_in)
        assert N_CONST == 5

        def prep(b, l, k, after, step=0, back=0):
            act.wait_ge(w_raw[k % 2], unit_fill(b, l, k) + 8 * step)
            if after:
                act.wait_ge(after[0].sem, after[0].at(*after[1:]) - back)
            act.wait_ge(*own.last(1))
            nc.scalar.activation(W[0][:, k % 2, :], W_raw[:, k % 2, :], ACT.Copy) \
                .then_inc(w_hi, own.reach(w_hi, unit(b, l, k) + 1 + step))

        def hi(b, l, name, out, in_, seg="", i=0, **more):
            act.wait_ge(*own.last(1))
            nc.scalar.activation(out, in_, ACT.Copy, **more).then_inc(b.hi.sem, own.event(b.hi, l, name, seg, i))

        def root(b, l, name, n):
            act.wait_ge(b.ss.sem, b.ss.at(l, name))
            act.wait_ge(*own.last(1))
            nc.scalar.activation(NR[:, :], NB[:, 0:4], ACT.Sqrt, bias=EPSC[:, :], scale=1.0 / n) \
                .then_inc(b.rt.sem, own.event(b.rt, l, name))

        def exps(b, l, name, w, scale, sink=None, seg="", i=0):
            act.wait_ge(b.red.sem, b.red.at(l, name, seg, i))
            for q in range(2):
                if sink is not None:
                    act.wait_ge(*own.last(1))
                    nc.scalar.activation(SM[:, 8 + q:9 + q], PAR1[:, sink:sink + 1], ACT.Exp, bias=SM[:,
                                         2 + q:3 + q]) \
                        .then_inc(act_step, own.step())
                act.wait_ge(*own.last(1))
                ins = nc.scalar.activation(PR[:, q, 0:w], PR[:, q, 0:w], ACT.Exp, bias=SM[:, 2 + q:3 + q],
                                           scale=scale, accum_out=SM[:, 4 + q:5 + q])
                if q:
                    ins.then_inc(b.ex.sem, own.event(b.ex, l, name, seg, i))
                else:
                    ins.then_inc(act_step, own.step())

        act.wait_ge(start, 1)
        nc.scalar.activation(EPSC[:, :], ones[:, 0:1], ACT.Copy, scale=EPS).then_inc(act_step, own.step())
        prep(1, 0, 0, None)
        with act.Fori(0, DEPTH) as l:
            own.enter(l, ACT_ORDER_1)
            act.wait_ge(b1.layer.sem, b1.layer.at(l, "end") - 1)
            load(PAR1[:, :], dram["par1"][bass.ds(l, 1)].rearrange("a p n -> p (a n)"), par_in)

            def load_bias(h):
                load(BT[:, h % 2, :, :], dram["bias"][bass.ds(4 * l + h, 1)].rearrange(
                    "a p (j c) -> p (a j) c", j=14), bias_in[h % 2])

            load_bias(0)
            load_bias(1)

            def begin(name):
                n = B1_CHUNKS.index(name)
                if n % 2:
                    return
                k = n // 2 + 1
                if k == 1:
                    prep(1, l, 1, (b1.done, l, "dq0"), back=1)
                elif k < U1:
                    prep(1, l, k, (b1.done, l, B1_CHUNKS[2 * k - 3]))
                else:
                    prep(1, l, U1, (b1.done, l, B1_CHUNKS[2 * k - 3]))

            def chunk(name):
                begin(name)
                n = B1_CHUNKS.index(name)
                kind, c, bank_ = name[:2], n % 2, G[n % 2]
                if kind[0] == "o":
                    return
                act.wait_ge(b1.done.sem, b1.done.at(l, name))
                if kind in ("dq", "dk"):
                    hi(b1, l, name, (AQ if kind == "dq" else AK)[0][:, c, :], bank_[:, :])
                elif kind == "dv":
                    hi(b1, l, name, AV[0][:, :, c * P:(c + 1) * P],
                       bank_[:, :].rearrange("p (t n) -> p t n", t=4))
                elif kind in ("dz", "cz", "bz", "az"):
                    act.wait_ge(*own.last(1))
                    nc.scalar.activation(TH, bank_[:, :], ACT.Tanh, scale=0.5) \
                        .then_inc(b1.aux.sem, own.event(b1.aux, l, name))
                elif kind == "av":
                    act.wait_ge(*own.last(1))
                    nc.scalar.activation(CA[:, c, :], bank_[:, :], ACT.Tanh, scale=0.5) \
                        .then_inc(b1.aux.sem, own.event(b1.aux, l, name))
                elif kind == "bc":
                    act.wait_ge(*own.last(1))
                    nc.scalar.activation(CB[:, c, :], bank_[:, :], ACT.Copy) \
                        .then_inc(b1.aux.sem, own.event(b1.aux, l, name))
                elif kind == "cq":
                    act.wait_ge(b1.pre.sem, b1.pre.at(l, name))
                    hi(b1, l, name, AQ[0][:, c, :], PRE[:, c, :])
                elif name == "ck0":
                    act.wait_ge(b1.pre.sem, b1.pre.at(l, name))
                    for g in range(2):
                        for half in range(2):
                            hi(b1, l, f"ck{2 * g + half}", AK[0][half * HD:(half + 1) * HD, g, :],
                               PRE[g * HD:(g + 1) * HD, 0, :])
                elif name == "ck1":
                    hi(b1, l, "cv", AV[0][:, :, 0:P], bank_[:, :].rearrange("p (t n) -> p t n", t=4))
                if kind in ("bz", "az"):
                    i = [k for k, v in FILL.items() if v == name][0]
                    act.wait_ge(b1.pre.sem, b1.pre.at(l, "y" + name))
                    hi(b1, l, "y" + name, Y[0][:, (2 if kind == "bz" else 0) + c, :], PRE[:, (i + 1) % 2, :])
                if kind in ("dz", "cz"):
                    act.wait_ge(b1.free.sem, b1.free.at(l, name))

            begin("dq0")
            root(b1, l, "n", D)
            for k in range(KT):
                act.wait_ge(b1.pre.sem, b1.pre.at(l, f"n{k}"))
                hi(b1, l, f"n{k}", H[0][:, k, :], PRE[:, k % 2, :])
            for name in ("dq0", "dq1", "dk0", "dk1", "dv0", "dv1"):
                if name != "dq0":
                    chunk(name)
                else:
                    act.wait_ge(b1.done.sem, b1.done.at(l, name))
                    hi(b1, l, name, AQ[0][:, 0, :], G[0][:, :])

            def softmax(i):
                w = P * len(b1_keys(i))
                exps(b1, l, str(i), w, 1.0, None if i < STEPS else P1["sink"] + (i - STEPS) // 2)
                if i == 1:
                    load_bias(2)
                if i == 3:
                    load_bias(3)
                if i == STEPS - 1:
                    load(ROPE[:, 0:2 * S], dram["rope1"], rope_in)

            softmax(0)
            chunk("dz0")
            chunk("dz1")
            for i in range(2 * STEPS):
                if i == STEPS:
                    for name in ("cq0", "cq1", "ck0", "ck1", "cz0"):
                        chunk(name)
                    softmax(i)
                    chunk("cz1")
                act.wait_ge(b1.tr.sem, b1.tr.at(l, str(i)))
                act.wait_ge(b1.pv.sem, b1.pv.at(l, str(i)) - 1)
                n = len(b1_keys(i))
                hi(b1, l, f"pt{i}a", PT1[0][:, 0:2, :], TB[0][:, :].rearrange("p (a n) -> p a n", a=2))
                hi(b1, l, f"pt{i}b", PT1[0][:, 2:n, :],
                   TB[1][:, 0:256 * (n - 2)].rearrange("p (a n) -> p a n", a=n - 2))
                if i % STEPS < STEPS - 1:
                    softmax(i + 1)
                if i == LN_STEP:
                    root(b1, l, "var", 2 * P)
                    for c in range(2):
                        act.wait_ge(ln_in, 2 * l + (c + 1))
                        act.wait_ge(*own.last(1))
                        nc.scalar.activation(TMP[:, c, :], CA[:, c, :], ACT.Tanh, scale=0.5) \
                            .then_inc(b1.aux.sem, own.event(b1.aux, l, f"ln{c}"))
                    act.wait_ge(ln_out, l + 1)
                if i in FILL:
                    chunk(FILL[i])
                h, half = (i % STEPS) // 2, i % 2
                r = slice(HD * (h % 2), HD * (h % 2) + HD)
                act.wait_ge(b1.pre.sem, b1.pre.at(l, f"y{i}"))
                hi(b1, l, f"y{i}", Y[0][r, (6 if i < STEPS else 4) + h // 2, half * 256:(half + 1) * 256],
                   PRE[r, i % 2, 0:256])
            for k in range(4):
                begin(f"o{k}0")
            act.wait_ge(*own.last(0))
            nc.scalar.activation(spare_a[:, :], ones[:, 0:1], ACT.Copy).then_inc(act_step, own.step())
        own.leave(DEPTH)

        root(bf, 0, "n", D)
        act.wait_ge(start, 1)
        load(CS2[:, :], dram["rope2"], par_in)
        load(IC[:, :, :], dram["counts"], par_in)
        with act.Fori(0, DEPTH) as l:
            own.enter(l, ACT_ORDER_2)
            act.wait_ge(b2.layer.sem, b2.layer.at(l, "end") - 1)
            load(PAR2[:, :], dram["par2"][bass.ds(l, 1)].rearrange("a p n -> p (a n)"), par_in)
            load(MC[:, :], dram["causal"], par_in)
            prep(2, l, 1, (b2.done, l, "q00"), back=1)
            root(b2, l, "n", D)
            for k in range(KT):
                act.wait_ge(b2.pre.sem, b2.pre.at(l, f"n{k}"))
                hi(b2, l, f"n{k}", H[0][:, k, :], PRE[:, k % 2, :])
            prep(2, l, 2, (b2.done, l, "q01"))
            prep(2, l, 3, (b2.done, l, "kr"))
            root(b2, l, "q", 3 * P)
            for k in range(5):
                if k == 3:
                    root(b2, l, "kv", 2 * P)
                act.wait_ge(b2.pre.sem, b2.pre.at(l, f"l{k}"))
                hi(b2, l, f"l{k}", lat(0, k), PRE[:, k % 2, :])
            act.wait_ge(b2.pre.sem, b2.pre.at(l, "kr"))
            act.wait_ge(*own.last(1))
            nc.scalar.activation(K2[0][64:96, 0, :], PRE[64:96, 1, :], ACT.Copy).then_inc(act_step, own.step())
            hi(b2, l, "kr", K2[0][64:96, 1, :], PRE[64:96, 1, :])
            act.wait_ge(*own.last(0))
            nc.scalar.activation(spare_a[:, :], ones[:, 0:1], ACT.Copy).then_inc(act_step, own.step())
            with act.Fori(0, 2) as j:
                own.enter(j, ACT_ORDER_H)
                for jj in range(2):
                    uk = 3 + 3 * jj
                    if jj == 0:
                        prep(2, l, uk + 1, (b2.done, l, "q00", "h", j), step=6 * j, back=1)
                    else:
                        prep(2, l, uk + 1, (b2.done, l, "g03", "h", j), step=6 * j)

                    def softmax(s):
                        exps(b2, l, f"{jj}{s}", (256, 512)[s % 2], 96.0 ** -0.5, None, "h", j)

                    def q_part(a):
                        act.wait_ge(b2.pre.sem, b2.pre.at(l, f"q{jj}{a}", "h", j))
                        hi(b2, l, f"q{jj}{a}", Q2[0][0:96, :], PRE[0:96, a, :], "h", j)

                    q_part(0)
                    act.wait_ge(b2.done.sem, b2.done.at(l, f"k{jj}0", "h", j))
                    for a in range(2):
                        hi(b2, l, f"k{jj}{a}", K2[0][0:64, a, :], G[1][a * 64:(a + 1) * 64, :], "h", j)
                    act.wait_ge(b2.done.sem, b2.done.at(l, f"v{jj}0", "h", j))
                    hi(b2, l, f"v{jj}", V2[0][:, :, :], G[0][:, :].rearrange("p (t n) -> p t n", t=4), "h", j)
                    softmax(0)
                    for s in range(4):
                        act.wait_ge(b2.tr.sem, b2.tr.at(l, f"{jj}{s}", "h", j))
                        act.wait_ge(b2.pv.sem, b2.pv.at(l, f"{jj}{s}", "h", j) - 1)
                        for n in range(1 + s % 2):
                            hi(b2, l, f"pt{jj}{s}" + "ab"[n], PT2[0][:, 2 * n:2 * n + 2, :],
                               TB[n][:, :].rearrange("p (a n) -> p a n", a=2), "h", j)
                        if s == 0:
                            softmax(1)
                            q_part(1)
                            prep(2, l, uk + 2, (b2.done, l, f"q{jj}1", "h", j), step=6 * j)
                        elif s < 3:
                            softmax(s + 1)
                        if s == 2:
                            prep(2, l, uk + 3, (b2.done, l, f"g{jj}1", "h", j), step=6 * j)
                        act.wait_ge(b2.done.sem, b2.done.at(l, f"g{jj}{s}", "h", j))
                        g, c = divmod(s, 2)
                        col = g * 8 + 2 * jj + c
                        act.wait_ge(*own.last(1))
                        nc.scalar.activation(GT[:, bass.ds(4 * j + col, 1), :].rearrange("p a n -> p (a n)"),
                                             G[c][:, :], ACT.Tanh, bias=HB[:, bass.ds(4 * j + (4 + col), 1)],
                                             scale=0.5) \
                            .then_inc(b2.aux.sem, own.event(b2.aux, l, f"g{jj}{s}", "h", j))
                        act.wait_ge(b2.pv.sem, b2.pv.at(l, f"{jj}{s}", "h", j))
                        a, half = divmod(s, 2)
                        r = slice(a * HD, (a + 1) * HD)
                        hi(b2, l, f"y{jj}{s}",
                           Y[0][r, bass.ds(2 * j + (2 + jj), 1), half * 256:(half + 1) * 256].rearrange(
                               "p a n -> p (a n)"), OB[r, 0:256], "h", j)
                act.wait_ge(*own.last(0))
                nc.scalar.activation(spare_a[:, :], ones[:, 0:1], ACT.Copy).then_inc(act_step, own.step())
            own.leave(2)
            prep(2, l, 16, (b2.done, l, "g13", "h", 1))
            prep(2, l, 17, (b2.done, l, "pl1", "mid"))
            for n in range(2):
                act.wait_ge(b2.pre.sem, b2.pre.at(l, f"pm{n}", "mid"))
                hi(b2, l, f"pm{n}", MX[0][:, n, :], PRE[:, n, :], "mid")
            prep(2, l, 18, (b2.done, l, "lr1", "mid"))
            for n in range(2):
                act.wait_ge(b2.pre.sem, b2.pre.at(l, f"py{n}", "mid"))
                hi(b2, l, f"py{n}", Y[0][:, n, :], PRE[:, n, :], "mid")
            for n in range(2):
                act.wait_ge(b2.pre.sem, b2.pre.at(l, f"uc{n}", "mid"))
                hi(b2, l, f"uc{n}", MX[0][:, n, :], L[:, n, :], "mid")
            act.wait_ge(b2.lru.sem, b2.lru.at(l, "sp"))
            act.wait_ge(*own.last(1))
            nc.scalar.activation(LS[:, 2:4], LS[:, 0:2], ACT.Exp, scale=-1.0) \
                .then_inc(b2.aux.sem, own.event(b2.aux, l, "sp", "mid"))
            for c in range(2):
                act.wait_ge(b2.sm.sem, b2.sm.at(l, f"a{c}"))
                act.wait_ge(*own.last(1))
                nc.scalar.activation(L[:, 2, :], TB[c][:, :], ACT.Tanh, bias=HB[:, c:c + 1], scale=0.5) \
                    .then_inc(b2.aux.sem, own.event(b2.aux, l, f"ra{c}", "mid"))
                act.wait_ge(b2.sm.sem, b2.sm.at(l, f"x{c}"))
                act.wait_ge(*own.last(1))
                nc.scalar.activation(L[:, 3, :], (OB, NB)[c][:, :], ACT.Tanh, bias=HB[:, 2 + c:3 + c], scale=0.5) \
                    .then_inc(b2.aux.sem, own.event(b2.aux, l, f"rx{c}", "mid"))
                if c == 0:
                    act.wait_ge(ls_ready, l + 1)
                act.wait_ge(*own.last(1))
                nc.scalar.activation(L[:, 4, :], L[:, 2, :], ACT.Tanh, bias=LS[:, 12 + c:13 + c], scale=LS[:,
                                     12 + c:13 + c]) \
                    .then_inc(b2.aux.sem, own.event(b2.aux, l, f"lt{c}", "mid"))
                act.wait_ge(*own.last(1))
                nc.scalar.activation(L[:, 5, :], L[:, 2, :], ACT.Exp, bias=LS[:, 14 + c:15 + c], scale=LS[:,
                                     14 + c:15 + c]) \
                    .then_inc(b2.aux.sem, own.event(b2.aux, l, f"la{c}", "mid"))
                act.wait_ge(*own.last(0))
                nc.scalar.activation(L[:, 6, :], L[:, 5, :], ACT.Square) \
                    .then_inc(b2.aux.sem, own.event(b2.aux, l, f"sq{c}", "mid"))
                act.wait_ge(b2.lru.sem, b2.lru.at(l, f"c{c}"))
                act.wait_ge(*own.last(1))
                nc.scalar.activation(L[:, 6, :], L[:, 4, :], ACT.Sqrt) \
                    .then_inc(b2.aux.sem, own.event(b2.aux, l, f"rt{c}", "mid"))
                act.wait_ge(b2.pre.sem, b2.pre.at(l, f"lh{c}", "mid"))
                hi(b2, l, f"lh{c}", Y[0][:, 6 + c, :], PRE[:, c, :], "mid")
            act.wait_ge(*own.last(0))
            nc.scalar.activation(spare_a[:, :], ones[:, 0:1], ACT.Copy).then_inc(act_step, own.step())
            with act.Fori(0, 4) as m:
                own.enter(m, ACT_ORDER_M)
                act.wait_ge(b2.sm.sem, b2.sm.at(l, "x1"))
                prep(2, l, 19, (b2.br, l, "0", "m", m), step=2 * m, back=1)
                for c in range(2):
                    act.wait_ge(b2.done.sem, b2.done.at(l, f"t{c}", "m", m))
                    act.wait_ge(*own.last(1))
                    nc.scalar.activation(L[:, c, :], G[c][:, :], ACT.Tanh, scale=0.5, bias=HB[:,
                                         bass.ds(2 * m + (20 + c), 1)]) \
                        .then_inc(b2.aux.sem, own.event(b2.aux, l, f"t{c}", "m", m))
                prep(2, l, 20, (b2.done, l, "t1", "m", m), step=2 * m)
                for c in range(2):
                    act.wait_ge(b2.pre.sem, b2.pre.at(l, f"b{c}", "m", m))
                    hi(b2, l, f"b{c}", MRG[0][:, bass.ds(2 * m + c, 1), :].rearrange("p a n -> p (a n)"),
                       PRE[:, c, :], "m", m, scale=0.5)
                act.wait_ge(*own.last(0))
                nc.scalar.activation(spare_a[:, :], ones[:, 0:1], ACT.Copy).then_inc(act_step, own.step())
            own.leave(4)
            prep(2, l, 27, (b2.br, l, "1", "m", 3))
            for k in range(28, 31):
                prep(2, l, k, (b2.done, l, f"o{2 * (k - 28) + 1}", "out"))
            root(b2, l, "e", D)
            for k in range(KT):
                act.wait_ge(b2.pre.sem, b2.pre.at(l, f"e{k}", "n2"))
                hi(b2, l, f"e{k}", H[0][:, k, :], PRE[:, k % 2, :], "n2")
            act.wait_ge(*own.last(0))
            nc.scalar.activation(spare_a[:, :], ones[:, 0:1], ACT.Copy).then_inc(act_step, own.step())
            with act.Fori(0, 4) as f:
                own.enter(f, ACT_ORDER_F)
                for n in range(KT):
                    if n % 2 == 0:
                        k = 31 + n // 2
                        if n == 0:
                            prep(2, l, k, (b2.done, l, "u0", "f", f), step=8 * f, back=1)
                        else:
                            prep(2, l, k, (b2.done, l, f"u{n - 1}", "f", f), step=8 * f)
                    act.wait_ge(b2.done.sem, b2.done.at(l, f"u{n}", "f", f))
                    act.wait_ge(*own.last(1))
                    nc.scalar.activation(TMP[:, n % 2, :], G[n % 2][:, :], ACT.Relu) \
                        .then_inc(b2.aux.sem, own.event(b2.aux, l, f"u{n}", "f", f))
                    act.wait_ge(b2.pre.sem, b2.pre.at(l, f"u{n}", "f", f))
                    hi(b2, l, f"u{n}", Y[0][:, n, :], PRE[:, n % 2, :], "f", f)
                for n in range(4):
                    last = ("u7", "d1", "d3", "d5")[n]
                    prep(2, l, 35 + n, (b2.done, l, last, "f", f), step=8 * f)
                act.wait_ge(*own.last(0))
                nc.scalar.activation(spare_a[:, :], ones[:, 0:1], ACT.Copy).then_inc(act_step, own.step())
            own.leave(4)
        own.leave(DEPTH)
        root(bf, 1, "n", D)

    @block.vector
    def _(dve):
        own = Own(dve_step)

        def lo(b, l, name, out, in_, hi_, seg="", i=0, half=False, behind=1):
            dve.wait_ge(b.hi.sem, b.hi.at(l, name, seg, i))
            dve.wait_ge(*own.last(behind))
            if half:
                ins = nc.vector.scalar_tensor_tensor(out, in_, 0.5, hi_.bitcast(F32), ALU.mult, ALU.subtract)
            else:
                ins = nc.vector.tensor_tensor(out, in_, hi_.bitcast(F32), ALU.subtract)
            ins.then_inc(b.lo.sem, own.event(b.lo, l, name, seg, i))

        def mark(count, l, name, seg="", i=0):
            dve.wait_ge(*own.last(0))
            nc.vector.memset(spare_v[:, :], 0.0).then_inc(count.sem, own.event(count, l, name, seg, i))

        def diagonals(b, l, name):
            dve.wait_ge(b.rt.sem, b.rt.at(l, name))
            dve.wait_ge(*own.last(0))
            nc.vector.reciprocal(NR[:, :], NR[:, :]).then_inc(dve_step, own.step())
            for t in range(4):
                dve.wait_ge(*own.last(1 if t else 0))
                ins = nc.vector.tensor_scalar(TMP[:, 0, t * P:(t + 1) * P], ident[:, :], NR[:, t:t + 1], None, ALU.mult)
                if t == 3:
                    ins.then_inc(b.dg.sem, own.event(b.dg, l, name))
                else:
                    ins.then_inc(dve_step, own.step())
            dve.wait_ge(b.bc.sem, b.bc.at(l, name))

        def norm_to_h(b, l, name, first, gains, seg=""):
            diagonals(b, l, name)

            def rest(k):
                lo(b, l, f"{first}{k}", H[1][:, k, :], PRE[:, k % 2, :], H[0][:, k, :], seg)

            for k in range(KT):
                dve.wait_ge(*own.last(1))
                nc.vector.scalar_tensor_tensor(PRE[:, k % 2, :], X[:, k, :], gains[:, k:k + 1], NB[:, :],
                                               ALU.mult, ALU.mult) \
                    .then_inc(b.pre.sem, own.event(b.pre, l, f"{first}{k}", seg))
                if k:
                    rest(k - 1)
            rest(KT - 1)

        def squares(acc, src, first):
            if first:
                dve.wait_ge(*own.last(0))
                nc.vector.tensor_tensor(acc, src, src, ALU.mult).then_inc(dve_step, own.step())
            else:
                dve.wait_ge(*own.last(0))
                nc.vector.tensor_tensor(PRE[:, 1, :], src, src, ALU.mult).then_inc(dve_step, own.step())
                dve.wait_ge(*own.last(0))
                nc.vector.tensor_tensor(acc, acc, PRE[:, 1, :], ALU.add).then_inc(dve_step, own.step())

        def residual(b, l, name, k, acc, seg="", i=0):
            dve.wait_ge(b.done.sem, b.done.at(l, name, seg, i))
            dve.wait_ge(*own.last(0))
            nc.vector.tensor_tensor(X[:, k, :], X[:, k, :], G[k % 2][:, :], ALU.add) \
                .then_inc(b.free.sem, own.event(b.free, l, name, seg, i))
            squares(acc, X[:, k, :], k == 0)

        def row_max(b, l, name, w, masks, scale, exp_scale, seg="", i=0, sink=None):
            dve.wait_ge(b.sc.sem, b.sc.at(l, name, seg, i))
            dve.wait_ge(*own.last(0))
            nc.vector.memset(spare_v[:, :], 0.0).then_inc(dve_step, own.step())
            for q in range(2):
                nc.vector.tensor_tensor_reduce(PR[:, q, 0:w], SC[q][:, 0:w], masks[q], scale, -3e38, ALU.add,
                                               ALU.max, SM[:, q:q + 1]) \
                    .then_inc(dve_step, own.step())
            if sink is not None:
                dve.wait_ge(*own.last(0))
                nc.vector.tensor_scalar(SM[:, 0:2], SM[:, 0:2], PAR1[:, sink:sink + 1], None, ALU.max) \
                    .then_inc(dve_step, own.step())
            dve.wait_ge(*own.last(0))
            nc.vector.tensor_scalar(SM[:, 2:4], SM[:, 0:2], -exp_scale, None, ALU.mult) \
                .then_inc(b.red.sem, own.event(b.red, l, name, seg, i))

        def normalise(b, l, name, w, sink, seg="", i=0):
            dve.wait_ge(b.ex.sem, b.ex.at(l, name, seg, i))
            if sink is not None:
                dve.wait_ge(*own.last(0))
                nc.vector.tensor_tensor(SM[:, 4:6], SM[:, 4:6], SM[:, 8:10], ALU.add).then_inc(dve_step, own.step())
            dve.wait_ge(*own.last(0))
            nc.vector.reciprocal(SM[:, 6:8], SM[:, 4:6]).then_inc(dve_step, own.step())
            for q in range(2):
                dve.wait_ge(*own.last(q))
                ins = nc.vector.tensor_scalar(PR[:, q, 0:w], PR[:, q, 0:w], SM[:, 6 + q:7 + q], None, ALU.mult)
                if q:
                    ins.then_inc(b.pn.sem, own.event(b.pn, l, name, seg, i))
                else:
                    ins.then_inc(dve_step, own.step())

        for tile in (HA, CX):
            nc.vector.memset(tile[:, :, :], 0.0).then_inc(dve_step, own.step())
        dve.wait_ge(start, 1)
        dve.wait_ge(consts_in, 16 * N_CONST)
        for k in range(KT):
            squares(ACC1[:, :], X[:, k, :], k == 0)

        with dve.Fori(0, DEPTH) as l:
            own.enter(l, DVE_ORDER_1)
            mark(b1.acc, l, "n")
            dve.wait_ge(par_in, 16 * l + 16)
            dve.wait_ge(*own.last(0))
            nc.vector.tensor_scalar(PAR1[:, P1["conv_a_w"]:P1["conv_a_w"] + 2 * CONV_A], PAR1[:,
                                    P1["conv_a_w"]:P1["conv_a_w"] + 2 * CONV_A], 0.5, None, ALU.mult) \
                .then_inc(dve_step, own.step())
            norm_to_h(b1, l, "n", "n", PAR1[:, P1["norm_g"]:P1["norm_g"] + KT])

            def par(name, k=0):
                return PAR1[:, P1[name] + k:P1[name] + k + 1]

            taps = iter([(j, c) for j in range(CONV_A) for c in range(2)])

            def conv_a(n):
                for _ in range(n):
                    j, c = next(taps)
                    src, w = HA[:, c, j:j + S], par("conv_a_w", c * CONV_A + j)
                    if j == 0:
                        dve.wait_ge(*own.last(1))
                        nc.vector.tensor_scalar(CA[:, c, :], src, w, par("conv_a_b", c), ALU.mult, ALU.add) \
                            .then_inc(dve_step, own.step())
                    else:
                        dve.wait_ge(*own.last(1))
                        nc.vector.scalar_tensor_tensor(CA[:, c, :], src, w, CA[:, c, :], ALU.mult, ALU.add) \
                            .then_inc(dve_step, own.step())

            def softmax_max(i):
                if i < STEPS:
                    h, half = i // 2, i % 2
                    if half == 0:
                        dve.wait_ge(bias_in[h % 2], 32 * l + 16 * (h // 2 + 1))
                        dve.wait_ge(*own.last(0))
                        nc.vector.scalar_tensor_tensor(BT[:, h % 2, :, :], BT[:, h % 2, :, :], 8.0, NM[:,
                                                       :].unsqueeze(1).broadcast_to([P, 14, GRID]), ALU.mult,
                                                       ALU.add) \
                            .then_inc(dve_step, own.step())
                    flat = BT[:, h % 2, :, :].rearrange("p a b -> p (a b)")
                    masks = [flat[:, (6 - 2 * qb) * GRID:(14 - 2 * qb) * GRID] for qb in (2 * half, 2 * half + 1)]
                    row_max(b1, l, str(i), S, masks, 0.125, 1.0)
                else:
                    half, lo_ = i % 2, b1_keys(i)[0] * P
                    masks = [MS[:, lo_ - P * qb + 256:lo_ - P * qb + 640] for qb in (2 * half, 2 * half + 1)]
                    row_max(b1, l, str(i), 3 * P, masks, 0.125, 1.0, sink=P1["sink"] + (i - STEPS) // 2)

            def softmax_rest(i):
                normalise(b1, l, str(i), P * len(b1_keys(i)), True if i >= STEPS else None)

            def rope(name, c):
                bank_ = G[c]
                dve.wait_ge(*own.last(0))
                nc.vector.tensor_tensor(TMP[:, 0, :], bank_[:, :], COS1, ALU.mult).then_inc(dve_step, own.step())
                for q in range(4):
                    to, of = slice((q ^ 1) * 32, (q ^ 1) * 32 + 32), slice(q * 32, q * 32 + 32)
                    dve.wait_ge(*own.last(1))
                    ins = nc.vector.tensor_tensor(TMP[to, 1, :], bank_[of, :], SIN1[of, :], ALU.mult)
                    if q == 3:
                        ins.then_inc(b1.free.sem, own.event(b1.free, l, name))
                    else:
                        ins.then_inc(dve_step, own.step())
                dve.wait_ge(*own.last(0))
                nc.vector.tensor_tensor(PRE[:, c, :], TMP[:, 0, :], TMP[:, 1, :], ALU.add) \
                    .then_inc(b1.pre.sem, own.event(b1.pre, l, name))

            def chunk(name):
                kind, c, bank_ = name[:2], B1_CHUNKS.index(name) % 2, G[B1_CHUNKS.index(name) % 2]
                if kind in ("av", "bc"):
                    return
                dve.wait_ge(b1.done.sem, b1.done.at(l, name))
                if kind in ("dq", "dk"):
                    t = AQ if kind == "dq" else AK
                    lo(b1, l, name, t[1][:, c, :], bank_[:, :], t[0][:, c, :])
                elif kind == "dv":
                    lo(b1, l, name, AV[1][:, :, c * P:(c + 1) * P],
                              bank_[:, :].rearrange("p (t n) -> p t n", t=4), AV[0][:, :, c * P:(c + 1) * P])
                elif kind in ("dz", "cz"):
                    dve.wait_ge(b1.aux.sem, b1.aux.at(l, name))
                    dve.wait_ge(*own.last(0))
                    nc.vector.scalar_tensor_tensor(ZB[:, c, :], TH, 1.0, bank_[:, :], ALU.add, ALU.mult) \
                        .then_inc(b1.free.sem, own.event(b1.free, l, name))
                elif kind == "au":
                    dve.wait_ge(b1.aux.sem, b1.aux.at(l, f"av{c}"))
                    dve.wait_ge(*own.last(0))
                    nc.vector.scalar_tensor_tensor(HA[:, c, PAD_A:PAD_A + S], CA[:, c, :], 1.0, bank_[:, :],
                                                   ALU.add, ALU.mult) \
                        .then_inc(b1.free.sem, own.event(b1.free, l, name))
                elif kind == "bx":
                    dve.wait_ge(b1.aux.sem, b1.aux.at(l, f"bc{c}"))
                    dve.wait_ge(*own.last(0))
                    nc.vector.tensor_tensor(CX[:, c, 1:1 + S], CB[:, c, :], bank_[:, :], ALU.mult) \
                        .then_inc(b1.free.sem, own.event(b1.free, l, name))
                    for j in range(3):
                        src, w = CX[:, c, j:j + S], par("conv_b_w", c * 3 + j)
                        if j == 0:
                            dve.wait_ge(*own.last(0))
                            nc.vector.tensor_scalar(CB[:, c, :], src, w, None, ALU.mult) \
                                .then_inc(dve_step, own.step())
                        else:
                            dve.wait_ge(*own.last(0))
                            nc.vector.scalar_tensor_tensor(CB[:, c, :], src, w, CB[:, c, :], ALU.mult, ALU.add) \
                                .then_inc(dve_step, own.step())
                elif kind == "bb":
                    dve.wait_ge(*own.last(0))
                    nc.vector.tensor_tensor(CB[:, c, :], CB[:, c, :], bank_[:, :], ALU.mult) \
                        .then_inc(b1.free.sem, own.event(b1.free, l, name))
                elif kind in ("bz", "az"):
                    i = [k for k, n in FILL.items() if n == name][0]
                    pre = PRE[:, (i + 1) % 2, :]
                    dve.wait_ge(b1.aux.sem, b1.aux.at(l, name))
                    dve.wait_ge(*own.last(0))
                    nc.vector.scalar_tensor_tensor(pre, TH, 1.0, bank_[:, :], ALU.add, ALU.mult) \
                        .then_inc(b1.free.sem, own.event(b1.free, l, name))
                    src, scale, tile = (CB, 0.5, 2 + c) if kind == "bz" else (CA, 0.25, c)
                    dve.wait_ge(*own.last(0))
                    nc.vector.scalar_tensor_tensor(pre, pre, scale, src[:, c, :], ALU.mult, ALU.mult) \
                        .then_inc(b1.pre.sem, own.event(b1.pre, l, "y" + name))
                    lo(b1, l, "y" + name, Y[1][:, tile, :], pre, Y[0][:, tile, :])
                elif kind == "cq":
                    dve.wait_ge(rope_in, 16 * l + 16)
                    rope(name, c)
                    lo(b1, l, name, AQ[1][:, c, :], PRE[:, c, :], AQ[0][:, c, :])
                elif name == "ck0":
                    rope(name, c)
                    dve.wait_ge(b1.hi.sem, b1.hi.at(l, "ck3"))
                    for g in range(2):
                        for half in range(2):
                            r = slice(g * HD, (g + 1) * HD)
                            lo(b1, l, f"ck{2 * g + half}", AK[1][half * HD:(half + 1) * HD, g, :],
                                      PRE[r, 0, :], AK[0][r, g, :])
                elif name == "ck1":
                    lo(b1, l, "cv", AV[1][:, :, 0:P], bank_[:, :].rearrange("p (t n) -> p t n", t=4),
                              AV[0][:, :, 0:P])

            def lo_y(i):
                h, half = (i % STEPS) // 2, i % 2
                r = slice(HD * (h % 2), HD * (h % 2) + HD)
                tile, cols = (6 if i < STEPS else 4) + h // 2, slice(half * 256, (half + 1) * 256)
                lo(b1, l, f"y{i}", Y[1][r, tile, cols], PRE[r, i % 2, 0:256], Y[0][r, tile, cols])

            for name in ("dq0", "dq1", "dk0", "dk1", "dv0", "dv1"):
                chunk(name)
            softmax_max(0)
            softmax_rest(0)
            chunk("dz0")
            chunk("dz1")
            for i in range(2 * STEPS):
                if i:
                    lo_y(i - 1)
                if i == STEPS:
                    for name in ("cq0", "cq1", "ck0", "ck1"):
                        chunk(name)
                    conv_a(TAPS["cz0"])
                    chunk("cz0")
                    softmax_max(i)
                    softmax_rest(i)
                    conv_a(TAPS["cz1"])
                    chunk("cz1")
                n = len(b1_keys(i))
                lo(b1, l, f"pt{i}a", PT1[1][:, 0:2, :], TB[0][:, :].rearrange("p (a n) -> p a n", a=2),
                          PT1[0][:, 0:2, :])
                lo(b1, l, f"pt{i}b", PT1[1][:, 2:n, :],
                          TB[1][:, 0:256 * (n - 2)].rearrange("p (a n) -> p a n", a=n - 2), PT1[0][:, 2:n, :])
                if i == LN_STEP:
                    mark(b1.acc, l, "mean")
                if i % STEPS < STEPS - 1:
                    softmax_max(i + 1)
                    softmax_rest(i + 1)
                if i == LN_STEP:
                    dve.wait_ge(b1.ss.sem, b1.ss.at(l, "mean"))
                    for c in range(2):
                        dve.wait_ge(*own.last(1))
                        nc.vector.scalar_tensor_tensor(CA[:, c, :], NB[:, :], -1.0 / (2 * P), CA[:, c, :],
                                                       ALU.mult, ALU.add) \
                            .then_inc(dve_step, own.step())
                    dve.wait_ge(*own.last(0))
                    nc.vector.tensor_tensor(ACC1[:, :], CA[:, 0, :], CA[:, 0, :], ALU.mult) \
                        .then_inc(dve_step, own.step())
                    dve.wait_ge(*own.last(0))
                    nc.vector.tensor_tensor(TMP[:, 1, :], CA[:, 1, :], CA[:, 1, :], ALU.mult) \
                        .then_inc(dve_step, own.step())
                    dve.wait_ge(*own.last(0))
                    nc.vector.tensor_tensor(ACC1[:, :], ACC1[:, :], TMP[:, 1, :], ALU.add) \
                        .then_inc(b1.acc.sem, own.event(b1.acc, l, "var"))
                    diagonals(b1, l, "var")
                    for c in range(2):
                        dve.wait_ge(*own.last(0))
                        nc.vector.tensor_tensor(CA[:, c, :], CA[:, c, :], NB[:, :], ALU.mult) \
                            .then_inc(dve_step, own.step())
                        dve.wait_ge(*own.last(0))
                        nc.vector.tensor_scalar(CA[:, c, :], CA[:, c, :], par("ln_g", c), par("ln_b", c),
                                                ALU.mult, ALU.add).then_inc(ln_in, own.reach(ln_in, 2 * l + (c + 1)))
                    for c in range(2):
                        dve.wait_ge(b1.aux.sem, b1.aux.at(l, f"ln{c}"))
                        dve.wait_ge(*own.last(0))
                        ins = nc.vector.scalar_tensor_tensor(CA[:, c, :], TMP[:, c, :], 1.0, CA[:, c, :],
                                                            ALU.add, ALU.mult)
                        if c:
                            ins.then_inc(ln_out, own.reach(ln_out, l + 1))
                        else:
                            ins.then_inc(dve_step, own.step())
                if i in TAPS:
                    conv_a(TAPS[i])
                if i in FILL:
                    chunk(FILL[i])
                h, half = (i % STEPS) // 2, i % 2
                of = HD * (h % 2) if i < STEPS else HD * (h // 2)
                r = slice(HD * (h % 2), HD * (h % 2) + HD)
                dve.wait_ge(b1.pv.sem, b1.pv.at(l, str(i)))
                dve.wait_ge(*own.last(0))
                nc.vector.scalar_tensor_tensor(PRE[r, i % 2, 0:256], OB[of:of + HD, 0:256], 0.5, ZB[r, h // 2,
                                               half * 256:(half + 1) * 256], ALU.mult, ALU.mult) \
                    .then_inc(b1.pre.sem, own.event(b1.pre, l, f"y{i}"))
            lo_y(2 * STEPS - 1)
            assert next(taps, None) is None
            for k in range(KT):
                residual(b1, l, f"o{k // 2}{k % 2}", k, ACC1[:, :])
            mark(b1.layer, l, "end")
            dve.wait_ge(*own.last(0))
            nc.vector.memset(spare_v[:, :], 0.0).then_inc(dve_step, own.step())
        own.leave(DEPTH)

        def final_norm(which, out_count=None):
            mark(bf.acc, which, "n")
            diagonals(bf, which, "n")
            for k in range(KT):
                dve.wait_ge(*own.last(1))
                ins = nc.vector.scalar_tensor_tensor(X[:, k, :], X[:, k, :], PARF[:,
                                                     which * KT + k:which * KT + k + 1], NB[:, :], ALU.mult,
                                                     ALU.mult)
                if out_count:
                    ins.then_inc(out_count.sem, own.event(out_count, 0, str(k)))
                else:
                    ins.then_inc(dve_step, own.step())

        final_norm(0)
        for k in range(KT):
            squares(ACC2, X[:, k, :], k == 0)

        with dve.Fori(0, DEPTH) as l:
            own.enter(l, DVE_ORDER_2)
            mark(b2.acc, l, "n")
            dve.wait_ge(par_in, 32 * l + 96)
            dve.wait_ge(*own.last(1))
            nc.vector.tensor_scalar(HB[:, 0:4], PAR2[:, P2["b_a"]:P2["b_a"] + 4], 0.5, None, ALU.mult) \
                .then_inc(dve_step, own.step())
            dve.wait_ge(*own.last(1))
            nc.vector.tensor_scalar(HB[:, 4:28], PAR2[:, P2["b_gate"]:P2["b_gate"] + 24], 0.5, None, ALU.mult) \
                .then_inc(dve_step, own.step())
            norm_to_h(b2, l, "n", "n", PAR2[:, P2["g_mix"]:P2["g_mix"] + KT])

            def par(name, k=0):
                return PAR2[:, P2[name] + k:P2[name] + k + 1]

            for n, name in enumerate(lats):
                dve.wait_ge(b2.done.sem, b2.done.at(l, name))
                dve.wait_ge(*own.last(1))
                nc.vector.tensor_copy(GT[:, n, :], G[n % 2][:, :]).then_inc(b2.free.sem, own.event(b2.free, l, name))
                if n < 3:
                    squares(ACC2, GT[:, n, :], n == 0)
                if n == 2:
                    mark(b2.acc, l, "q")
            diagonals(b2, l, "q")
            for k in range(5):
                if k == 3:
                    squares(ACC2, GT[:, 4, :], True)
                    squares(ACC2, GT[:, 5, :], False)
                    mark(b2.acc, l, "kv")
                    diagonals(b2, l, "kv")
                dve.wait_ge(*own.last(0))
                nc.vector.scalar_tensor_tensor(PRE[:, k % 2, :], GT[:, (0, 1, 2, 4, 5)[k], :], par("g_lat", k),
                                               NB[:, :], ALU.mult, ALU.mult) \
                    .then_inc(b2.pre.sem, own.event(b2.pre, l, f"l{k}"))
                lo(b2, l, f"l{k}", lat(1, k), PRE[:, k % 2, :], lat(0, k))
            dve.wait_ge(*own.last(0))
            nc.vector.tensor_tensor(TMP[64:96, 0, :], GT[64:96, 3, :], CS2[64:96, :], ALU.mult) \
                .then_inc(dve_step, own.step())
            dve.wait_ge(*own.last(0))
            nc.vector.tensor_tensor(TMP[64:96, 1, :], GT[96:128, 3, :], CS2[96:128, :], ALU.mult) \
                .then_inc(dve_step, own.step())
            dve.wait_ge(*own.last(0))
            nc.vector.tensor_tensor(PRE[64:96, 1, :], TMP[64:96, 0, :], TMP[64:96, 1, :], ALU.add) \
                .then_inc(b2.pre.sem, own.event(b2.pre, l, "kr"))
            dve.wait_ge(b2.hi.sem, b2.hi.at(l, "kr"))
            for a in range(2):
                dve.wait_ge(*own.last(0))
                ins = nc.vector.tensor_tensor(K2[1][64:96, a, :], PRE[64:96, 1, :], K2[0][64:96, a,
                                              :].bitcast(F32), ALU.subtract)
                if a:
                    ins.then_inc(b2.lo.sem, own.event(b2.lo, l, "kr"))
                else:
                    ins.then_inc(dve_step, own.step())
            dve.wait_ge(*own.last(0))
            nc.vector.memset(spare_v[:, :], 0.0).then_inc(dve_step, own.step())
            with dve.Fori(0, 2) as j:
                own.enter(j, DVE_ORDER_H)
                for jj in range(2):
                    def q_part(a):
                        name = f"q{jj}{a}"
                        dve.wait_ge(b2.done.sem, b2.done.at(l, name, "h", j))
                        dve.wait_ge(*own.last(0))
                        nc.vector.tensor_copy(PRE[0:64, a, :], G[a][0:64, :]).then_inc(dve_step, own.step())
                        dve.wait_ge(*own.last(1))
                        nc.vector.tensor_tensor(TMP[64:96, 0, :], G[a][64:96, :], CS2[64:96, :], ALU.mult) \
                            .then_inc(dve_step, own.step())
                        dve.wait_ge(*own.last(1))
                        nc.vector.tensor_tensor(TMP[64:96, 1, :], G[a][96:128, :], CS2[96:128, :], ALU.mult) \
                            .then_inc(b2.free.sem, own.event(b2.free, l, name, "h", j))
                        dve.wait_ge(*own.last(0))
                        nc.vector.tensor_tensor(PRE[64:96, a, :], TMP[64:96, 0, :], TMP[64:96, 1, :], ALU.add) \
                            .then_inc(b2.pre.sem, own.event(b2.pre, l, name, "h", j))
                        lo(b2, l, name, Q2[1][0:96, :], PRE[0:96, a, :], Q2[0][0:96, :], "h", j)

                    def softmax(s):
                        w = (256, 512)[s % 2]
                        masks = [MC[:, 384 - P * qb:384 - P * qb + w] for qb in (2 * (s % 2), 2 * (s % 2) + 1)]
                        row_max(b2, l, f"{jj}{s}", w, masks, 1.0, 96.0 ** -0.5, "h", j)
                        normalise(b2, l, f"{jj}{s}", w, None, "h", j)

                    def lo_y(s):
                        a, half = divmod(s, 2)
                        r = slice(a * HD, (a + 1) * HD)

                        def at(part):
                            return Y[part][r, bass.ds(2 * j + (2 + jj), 1), half * 256:(half + 1) * 256].rearrange(
                                "p a n -> p (a n)")

                        lo(b2, l, f"y{jj}{s}", at(1), OB[r, 0:256], at(0), "h", j)

                    q_part(0)
                    for a in range(2):
                        lo(b2, l, f"k{jj}{a}", K2[1][0:64, a, :], G[1][a * 64:(a + 1) * 64, :],
                                  K2[0][0:64, a, :], "h", j)
                    lo(b2, l, f"v{jj}", V2[1][:, :, :], G[0][:, :].rearrange("p (t n) -> p t n", t=4),
                              V2[0][:, :, :], "h", j)
                    softmax(0)
                    for s in range(4):
                        if s:
                            lo_y(s - 1)
                        for n in range(1 + s % 2):
                            lo(b2, l, f"pt{jj}{s}" + "ab"[n], PT2[1][:, 2 * n:2 * n + 2, :],
                                      TB[n][:, :].rearrange("p (a n) -> p a n", a=2),
                                      PT2[0][:, 2 * n:2 * n + 2, :], "h", j)
                        if s == 0:
                            softmax(1)
                            q_part(1)
                        elif s < 3:
                            softmax(s + 1)
                    lo_y(3)
                dve.wait_ge(*own.last(0))
                nc.vector.memset(spare_v[:, :], 0.0).then_inc(dve_step, own.step())
            own.leave(2)

            dve.wait_ge(b2.done.sem, b2.done.at(l, "pl0", "mid"))
            dve.wait_ge(*own.last(0))
            nc.vector.memset(UP[:, :, :], 0.0).then_inc(dve_step, own.step())
            dve.wait_ge(*own.last(1))
            nc.vector.memset(L[:, :, :], 0.0).then_inc(dve_step, own.step())
            for n, name in enumerate(mid):
                dve.wait_ge(b2.done.sem, b2.done.at(l, name, "mid"))
                dve.wait_ge(*own.last(0))
                nc.vector.tensor_copy(UP[:, n, POOLPAD:], G[n % 2][:, :]) \
                    .then_inc(b2.free.sem, own.event(b2.free, l, name, "mid"))
                if n != 1:
                    continue
                flat = L[:, :, :].rearrange("p a n -> p (a n)")
                size = S + POOLPAD
                A_, B_ = flat[:, 0:size], flat[:, size:2 * size]
                for c in range(2):
                    u = UP[:, c, :]

                    def shifted(out, in_, by, rows=slice(0, P)):
                        dve.wait_ge(*own.last(0))
                        nc.vector.tensor_tensor(out[rows, POOLPAD:], in_[rows, POOLPAD:], in_[rows,
                                                POOLPAD - by:size - by], ALU.add) \
                            .then_inc(dve_step, own.step())

                    shifted(A_, u, 1)
                    shifted(B_, A_, 2)
                    sums = [(A_, 2), (B_, 4)]
                    if c:
                        shifted(A_, B_, 4)
                        shifted(B_, A_, 8, slice(64, P))
                        sums = [(A_, 8), (B_, 16)]
                    for g, (sum_, w) in enumerate(sums):
                        r = slice(64 * g, 64 * g + 64)
                        dve.wait_ge(*own.last(0))
                        nc.vector.scalar_tensor_tensor(PRE[r, c, :], sum_[r, POOLPAD:], 1.0 / w, u[r,
                                                       POOLPAD:], ALU.mult, ALU.subtract) \
                            .then_inc(dve_step, own.step())
                        dve.wait_ge(*own.last(0))
                        nc.vector.tensor_tensor(PRE[r, c, 0:POOLPAD], sum_[r, POOLPAD:2 * POOLPAD], IC[r, c,
                                                :], ALU.mult) \
                            .then_inc(dve_step, own.step())
                        dve.wait_ge(*own.last(0))
                        ins = nc.vector.tensor_tensor(PRE[r, c, 0:POOLPAD], PRE[r, c, 0:POOLPAD], u[r,
                                                      POOLPAD:2 * POOLPAD], ALU.subtract)
                        if g:
                            ins.then_inc(b2.pre.sem, own.event(b2.pre, l, f"pm{c}", "mid"))
                        else:
                            ins.then_inc(dve_step, own.step())
                    lo(b2, l, f"pm{c}", MX[1][:, c, :], PRE[:, c, :], MX[0][:, c, :], "mid")
            for c in range(2):
                dve.wait_ge(b2.sm.sem, b2.sm.at(l, f"p{c}"))
                dve.wait_ge(*own.last(0))
                nc.vector.tensor_scalar(PRE[:, c, :], SC[c][:, :], par("scale", c), None, ALU.mult) \
                    .then_inc(b2.pre.sem, own.event(b2.pre, l, f"py{c}", "mid"))
                lo(b2, l, f"py{c}", Y[1][:, c, :], PRE[:, c, :], Y[0][:, c, :], "mid")
            for c in range(2):
                for t in range(4):
                    src, w = UP[:, 2 + c, POOLPAD - 3 + t:POOLPAD - 3 + t + S], par("conv_w", 4 * c + t)
                    if t == 0:
                        dve.wait_ge(*own.last(0))
                        nc.vector.tensor_scalar(L[:, c, :], src, w, par("conv_b", c), ALU.mult, ALU.add) \
                            .then_inc(dve_step, own.step())
                    else:
                        dve.wait_ge(*own.last(0))
                        ins = nc.vector.scalar_tensor_tensor(L[:, c, :], src, w, L[:, c, :], ALU.mult, ALU.add)
                        if t == 3:
                            ins.then_inc(b2.pre.sem, own.event(b2.pre, l, f"uc{c}", "mid"))
                        else:
                            ins.then_inc(dve_step, own.step())
                lo(b2, l, f"uc{c}", MX[1][:, c, :], L[:, c, :], MX[0][:, c, :], "mid")
            lam = PAR2[:, P2["lam"]:P2["lam"] + 2]
            dve.wait_ge(*own.last(0))
            nc.vector.scalar_tensor_tensor(LS[:, 0:2], lam, -1.0, lam, ALU.mult, ALU.max) \
                .then_inc(b2.lru.sem, own.event(b2.lru, l, "sp"))
            dve.wait_ge(b2.aux.sem, b2.aux.at(l, "sp", "mid"))
            dve.wait_ge(*own.last(0))
            nc.vector.tensor_scalar(LS[:, 4:6], LS[:, 2:4], 2.0, None, ALU.add).then_inc(dve_step, own.step())
            dve.wait_ge(*own.last(0))
            nc.vector.reciprocal(LS[:, 4:6], LS[:, 4:6]).then_inc(dve_step, own.step())
            dve.wait_ge(*own.last(0))
            nc.vector.tensor_tensor(LS[:, 4:6], LS[:, 4:6], LS[:, 2:4], ALU.mult).then_inc(dve_step, own.step())
            dve.wait_ge(*own.last(0))
            nc.vector.tensor_tensor(LS[:, 6:8], LS[:, 4:6], LS[:, 4:6], ALU.mult).then_inc(dve_step, own.step())
            dve.wait_ge(*own.last(0))
            nc.vector.memset(LS[:, 8:10], 1.0 / 17).then_inc(dve_step, own.step())
            for d in range(15, 0, -2):
                dve.wait_ge(*own.last(0))
                nc.vector.tensor_tensor(LS[:, 8:10], LS[:, 8:10], LS[:, 6:8], ALU.mult) \
                    .then_inc(dve_step, own.step())
                dve.wait_ge(*own.last(0))
                nc.vector.tensor_scalar(LS[:, 8:10], LS[:, 8:10], 1.0 / d, None, ALU.add) \
                    .then_inc(dve_step, own.step())
            dve.wait_ge(*own.last(0))
            nc.vector.tensor_tensor(LS[:, 8:10], LS[:, 8:10], LS[:, 4:6], ALU.mult).then_inc(dve_step, own.step())
            dve.wait_ge(*own.last(0))
            nc.vector.tensor_scalar(LS[:, 10:12], lam, -1.0, 0.0, ALU.mult, ALU.max).then_inc(dve_step, own.step())
            dve.wait_ge(*own.last(0))
            nc.vector.scalar_tensor_tensor(LS[:, 10:12], LS[:, 8:10], 2.0, LS[:, 10:12], ALU.mult, ALU.add) \
                .then_inc(dve_step, own.step())
            dve.wait_ge(*own.last(0))
            nc.vector.tensor_scalar(LS[:, 12:14], LS[:, 10:12], 4.0, None, ALU.mult).then_inc(dve_step, own.step())
            dve.wait_ge(*own.last(0))
            nc.vector.tensor_scalar(LS[:, 14:16], LS[:, 10:12], -4.0, None, ALU.mult) \
                .then_inc(ls_ready, own.reach(ls_ready, l + 1))
            for c in range(2):
                dve.wait_ge(b2.aux.sem, b2.aux.at(l, f"sq{c}", "mid"))
                dve.wait_ge(*own.last(0))
                nc.vector.scalar_tensor_tensor(L[:, 4, :], L[:, 6, :], 1.0, L[:, 4, :], ALU.add, ALU.mult) \
                    .then_inc(b2.lru.sem, own.event(b2.lru, l, f"c{c}"))
                dve.wait_ge(*own.last(0))
                nc.vector.scalar_tensor_tensor(L[:, 3, :], L[:, 3, :], 1.0, L[:, c, :], ALU.add, ALU.mult) \
                    .then_inc(dve_step, own.step())
                dve.wait_ge(b2.aux.sem, b2.aux.at(l, f"rt{c}", "mid"))
                dve.wait_ge(*own.last(0))
                nc.vector.scalar_tensor_tensor(L[:, 3, :], L[:, 3, :], 0.5, L[:, 6, :], ALU.mult, ALU.mult) \
                    .then_inc(dve_step, own.step())
                dve.wait_ge(*own.last(0))
                nc.vector.tensor_tensor_scan(PRE[:, c, :], L[:, 5, :], L[:, 3, :], 0.0, ALU.mult, ALU.add) \
                    .then_inc(b2.pre.sem, own.event(b2.pre, l, f"lh{c}", "mid"))
                lo(b2, l, f"lh{c}", Y[1][:, 6 + c, :], PRE[:, c, :], Y[0][:, 6 + c, :], "mid")
            dve.wait_ge(*own.last(0))
            nc.vector.memset(spare_v[:, :], 0.0).then_inc(dve_step, own.step())
            with dve.Fori(0, 4) as m:
                own.enter(m, DVE_ORDER_M)
                for c in range(2):
                    A_, B_, C_ = ((SC[0], SC[1], TB[0]), (TB[1], OB, NB))[c]
                    dve.wait_ge(b2.br.sem, b2.br.at(l, str(c), "m", m))
                    dve.wait_ge(b2.aux.sem, b2.aux.at(l, f"t{c}", "m", m))

                    def gate(g):
                        return GT[:, bass.ds(2 * m + (8 * g + c), 1), :].rearrange("p a n -> p (a n)")

                    dve.wait_ge(*own.last(0))
                    nc.vector.scalar_tensor_tensor(TMP[:, 0, :], gate(0), 1.0, A_[:, :], ALU.add, ALU.mult) \
                        .then_inc(dve_step, own.step())
                    dve.wait_ge(*own.last(1))
                    nc.vector.scalar_tensor_tensor(TMP[:, 1, :], gate(1), 1.0, B_[:, :], ALU.add, ALU.mult) \
                        .then_inc(dve_step, own.step())
                    dve.wait_ge(*own.last(0))
                    nc.vector.tensor_tensor(TMP[:, 0, :], TMP[:, 0, :], TMP[:, 1, :], ALU.add) \
                        .then_inc(dve_step, own.step())
                    dve.wait_ge(*own.last(0))
                    nc.vector.scalar_tensor_tensor(TMP[:, 1, :], L[:, c, :], 1.0, C_[:, :], ALU.add, ALU.mult) \
                        .then_inc(b2.brf.sem, own.event(b2.brf, l, str(c), "m", m))
                    dve.wait_ge(*own.last(0))
                    nc.vector.tensor_tensor(PRE[:, c, :], TMP[:, 0, :], TMP[:, 1, :], ALU.add) \
                        .then_inc(b2.pre.sem, own.event(b2.pre, l, f"b{c}", "m", m))

                    def at(part):
                        return MRG[part][:, bass.ds(2 * m + c, 1), :].rearrange("p a n -> p (a n)")

                    lo(b2, l, f"b{c}", at(1), PRE[:, c, :], at(0), "m", m, half=True)
                dve.wait_ge(*own.last(0))
                nc.vector.memset(spare_v[:, :], 0.0).then_inc(dve_step, own.step())
            own.leave(4)
            for k in range(KT):
                residual(b2, l, f"o{k}", k, ACC2, "out")
            mark(b2.acc, l, "e")
            norm_to_h(b2, l, "e", "e", PAR2[:, P2["g_ffn"]:P2["g_ffn"] + KT], "n2")
            dve.wait_ge(*own.last(0))
            nc.vector.memset(spare_v[:, :], 0.0).then_inc(dve_step, own.step())
            with dve.Fori(0, 4) as f:
                own.enter(f, DVE_ORDER_F)
                for n in range(KT):
                    dve.wait_ge(b2.aux.sem, b2.aux.at(l, f"u{n}", "f", f))
                    dve.wait_ge(*own.last(1))
                    nc.vector.tensor_tensor(PRE[:, n % 2, :], TMP[:, n % 2, :], TMP[:, n % 2, :], ALU.mult) \
                        .then_inc(b2.pre.sem, own.event(b2.pre, l, f"u{n}", "f", f))
                    lo(b2, l, f"u{n}", Y[1][:, n, :], PRE[:, n % 2, :], Y[0][:, n, :], "f", f)
                for n in range(KT):
                    residual(b2, l, f"d{n}", n, ACC2, "f", f)
                dve.wait_ge(*own.last(0))
                nc.vector.memset(spare_v[:, :], 0.0).then_inc(dve_step, own.step())
            own.leave(4)
            mark(b2.layer, l, "end")
            dve.wait_ge(*own.last(0))
            nc.vector.memset(spare_v[:, :], 0.0).then_inc(dve_step, own.step())
        own.leave(DEPTH)
        final_norm(1, final)


def tables():
    f = np.float32
    t = np.arange(S, dtype=f)
    inv = (f(10000.0) ** (-np.arange(0, HD, 2, dtype=f) / f(HD))).astype(f)
    ang = (t[None, :] * inv[:, None]).astype(f)
    cos, sin = np.cos(ang), np.sin(ang)
    rope1 = np.concatenate([np.concatenate([cos] * 4, 0), np.concatenate([sin, -sin] * 2, 0)], 1).astype(f)
    inv = (f(10000.0) ** (-np.arange(0, 32, 2, dtype=f) / f(32))).astype(f)
    ang = (t[None, :] * inv[:, None]).astype(f)
    cos, sin = np.cos(ang), np.sin(ang)
    rope2 = np.concatenate([np.zeros((64, S), f), cos, cos, -sin, sin], 0).astype(f)
    q, k = np.arange(P)[:, None], np.arange(640)[None, :]
    window = np.where(np.abs(k - 256 - q) <= 128, 0.0, NEG).astype(f)
    causal = np.where(k - 384 <= q, 0.0, NEG).astype(f)
    c, kc = np.arange(GRID)[:, None], np.arange(GRID)[None, :]
    c0 = np.clip(c - 8, 0, GRID - 16)
    columns = np.where((kc >= c0) & (kc < c0 + 16), 0.0, NEG).astype(f)
    columns = np.concatenate([columns] * 2, 0)
    counts = np.zeros((P, 2, POOLPAD), f)
    for n, w in enumerate((2, 4, 8, 16)):
        counts[64 * (n % 2):64 * (n % 2) + 64, n // 2, :] = 1.0 / np.minimum(np.arange(POOLPAD) + 1, w)
    return {"rope1": rope1, "rope2": rope2, "window": window, "causal": causal, "columns": columns,
            "counts": counts, "ident": np.eye(P, dtype=f)}


def unit_of(w, col, width=256):
    kt = w.shape[0] // P
    out = np.zeros((P, KT, 256), np.float32)
    out[:, 0:kt, 0:width] = w[:, col:col + width].reshape(kt, P, width).transpose(1, 0, 2)
    return out.reshape(P, 2048)


def pack_stream(a):
    units = []
    for l in range(DEPTH):
        for u in B1_UNITS[:14]:
            units.append(unit_of(a["w_in"][l], B1_COLS[u]))
        for m in range(4):
            units.append(unit_of(a["w_out"][l], 256 * m))
    for l in range(DEPTH):
        w, q_up, kv_up = a["w_in_2"][l], a["w_q_up_2"][l], a["w_kv_up_2"][l]
        units.append(unit_of(w, 256))
        kr = w[:, 896:928]
        units.append(unit_of(np.concatenate([w[:, 512:640], np.zeros((D, 64), np.float32), kr,
                                             kr[:, 16:32], kr[:, 0:16]], 1), 0))
        units.append(unit_of(w, 640))
        for pair in range(4):
            q = []
            for h in (2 * pair, 2 * pair + 1):
                c = q_up[:, 96 * h:96 * h + 96]
                q += [c, c[:, 80:96], c[:, 64:80]]
            heads = [kv_up[:, P * h:P * h + P] for h in (2 * pair, 2 * pair + 1)]
            kv = np.concatenate([heads[0][:, 0:64], heads[1][:, 0:64], heads[0][:, 64:], heads[1][:, 64:]], 1)
            units.append(unit_of(np.concatenate([np.concatenate(q, 1), kv], 0), 0))
            for g in range(2):
                units.append(unit_of(w, 1184 + 1024 * g + 256 * pair))
        units.append(unit_of(w, 0))
        units.append(unit_of(w, 928))
        small = np.zeros((KT * P, P), np.float32)
        for n, name in enumerate(("w_pool_grp_2", "w_lru_a_2", "w_lru_x_2")):
            for g in range(4):
                at = (2 * n + g // 2) * P + 64 * (g % 2)
                small[at:at + 64, 64 * (g % 2):64 * (g % 2) + 64] = a[name][l][g]
        units.append(unit_of(small, 0, P))
        branches = np.concatenate([a["w_pool_proj_2"][l], a["w_mla_o_2"][l], a["w_lru_proj_2"][l]], 0)
        for m in range(4):
            units.append(unit_of(w, 1184 + 2048 + 256 * m))
            units.append(unit_of(branches, 256 * m))
        for m in range(4):
            units.append(unit_of(a["w_out_2"][l], 256 * m))
        for g in range(4):
            for m in range(4):
                units.append(unit_of(a["w_ff1_2"][l], 1024 * g + 256 * m))
            for m in range(4):
                units.append(unit_of(a["w_ff2_2"][l][1024 * g:1024 * (g + 1)], 256 * m))
    return np.stack(units)


def columns_of(x):
    return x.reshape(-1, P).T


def pack_params(a):
    par1, par2 = [], []
    for l in range(DEPTH):
        taps_a = a["conv_a_w"][l].reshape(CONV_A, 2, P).transpose(2, 1, 0).reshape(P, -1)
        taps_b = a["conv_b_w"][l].reshape(3, 2, P).transpose(2, 1, 0).reshape(P, -1)
        par1.append(np.concatenate([columns_of(a["norm_g"][l]), taps_a, columns_of(a["conv_a_b"][l]),
                                    columns_of(a["ln_a_g"][l]), columns_of(a["ln_a_b"][l]), taps_b,
                                    np.tile(a["swa_sink"][l][None, :], (P, 1))], 1))
        taps = a["conv_w_2"][l].reshape(4, 2, P).transpose(2, 1, 0).reshape(P, -1)
        par2.append(np.concatenate([columns_of(a["g_mix_2"][l]), columns_of(a["pool_scale_2"][l]),
                                    columns_of(a["g_q_2"][l]), columns_of(a["g_kv_2"][l]), taps,
                                    columns_of(a["conv_b_2"][l]), columns_of(a["b_lru_a_2"][l]),
                                    columns_of(a["b_lru_x_2"][l]), columns_of(a["lru_lambda_2"][l]),
                                    columns_of(a["b_gate_2"][l]), columns_of(a["g_ffn_2"][l])], 1))
    return np.stack(par1), np.stack(par2)


def slide_bias(rpb):
    flat = rpb.reshape(-1, 15, 31)
    wide = np.pad(flat, ((0, 0), (0, 0), (GRID - 16, GRID - 16)))
    out = np.stack([np.stack([wide[:, 1 - r:15 - r, GRID - 1 - cq:2 * GRID - 1 - cq] for cq in range(GRID)], 1)
                    for r in range(2)], 1)
    return out.reshape(-1, P, 14 * GRID)


def kernel(**inputs):
    import concourse.bacc as bacc
    from concourse.bass_utils import run_bass_kernel_spmd

    a = {k: np.asarray(v) for k, v in inputs.items()}
    arrays = dict(tables())
    arrays["x"] = np.ascontiguousarray(a["x"][0].T.reshape(KT, P, S).transpose(1, 0, 2))
    arrays["stream"] = pack_stream(a)
    arrays["par1"], arrays["par2"] = pack_params(a)
    arrays["finals"] = np.concatenate([columns_of(a["final_norm_g"]), columns_of(a["g_final_2"])], 1)
    arrays["bias"] = slide_bias(a["na_rpb"])
    nc = bacc.Bacc("TRN2", target_bir_lowering=False, num_devices=1)
    dram, feed = {}, {}
    for name, value in arrays.items():
        value = np.ascontiguousarray(value)
        feed[f"in_{name}"] = value
        dram[name] = nc.dram_tensor(f"in_{name}", value.shape, mybir.dt.from_np(value.dtype),
                                    kind="ExternalInput").ap()
    dram["out"] = nc.dram_tensor("out_0", (P, KT, S), F32, kind="ExternalOutput").ap()
    build(nc, dram)
    r = run_bass_kernel_spmd(nc, [feed], core_ids=[0])
    out = r.results[0]["out_0"]
    return np.ascontiguousarray(out.transpose(2, 1, 0).reshape(1, S, D))
```

```python
from contextlib import ExitStack

import numpy as np

import concourse.bass as bass
from concourse import mybir

F32 = mybir.dt.float32
F32R = mybir.dt.float32r
ALU = mybir.AluOpType
ACT = mybir.ActivationFunctionType

P = 128
S = 512
D = 1024
KT = D // P
DEPTH = 2
EPS = 1e-6
NEG = -8e30
HD = 64
GRID = 64
CONV_A = 31
PAD_A = CONV_A // 2
POOLPAD = 16
U1 = 18
U2 = 62
UNITS = DEPTH * (U1 + U2)

P1 = {}
_n = 0
for _k, _w in (("norm_g", 8), ("conv_a_w", 2 * CONV_A), ("conv_a_b", 2), ("ln_g", 2), ("ln_b", 2),
               ("conv_b_w", 6), ("sink", 4)):
    P1[_k] = _n
    _n += _w
NP1 = _n
P2 = {}
_n = 0
for _k, _w in (("g_mix", 8), ("scale", 2), ("g_lat", 5), ("conv_w", 8), ("conv_b", 2), ("b_a", 2),
               ("b_x", 2), ("lam", 2), ("b_gate", 24), ("g_ffn", 8)):
    P2[_k] = _n
    _n += _w
NP2 = _n


COUNTS = []


class Count:

    def __init__(self, sem, start, segments):
        self.sem, self.start, self.at_, off = sem, start, {}, 0
        for seg, reps, names in segments:
            for k, name in enumerate(names):
                assert (seg, name) not in self.at_, name
                self.at_[seg, name] = (off + k + 1, len(names))
            off += reps * len(names)
        self.total = off
        COUNTS.append(self)

    def at(self, l, name, seg="", i=0):
        k, step = self.at_[seg, name]
        return l * self.total + i * step + (self.start + k)

    def end(self):
        return self.start + DEPTH * self.total


class Own:

    def __init__(self, sem):
        self.sem, self.base, self.n, self.recent, self.outer = sem, 0, 0, [], []

    def step(self):
        self.n += 1
        self.recent.append((self.sem, self.base + self.n))
        return 1

    def reach(self, sem, value):
        self.recent.append((sem, value))
        return 1

    def event(self, count, l, name, seg="", i=0):
        return self.reach(count.sem, count.at(l, name, seg, i))

    def last(self, behind=0):
        return self.recent[max(0, len(self.recent) - 1 - behind)]

    def enter(self, i, per):
        self.outer.append((self.base, self.n, per))
        self.base, self.n = self.base + self.n + i * per, 0
        self.recent = 3 * [(self.sem, self.base)]

    def leave(self, times):
        base, n, per = self.outer.pop()
        assert self.n == per, f"the body counts {self.n}, not {per}"
        self.base, self.n = base, n + times * per
        self.recent = 3 * [(self.sem, self.base + self.n)]


B1_UNITS = ["dq", "dk", "dv", "dz", "av", "au", "bc", "bx", "cq", "ck", "cz", "bb", "bz", "az",
            "o0", "o1", "o2", "o3"]
B1_CHUNKS = [u + str(c) for u in B1_UNITS for c in range(2)]
B1_COLS = {"dq": 2560, "dk": 2816, "dv": 3072, "dz": 3328, "av": 256, "au": 0, "bc": 1024, "bx": 1280,
           "cq": 1792, "ck": 2048, "cz": 2304, "bb": 768, "bz": 1536, "az": 512}
N_CONST = 4
LN_STEP = 9
ACT_STEPS_1 = 35
ACT_STEPS_2 = 33
ACT_STEPS_H = 9
ACT_STEPS_M = 1
ACT_STEPS_F = 1
DVE_STEPS_1 = 234
DVE_STEPS_2 = 325
DVE_STEPS_H = 49
DVE_STEPS_M = 7
DVE_STEPS_F = 24
STEPS = 8
FILL = {0: "av0", 1: "av1", 2: "au0", 3: "au1", 4: "bc0", 5: "bc1", 6: "bx0", 7: "bx1",
        8: "bb0", 9: "bb1", 10: "bz0", 11: "bz1", 12: "az0", 13: "az1", 14: "o00", 15: "o01"}
LAST_Y = 5
TAPS = {4: 8, 5: 8, 6: 4, 7: 4, "cz0": 12, "cz1": 10, 8: 8, 9: 8}


def b1_splits():
    out = [f"n{k}" for k in range(KT)] + ["dq0", "dq1", "dk0", "dk1", "dv0", "dv1"]
    for i in range(2 * STEPS):
        if i == STEPS:
            out += ["cq0", "cq1", "ck0", "ck1", "ck2", "ck3", "cv"]
        out += [f"pt{i}a", f"pt{i}b"]
        fill = FILL.get(i, "")
        if i == LN_STEP + 4:
            out.append("y" + FILL[i - 1])
        if fill[:2] in ("bz", "az") and i != LN_STEP + 3:
            out.append("y" + fill)
        out.append(f"y{i}")
    return out


def head_names(jj):
    out = [f"q{jj}0", f"k{jj}0", f"k{jj}1", f"v{jj}"]
    for s in range(4):
        out += [f"pt{jj}{s}{b}" for b in ("ab" if s % 2 else "a")]
        if s == 0:
            out.append(f"q{jj}1")
        out.append(f"y{jj}{s}")
    return out


def build(nc, dram):
    COUNTS.clear()
    with ExitStack() as ctx:
        _build(nc, dram, ctx)


def _build(nc, dram, ctx):
    def sem(name):
        return ctx.enter_context(nc.semaphore(name))

    def sb(name, shape, dt=F32, where=ctx):
        return where.enter_context(nc.sbuf_tensor(name, shape, dt))

    def two(name, shape, where=ctx):
        return (sb(name + "_hi", shape, F32R, where), sb(name + "_lo", shape, F32R, where))

    X = sb("X", [P, KT, S])
    H = two("H", [P, KT, S])
    Y = two("Y", [P, KT, S])
    W_raw = sb("W_raw", [P, 2, 2048])
    W = two("W", [P, 2, 2048])
    PRE = sb("PRE", [P, 2, S])
    TMP = sb("TMP", [P, 2, S])
    ident = sb("ident", [P, P])
    ones = sb("ones", [P, P])
    PR = sb("PR", [P, 2, S])
    SM = sb("SM", [P, 16])
    NR = sb("NR", [P, 4])
    spare = sb("spare", [P, 1])
    spare_a = sb("spare_a", [P, 1])
    spare_v = sb("spare_v", [P, 1])
    EPSC = sb("EPSC", [P, 1])
    PARF = sb("PARF", [P, 2 * KT])

    banks = [ctx.enter_context(nc.psum_tensor(f"bank{i}", [P, S], F32)) for i in range(8)]
    G, SC, TB, OB, NB = banks[0:2], banks[2:4], banks[4:6], banks[6], banks[7]

    w_raw = [sem("w_raw0"), sem("w_raw1")]
    w_hi = sem("w_hi")
    w_lo = sem("w_lo")
    consts_in = sem("consts_in")
    x_in = [sem(f"x_in{k}") for k in range(4)]
    start = sem("start")
    par_in = sem("par_in")
    bias_in = [sem("bias_in0"), sem("bias_in1")]
    rope_in = sem("rope_in")
    x_out = sem("x_out")
    ln_in, ln_out, ls_ready = sem("ln_in"), sem("ln_out"), sem("ls_ready")
    act_step, dve_step, pool_step = sem("act_step"), sem("dve_step"), sem("pool_step")

    class Block:
        pass

    b1 = Block()
    b1.done = Count(sem("proj_done1"), 1, [("", 1, B1_CHUNKS)])
    split_names = b1_splits()
    b1.hi = Count(sem("split_hi1"), 0, [("", 1, split_names)])
    b1.lo = Count(sem("split_lo1"), 0, [("", 1, split_names)])
    b1.pre = Count(sem("pre1"), 0, [("", 1, [n for n in split_names if n[0] in "ny"
                                              or n in ("cq0", "cq1", "ck0")])])
    freed = [c for c in B1_CHUNKS if c[:2] not in ("dq", "dk", "dv", "av", "bc") and c != "ck1"]
    b1.free = Count(sem("proj_free1"), 1, [("", 1, freed)])
    b1.aux = Count(sem("act_aux1"), 0, [("", 1, ["dz0", "dz1", "av0", "av1", "bc0", "bc1", "cz0", "cz1",
                                                 "bz0", "bz1", "ln0", "ln1", "az0", "az1"])])
    steps = [str(i) for i in range(2 * STEPS)]
    b1.sc = Count(sem("scores1"), 0, [("", 1, steps)])
    b1.red = Count(sem("rowmax1"), 0, [("", 1, steps)])
    b1.ex = Count(sem("exp1"), 0, [("", 1, steps)])
    b1.pn = Count(sem("probs1"), 0, [("", 1, steps)])
    b1.tr = Count(sem("transposed1"), 0, [("", 1, steps)])
    b1.pv = Count(sem("attended1"), 1, [("", 1, steps)])
    norms1 = ["n", "mean", "var"]
    b1.acc = Count(sem("norm_acc1"), 0, [("", 1, norms1)])
    b1.ss = Count(sem("norm_sum1"), 0, [("", 1, norms1)])
    b1.rt = Count(sem("norm_root1"), 0, [("", 1, ["n", "var"])])
    b1.dg = Count(sem("norm_diag1"), 0, [("", 1, ["n", "var"])])
    b1.bc = Count(sem("norm_spread1"), 0, [("", 1, ["n", "var"])])
    b1.layer = Count(sem("layer1"), 1, [("", 1, ["end"])])

    b2 = Block()
    lats = ["kv0", "kv1", "q00", "q01", "q2", "kr"]
    pair_chunks = [f"{n}{jj}{s}" for jj in range(2) for n, s in
                   (("q", 0), ("k", 0), ("v", 0), ("q", 1), ("g", 0), ("g", 1), ("g", 2), ("g", 3))]
    gates = ["t0", "t1"]
    outs = [f"o{m}" for m in range(KT)]
    ups, downs = [f"u{m}" for m in range(KT)], [f"d{m}" for m in range(KT)]
    pools = ["lr0", "lr1", "pl0", "pl1"]
    b2.done = Count(sem("proj_done2"), 1, [("", 1, lats), ("h", 2, pair_chunks), ("mid", 1, pools + gates),
                                            ("m", 3, gates), ("out", 1, outs), ("f0", 1, ups),
                                            ("f", 3, downs + ups), ("f3", 1, downs)])
    mid = ["uc0", "uc1", "pm0", "pm1", "lh0", "lh1", "py0", "py1"]
    norm_tiles = [f"n{k}" for k in range(KT)]
    sp = [("", 1, norm_tiles + ["l0", "l3", "l4", "l1", "l2", "kr"]),
          ("h", 2, head_names(0) + head_names(1)), ("mid", 1, mid),
          ("m", 3, ["b0", "b1"]), ("m3", 1, ["b0", "b1"]),
          ("n2", 1, [f"e{k}" for k in range(KT)]), ("f0", 1, ups), ("f", 3, ups)]
    b2.hi = Count(sem("split_hi2"), 0, sp)
    b2.lo = Count(sem("split_lo2"), 0, sp)
    qnames = [f"q{jj}{a}" for jj in range(2) for a in range(2)]
    b2.pre = Count(sem("pre2"), 0, [("", 1, norm_tiles + ["l3", "l4", "kr"]), ("h", 2, qnames), ("mid", 1, mid),
                                     ("m", 3, ["b0", "b1"]), ("m3", 1, ["b0", "b1"]),
                                     ("f0", 1, ups), ("f", 3, ups)])
    b2.free = Count(sem("proj_free2"), 1, [("", 1, ["kv0", "kv1", "kr"]), ("h", 2, qnames),
                                            ("mid", 1, pools), ("out", 1, outs),
                                            ("f", 3, downs), ("f3", 1, downs)])
    b2.aux = Count(sem("act_aux2"), 2, [("", 1, ["sp"]), ("h", 2, [c for c in pair_chunks if c[0] == "g"]),
                                         ("mid", 1, ["ra0", "rx0", "lt0", "la0", "sq0",
                                                     "ra1", "rx1", "lt1", "la1", "sq1", "rt0", "rt1"] + gates),
                                         ("m", 3, gates), ("f0", 1, ups), ("f", 3, ups)])
    ps = [f"{jj}{s}" for jj in range(2) for s in range(4)]
    b2.sc = Count(sem("scores2"), 0, [("h", 2, ps)])
    b2.red = Count(sem("rowmax2"), 1, [("h", 2, ps)])
    b2.ex = Count(sem("exp2"), 0, [("h", 2, ps)])
    b2.pn = Count(sem("probs2"), 0, [("h", 2, ps)])
    b2.tr = Count(sem("transposed2"), 0, [("h", 2, ps)])
    b2.pv = Count(sem("attended2"), 1, [("h", 2, ps)])
    b2.sm = Count(sem("small2"), 0, [("", 1, ["a0", "x0", "a1", "x1", "p0", "p1"])])
    b2.br = Count(sem("branches2"), 1, [("m", 3, ["0", "1"]), ("m3", 1, ["0", "1"])])
    b2.brf = Count(sem("merged2"), 2, [("m", 3, ["0", "1"]), ("m3", 1, ["0", "1"])])
    b2.lru = Count(sem("lru_ready2"), 0, [("", 1, ["sp", "c0", "c1"])])
    norms2 = ["n", "kv", "q", "e"]
    b2.acc = Count(sem("norm_acc2"), 0, [("", 1, norms2)])
    b2.ss = Count(sem("norm_sum2"), 0, [("", 1, norms2)])
    b2.rt = Count(sem("norm_root2"), 0, [("", 1, ["n", "kv", "q"])])
    b2.dg = Count(sem("norm_diag2"), 0, [("", 1, norms2)])
    b2.bc = Count(sem("norm_spread2"), 0, [("", 1, norms2)])
    b2.layer = Count(sem("layer2"), 1, [("", 1, ["end"])])

    bf = Block()
    bf.ss, bf.rt, bf.dg, bf.bc = (Count(sem(f"norm_{n}F"), 0, [("", 1, ["n"])])
                                  for n in ("sum", "root", "diag", "spread"))
    final = Count(sem("final"), 0, [("", 1, [str(k) for k in range(KT)])])

    m1 = ExitStack()
    with m1:
        def t1(name, shape, dt=F32):
            return sb(name, shape, dt, m1)
        ACC1 = t1("ACC1", [P, S])
        PT1 = two("PT1", [P, 4, 256], m1)
        AQ, AK, AV = two("AQ", [P, 2, S], m1), two("AK", [P, 2, S], m1), two("AV", [P, 4, 256], m1)
        BT = t1("BT", [P, 2, 14, GRID])
        ROPE = BT[:, :, :, :].rearrange("p a b c -> p (a b c)")
        COS1, SIN1 = ROPE[:, 0:S], ROPE[:, S:2 * S]
        NM = t1("NM", [P, GRID])
        ZB = t1("ZB", [P, 2, S])
        HA = t1("HA", [P, 2, S + 2 * PAD_A])
        CA = t1("CA", [P, 2, S])
        CB = t1("CB", [P, 2, S])
        CX = t1("CX", [P, 2, S + 2])
        MS = t1("MS", [P, 640])
        PAR1 = t1("PAR1", [P, NP1])
    m2 = ExitStack()
    with m2:
        def t2(name, shape, dt=F32, where=m2):
            return sb(name, shape, dt, where)
        CS2 = t2("CS2", [P, S])
        PAR2 = t2("PAR2", [P, NP2])
        HB = t2("HB", [P, 28])
        LS = t2("LS", [P, 16])
        IC = t2("IC", [P, 2, POOLPAD])
        m2g = ExitStack()
        with m2g:
            GT = t2("GT", [P, 16, S], F32, m2g)
        QS = GT[:, 15, :]
        MRG = two("MRG", [P, KT, S], m2)
        m2a = ExitStack()
        with m2a:
            PT2 = two("PT2", [P, 4, 256], m2a)
            LX = two("LX", [P, S], m2a)
            Q2, K2, V2 = (two("Q2", [P, S], m2a), two("K2", [P, 2, S], m2a), two("V2", [P, 4, P], m2a))
            MC = t2("MC", [P, 640], F32, m2a)
        m2b = ExitStack()
        with m2b:
            UP = t2("UP", [P, 2, S + POOLPAD], F32, m2b)
            L = t2("L", [P, 2, 5, S], F32, m2b)
            SUMS = t2("SUMS", [P, 2, S + POOLPAD], F32, m2b)
    RB = L[:, 0, 0, :]
    block = ctx.enter_context(nc.Block())
    ACC2 = PR[:, 0, :]
    ACCG = HA[:, 0, PAD_A:PAD_A + S]
    TH = TMP[:, 1, :]

    def lat(p, k):
        return LX[p][:, :] if k == 4 else Y[p][:, (0, 1, 6, 7)[k], :]

    def unit(b, l, k):
        return l * (U1 if b == 1 else U2) + (k if b == 1 else DEPTH * U1 + k)

    def unit_fill(b, l, k):
        per, first = (U1, 0) if b == 1 else (U2, DEPTH * U1)
        return l * (8 * per) + 16 * ((first + k) // 2 + 1)

    @block.sync
    def _(sp):
        with sp.Fori(0, UNITS // 2) as i:
            for s in range(2):
                sp.wait_ge(w_lo, 2 * i + s + 1)
                sp.dma_start(W_raw[:, s, :], dram["stream"][bass.ds(2 * i + s, 1)].rearrange(
                    "a p n -> p (a n)")).then_inc(w_raw[s], 16)
        sp.wait_ge(w_raw[0], 16 * (UNITS // 2))
        sp.sem_inc(w_raw[0], 16)
        for k in range(KT):
            sp.wait_ge(final.sem, final.at(0, str(k)))
            sp.dma_start(dram["out"][:, k, :], X[:, k, :]).then_inc(x_out, 16)
        sp.wait_ge(x_out, 16 * KT)

    @block.gpsimd
    def _(pool):
        nc.gpsimd.memset(ones[:], 1.0).then_inc(start, 1)
        n = 0
        for first, times in [(w_lo, 2)] + [(c.sem, c.start) for c in COUNTS if c.start]:
            for _ in range(times):
                if n:
                    pool.wait_ge(pool_step, n)
                nc.gpsimd.memset(spare[:], 0.0).then_inc(pool_step, 1)
                n += 1
                pool.wait_ge(pool_step, n)
                pool.sem_inc(first, 1)
        with pool.Fori(0, UNITS // 2) as i:
            for s in range(2):
                pool.wait_ge(w_hi, 2 * i + s + 1)
                nc.gpsimd.tensor_tensor(W[1][:, s, :], W_raw[:, s, :], W[0][:, s, :].bitcast(F32),
                                        ALU.subtract).then_inc(w_lo, 1)

    def w_tile(part, s, kt, lo, n):
        return W[part][:, s, kt * 256 + lo:kt * 256 + lo + n]

    def three(pe, out, pairs, skip=False, begun=False, more=False):
        n = len(pairs)
        for k, (lhs, rhs) in enumerate(pairs):
            for a, b in ((0, 0), (0, 1), (1, 0)):
                mm = pe.matmul(out, lhs[a], rhs[b], start=(not begun and k == 0 and a == 0 and b == 0),
                               stop=(not more and k == n - 1 and a == 1), skip_group_check=skip or begun or more)
        return mm

    def tiles(src):
        return lambda p, k: src[p][:, k, :]

    def chunk_pairs(s, c, src, kts=range(KT), at=0):
        return [([w_tile(p, s, at + k, c * P, P) for p in range(2)],
                 [src[p][:, kt, :] for p in range(2)]) for k, kt in enumerate(kts)]

    def token_major(pe, out, s, c, src, kts=range(KT), at=0):
        for t in range(4):
            mm = three(pe, out[:, t * P:(t + 1) * P],
                       [([src(p, kt)[:, t * P:(t + 1) * P] for p in range(2)],
                         [w_tile(p, s, at + k, c * P, P) for p in range(2)]) for k, kt in enumerate(kts)],
                       skip=True)
        return mm

    def by_tiles(pe, slot, src, ready):
        last = [None, None]
        for kt in range(KT):
            ready(kt)
            for c in range(2):
                for a, b in ((0, 0), (0, 1), (1, 0)):
                    last[c] = pe.matmul(G[c][:, :], w_tile(a, slot, kt, c * P, P), src[b][:, kt, :],
                                        start=(kt == 0 and a == 0 and b == 0),
                                        stop=(kt == KT - 1 and a == 1), skip_group_check=True)
        return last

    def pe_norm(pe, b, l, name, acc):
        pe_sums(pe, b, l, name, acc)
        pe_spread(pe, b, l, name)

    def pe_sums(pe, b, l, name, acc, ready=None):
        count, at = ready or (b.acc, l)
        pe.wait_ge(count.sem, count.at(at, name))
        for t in range(4):
            mm = pe.matmul(NB[:, t:t + 1], acc[:, t * P:(t + 1) * P], ones[:, 0:1], start=True, stop=True,
                           skip_group_check=True)
        mm.then_inc(b.ss.sem, 1)

    def pe_spread(pe, b, l, name, diagonal=TMP[:, 0, :], bank=NB):
        pe.wait_ge(b.dg.sem, b.dg.at(l, name))
        for t in range(4):
            mm = pe.matmul(bank[:, t * P:(t + 1) * P], ones[:, :], diagonal[:, t * P:(t + 1) * P],
                           start=True, stop=True, skip_group_check=True)
        mm.then_inc(b.bc.sem, 1)

    def pe_transposes(pe, n_blocks):
        for n in range(n_blocks):
            for q in range(2):
                mm = pe.transpose(TB[n // 2][:, (n % 2) * 256 + q * P:(n % 2) * 256 + (q + 1) * P],
                                  PR[:, q, n * P:(n + 1) * P], ident[:, :])
        return mm

    def b1_keys(i):
        return (0, 1, 2, 3) if i < STEPS else ((0, 1, 2), (1, 2, 3))[i % 2]

    @block.tensor
    def _(pe):
        pe.wait_ge(start, 1)
        pe.wait_ge(consts_in, 16 * N_CONST)

        def begin_unit(b, l, k):
            pe.wait_ge(w_lo, unit(b, l, k) + 3)

        with pe.Fori(0, DEPTH) as l:
            pe_norm(pe, b1, l, "n", ACC1)

            def free_bank(n):
                if n < 2:
                    pe.wait_ge(b1.free.sem, b1.free.at(l, "dz0") - 1)
                    return
                name = B1_CHUNKS[n - 2]
                if ("", name) in b1.free.at_:
                    pe.wait_ge(b1.free.sem, b1.free.at(l, name))
                else:
                    reader = b1.aux if ("", name) in b1.aux.at_ else b1.lo
                    pe.wait_ge(reader.sem, reader.at(l, "cv" if name == "ck1" else name))

            def chunk(name):
                n = B1_CHUNKS.index(name)
                k, c = divmod(n, 2)
                if c == 0:
                    begin_unit(1, l, k)
                free_bank(n)
                out = G[c]
                if name in ("dv0", "dv1", "ck1"):
                    mm = token_major(pe, out, k % 2, c, tiles(H))
                elif name in ("o00", "o01"):
                    pe.wait_ge(b1.lo.sem, b1.lo.at(l, "yaz1"))
                    pairs = chunk_pairs(k % 2, c, Y)
                    three(pe, out[:, :], pairs[:LAST_Y] + pairs[LAST_Y + 1:], more=True)
                    return
                elif name[0] == "o":
                    mm = three(pe, out[:, :], chunk_pairs(k % 2, c, Y))
                else:
                    mm = three(pe, out[:, :], chunk_pairs(k % 2, c, H))
                mm.then_inc(b1.done.sem, 1)

            def scores(i):
                if i in (0, STEPS):
                    pe.wait_ge(b1.lo.sem, b1.lo.at(l, "dk1" if i == 0 else "ck3"))
                if i >= 1:
                    pe.wait_ge(b1.red.sem, b1.red.at(l, str(i - 1)))
                h, half = (i % STEPS) // 2, i % 2
                kbs = b1_keys(i)
                lo, hi = kbs[0] * P, (kbs[-1] + 1) * P
                r = slice(HD * (h % 2), HD * (h % 2) + HD)
                for q in range(2):
                    qb = (2 * half + q) * P
                    mm = three(pe, SC[q][:, 0:hi - lo], [([AQ[p][r, h // 2, qb:qb + P] for p in range(2)],
                                                         [AK[p][r, h // 2, lo:hi] for p in range(2)])])
                mm.then_inc(b1.sc.sem, 1)

            def transposes(i):
                pe.wait_ge(b1.pn.sem, b1.pn.at(l, str(i)))
                if i >= 1:
                    pe.wait_ge(b1.lo.sem, b1.lo.at(l, f"pt{i - 1}b"))
                pe_transposes(pe, len(b1_keys(i))).then_inc(b1.tr.sem, 1)

            def attend(i):
                pe.wait_ge(b1.lo.sem, b1.lo.at(l, f"pt{i}b"))
                if i == 0:
                    pe.wait_ge(b1.lo.sem, b1.lo.at(l, "dv1"))
                if i == STEPS:
                    pe.wait_ge(b1.lo.sem, b1.lo.at(l, "cv"))
                if i >= 1:
                    pe.wait_ge(b1.pre.sem, b1.pre.at(l, f"y{i - 1}"))
                pair = (i // 4) % 2 if i < STEPS else 0
                three(pe, OB[:, 0:256], [([AV[p][:, kb, pair * P:(pair + 1) * P] for p in range(2)],
                                          [PT1[p][:, n, :] for p in range(2)])
                                         for n, kb in enumerate(b1_keys(i))]).then_inc(b1.pv.sem, 1)

            begin_unit(1, l, 0)
            free_bank(0)
            for mm in by_tiles(pe, 0, H, lambda kt: pe.wait_ge(b1.lo.sem, b1.lo.at(l, f"n{kt}"))):
                mm.then_inc(b1.done.sem, 1)
            for name in ("dk0", "dk1", "dv0", "dv1"):
                chunk(name)
            scores(0)
            chunk("dz0")
            chunk("dz1")
            for i in range(2 * STEPS):
                if i == STEPS:
                    for name in ("cq0", "cq1", "ck0", "ck1", "cz0"):
                        chunk(name)
                    scores(i)
                    chunk("cz1")
                if i % STEPS < STEPS - 1:
                    scores(i + 1)
                transposes(i)
                if i in FILL:
                    chunk(FILL[i])
                if i == LN_STEP + 3:
                    pe_spread(pe, b1, l, "var")
                if i == LN_STEP + 1:
                    pe.wait_ge(b1.acc.sem, b1.acc.at(l, "mean"))
                    for c in range(2):
                        mm = pe.matmul(NB[:, :], ones[:, :], CA[:, c, :], start=(c == 0), stop=(c == 1))
                    mm.then_inc(b1.ss.sem, 1)
                if i == LN_STEP + 2:
                    pe_sums(pe, b1, l, "var", ACC1)
                attend(i)
            pe.wait_ge(b1.lo.sem, b1.lo.at(l, f"y{2 * STEPS - 1}"))
            for c in range(2):
                three(pe, G[c][:, :], chunk_pairs(0, c, Y, (LAST_Y,), LAST_Y), begun=True).then_inc(b1.done.sem, 1)
            for k in range(1, 4):
                for c in range(2):
                    chunk(f"o{k}{c}")

        pe_sums(pe, bf, 0, "n", ACC1, (b1.acc, DEPTH))
        pe_spread(pe, bf, 0, "n", bank=OB)

        with pe.Fori(0, DEPTH) as l:
            pe_norm(pe, b2, l, "n", ACC2)
            begin_unit(2, l, 0)
            pe.wait_ge(b2.free.sem, b2.free.at(l, "kv0") - 1)
            for mm in by_tiles(pe, 0, H, lambda kt: pe.wait_ge(b2.lo.sem, b2.lo.at(l, f"n{kt}"))):
                mm.then_inc(b2.done.sem, 1)
            for n, name in enumerate(lats[2:]):
                k, c = 1 + n // 2, n % 2
                if c == 0:
                    begin_unit(2, l, k)
                if n < 2:
                    pe.wait_ge(b2.free.sem, b2.free.at(l, f"kv{n}"))
                else:
                    pe.wait_ge(b2.lo.sem, b2.lo.at(l, f"l{n - 2}"))
                three(pe, G[c][:, :], chunk_pairs(k % 2, c, H)).then_inc(b2.done.sem, 1)
                if name == "q00":
                    pe_sums(pe, b2, l, "kv", ACC2)
                if name == "q01":
                    pe_spread(pe, b2, l, "kv")
            pe_norm(pe, b2, l, "q", ACC2)

            with pe.Fori(0, 2) as j:
                pe.wait_ge(b2.lo.sem, b2.lo.at(l, "l2"))
                for jj in range(2):
                    uk = 3 + 3 * jj
                    ju = unit(2, l, uk) + 6 * j
                    slot = uk % 2

                    pe.wait_ge(w_lo, ju + 3)

                    def bank(count, name, back=0):
                        pe.wait_ge(count.sem, count.at(l, name, "h", j) - back)

                    def q_chunk(a):
                        lhs = [([w_tile(p, slot, kt, a * P, P) for p in range(2)],
                                [lat(p, kt) for p in range(2)]) for kt in range(3)]
                        return three(pe, G[a][:, :], lhs)

                    bank(b2.aux, f"g{jj}0", 2)
                    q_chunk(0).then_inc(b2.done.sem, 1)
                    bank(b2.aux, f"g{jj}0", 1)
                    bank(b2.free, f"q{jj}0", 1)
                    three(pe, G[1][:, :], [([w_tile(p, slot, 3 + kt, 0, P) for p in range(2)],
                                            [lat(p, 3 + kt) for p in range(2)]) for kt in range(2)]
                          ).then_inc(b2.done.sem, 1)
                    pe.wait_ge(b2.lo.sem, b2.lo.at(l, "kr"))
                    token_major(pe, NB, slot, 1, lat, (3, 4), 3).then_inc(b2.done.sem, 1)

                    def scores(s):
                        a, half = divmod(s, 2)
                        bank(b2.lo, f"q{jj}{a}")
                        if s == 0:
                            bank(b2.lo, f"k{jj}1")
                        bank(b2.red, f"{jj}{s}", 1)
                        for q in range(2):
                            qb = (2 * half + q) * P
                            w = (256, 512)[half]
                            mm = three(pe, SC[q][:, 0:w], [([Q2[p][0:96, qb:qb + P] for p in range(2)],
                                                           [K2[p][0:96, a, 0:w] for p in range(2)])])
                        mm.then_inc(b2.sc.sem, 1)

                    scores(0)
                    q_chunk(1).then_inc(b2.done.sem, 1)
                    for s in range(4):
                        a, half = divmod(s, 2)
                        if s < 3:
                            scores(s + 1)
                        bank(b2.pn, f"{jj}{s}")
                        if s:
                            bank(b2.lo, f"pt{jj}{s - 1}" + ("b" if (s - 1) % 2 else "a"))
                        pe_transposes(pe, 4 if half else 2).then_inc(b2.tr.sem, 1)
                        gk = uk + 1 + s // 2
                        if s % 2 == 0:
                            pe.wait_ge(w_lo, unit(2, l, gk) + 6 * j + 3)
                        if s == 0:
                            bank(b2.free, f"q{jj}0")
                        elif s == 1:
                            bank(b2.free, f"q{jj}1")
                        else:
                            bank(b2.aux, f"g{jj}{s - 2}")
                        three(pe, G[s % 2][:, :], chunk_pairs(gk % 2, s % 2, H)).then_inc(b2.done.sem, 1)
                        bank(b2.lo, f"pt{jj}{s}" + ("b" if half else "a"))
                        if s:
                            bank(b2.lo, f"y{jj}{s - 1}")
                        three(pe, OB[:, 0:256], [([V2[p][:, kb, :] for p in range(2)],
                                                  [PT2[p][:, kb, :] for p in range(2)])
                                                 for kb in range(4 if half else 2)]).then_inc(b2.pv.sem, 1)

            for n, name in enumerate(pools):
                k, c = 15 + n // 2, n % 2
                if c == 0:
                    begin_unit(2, l, k)
                if n < 2:
                    pe.wait_ge(b2.aux.sem, b2.aux.at(l, f"g1{2 + n}", "h", 1))
                else:
                    pe.wait_ge(b2.free.sem, b2.free.at(l, pools[n - 2], "mid"))
                three(pe, G[c][:, :], chunk_pairs(k % 2, c, H)).then_inc(b2.done.sem, 1)

            def small(name, src, operand, out):
                pe.wait_ge(b2.lo.sem, b2.lo.at(l, src, "mid"))
                col = {"p": 0, "a": 2, "x": 4}[name[0]] + int(name[1])
                three(pe, out[:, :], [([w_tile(p, 1, col, 0, P) for p in range(2)],
                                       [Y[p][:, operand, :] for p in range(2)])]).then_inc(b2.sm.sem, 1)

            def gate_chunks(slot, bank_read, chunks=range(2)):
                for c in chunks:
                    bank_read(c)
                    three(pe, G[c][:, :], chunk_pairs(slot, c, H)).then_inc(b2.done.sem, 1)

            begin_unit(2, l, 17)
            for c in range(2):
                small(f"a{c}", f"uc{c}", 6 + c, TB[c])
                small(f"x{c}", f"uc{c}", 6 + c, (OB, NB)[c])
            begin_unit(2, l, 18)

            def pool_read(c):
                pe.wait_ge(b2.free.sem, b2.free.at(l, f"pl{c}", "mid"))

            gate_chunks(0, pool_read, (0,))
            for c in range(2):
                small(f"p{c}", f"pm{c}", c, SC[c])
            gate_chunks(0, pool_read, (1,))

            def branches(seg, i):
                for c in range(2):
                    pe.wait_ge(b2.brf.sem, b2.brf.at(l, str(c), seg, i) - 2)
                    pe.wait_ge(b2.aux.sem, b2.aux.at(l, "rx1", "mid"))
                    pool_, mla, lru = ((SC[0], TB[0], SC[1]), (TB[1], OB, NB))[c]
                    three(pe, mla[:, :], chunk_pairs(1, c, Y, (2, 3, 4, 5), 2))
                    pe.wait_ge(b2.pre.sem, b2.pre.at(l, "py1", "mid"))
                    pe.wait_ge(b2.lo.sem, b2.lo.at(l, "py1", "mid"))
                    three(pe, lru[:, :], chunk_pairs(1, c, Y, (6, 7), 6))
                    three(pe, pool_[:, :], chunk_pairs(1, c, Y, (0, 1), 0)).then_inc(b2.br.sem, 1)

            with pe.Fori(0, 3) as m:
                pe.wait_ge(w_lo, unit(2, l, 19) + 2 * m + 3)
                branches("m", m)
                pe.wait_ge(w_lo, unit(2, l, 20) + 2 * m + 3)
                gate_chunks(0, lambda c: pe.wait_ge(b2.aux.sem, b2.aux.at(l, f"t{c}", "m", m) - 2))
            begin_unit(2, l, 25)
            branches("m3", 0)
            begin_unit(2, l, 26)
            pe.wait_ge(b2.lo.sem, b2.lo.at(l, "b1", "m", 2))
            for c in range(2):
                pe.wait_ge(b2.aux.sem, b2.aux.at(l, f"t{c}", "m", 2))
                three(pe, G[c][:, :], chunk_pairs(0, c, MRG)[:6], more=True)
            pe.wait_ge(b2.lo.sem, b2.lo.at(l, "b1", "m3"))
            for c in range(2):
                three(pe, G[c][:, :], chunk_pairs(0, c, MRG)[6:], begun=True).then_inc(b2.done.sem, 1)
            for n in range(2, KT):
                k, c = 26 + n // 2, n % 2
                if c == 0:
                    begin_unit(2, l, k)
                pe.wait_ge(b2.free.sem, b2.free.at(l, f"o{n - 2}", "out"))
                three(pe, G[c][:, :], chunk_pairs(k % 2, c, MRG)).then_inc(b2.done.sem, 1)

            def up(first, seg, i, bank_read):
                for n in range(KT):
                    if n % 2 == 0:
                        pe.wait_ge(w_lo, first + n // 2 + 3)
                    if n < 2:
                        bank_read(n)
                    else:
                        pe.wait_ge(b2.aux.sem, b2.aux.at(l, f"u{n - 2}", seg, i))
                    pairs = chunk_pairs(n // 2 % 2, n % 2, H)
                    if seg == "f0" and n == 0:
                        three(pe, G[0][:, :], pairs[:KT - 1], more=True)
                        pe.wait_ge(b2.lo.sem, b2.lo.at(l, f"e{KT - 1}", "n2"))
                        three(pe, G[0][:, :], pairs[KT - 1:], begun=True).then_inc(b2.done.sem, 1)
                    else:
                        three(pe, G[n % 2][:, :], pairs).then_inc(b2.done.sem, 1)
                    if seg == "f0" and n == 0:
                        pe_sums(pe, b2, l, "e", ACC2)

            def down(first, seg, i, last_up):
                for n in range(KT):
                    if n % 2 == 0:
                        pe.wait_ge(w_lo, first + n // 2 + 3)
                    if n < 2:
                        pe.wait_ge(b2.aux.sem, last_up(b2.aux, 6 + n))
                    else:
                        pe.wait_ge(b2.free.sem, b2.free.at(l, f"d{n - 2}", seg, i))
                    pairs = chunk_pairs(n // 2 % 2, n % 2, Y)
                    if n == 0:
                        pe.wait_ge(b2.lo.sem, last_up(b2.lo, KT - 2))
                        three(pe, G[0][:, :], pairs[:KT - 1], more=True)
                        pe.wait_ge(b2.lo.sem, last_up(b2.lo, KT - 1))
                        three(pe, G[0][:, :], pairs[KT - 1:], begun=True).then_inc(b2.done.sem, 1)
                    else:
                        three(pe, G[n % 2][:, :], pairs).then_inc(b2.done.sem, 1)

            pe.wait_ge(b2.lo.sem, b2.lo.at(l, f"e{KT - 2}", "n2"))
            up(unit(2, l, 30), "f0", 0, lambda n: pe.wait_ge(b2.free.sem, b2.free.at(l, f"o{6 + n}", "out")))
            pe_spread(pe, b2, l, "e", PR[:, 1, :])
            with pe.Fori(0, 3) as f:
                down(unit(2, l, 34) + 8 * f, "f", f, lambda count, n: count.at(l, "u0", "f", f) + (n - KT))
                up(unit(2, l, 38) + 8 * f, "f", f,
                   lambda n: pe.wait_ge(b2.free.sem, b2.free.at(l, f"d{6 + n}", "f", f)))
            down(unit(2, l, 58), "f3", 0, lambda count, n: count.at(l, f"u{n}", "f", 2))
        pe_sums(pe, bf, 1, "n", ACC2, (b2.acc, DEPTH))
        pe_spread(pe, bf, 1, "n", bank=OB)

    @block.scalar
    def _(act):
        own = Own(act_step)

        def load(dst, src, sem_):
            act.dma_start(dst, src).then_inc(sem_, 16)

        for k in range(4):
            load(X[:, 2 * k:2 * k + 2, :], dram["x"][:, 2 * k:2 * k + 2, :], x_in[k])
        for dst, src in ((ident[:, :], "ident"), (MS[:, :], "window"), (NM[:, :], "columns"),
                         (PARF[:, :], "finals")):
            load(dst, dram[src], consts_in)

        def prep(b, l, k, after, step=0, back=0):
            act.wait_ge(w_raw[k % 2], unit_fill(b, l, k) + 8 * step)
            if after:
                act.wait_ge(after[0].sem, after[0].at(*after[1:]) - back)
            act.wait_ge(*own.last(1))
            nc.scalar.activation(W[0][:, k % 2, :], W_raw[:, k % 2, :], ACT.Copy) \
                .then_inc(w_hi, own.reach(w_hi, unit(b, l, k) + 1 + step))

        def hi(b, l, name, out, in_, seg="", i=0, **more):
            act.wait_ge(*own.last(1))
            nc.scalar.activation(out, in_, ACT.Copy, **more).then_inc(b.hi.sem, own.event(b.hi, l, name, seg, i))

        def root(b, l, name, n):
            act.wait_ge(*own.last(0))
            nc.scalar.activation(spare_a[:, :], ones[:, 0:1], ACT.Sqrt).then_inc(act_step, own.step())
            act.wait_ge(b.ss.sem, b.ss.at(l, name))
            act.wait_ge(*own.last(1))
            nc.scalar.activation(NR[:, :], NB[:, 0:4], ACT.Sqrt, bias=EPSC[:, :], scale=1.0 / n) \
                .then_inc(b.rt.sem, own.event(b.rt, l, name))

        def exps(b, l, name, w, scale, sink=None, seg="", i=0):
            act.wait_ge(b.red.sem, b.red.at(l, name, seg, i))
            for q in range(2):
                if sink is not None:
                    act.wait_ge(*own.last(1))
                    nc.scalar.activation(SM[:, 8 + q:9 + q], PAR1[:, sink:sink + 1], ACT.Exp, bias=SM[:,
                                         2 + q:3 + q]) \
                        .then_inc(act_step, own.step())
                act.wait_ge(*own.last(1))
                ins = nc.scalar.activation(PR[:, q, 0:w], PR[:, q, 0:w], ACT.Exp, bias=SM[:, 2 + q:3 + q],
                                           scale=scale, accum_out=SM[:, 4 + q:5 + q])
                if q:
                    ins.then_inc(b.ex.sem, own.event(b.ex, l, name, seg, i))
                else:
                    ins.then_inc(act_step, own.step())

        act.wait_ge(start, 1)
        nc.scalar.activation(EPSC[:, :], ones[:, 0:1], ACT.Copy, scale=EPS).then_inc(act_step, own.step())
        prep(1, 0, 0, None)
        with act.Fori(0, DEPTH) as l:
            own.enter(l, ACT_STEPS_1)
            act.wait_ge(b1.layer.sem, b1.layer.at(l, "end") - 1)
            load(PAR1[:, :], dram["par1"][bass.ds(l, 1)].rearrange("a p n -> p (a n)"), par_in)

            def load_bias(h):
                load(BT[:, h % 2, :, :], dram["bias"][bass.ds(4 * l + h, 1)].rearrange(
                    "a p (j c) -> p (a j) c", j=14), bias_in[h % 2])

            load_bias(0)
            load_bias(1)
            root(b1, l, "n", D)

            def begin(name):
                n = B1_CHUNKS.index(name)
                if n % 2:
                    return
                k = n // 2 + 1
                if k == 1:
                    prep(1, l, 1, (b1.done, l, "dq0"), back=1)
                else:
                    prep(1, l, k, (b1.done, l, B1_CHUNKS[2 * k - 3]))

            def chunk(name, begun=False):
                if not begun:
                    begin(name)
                n = B1_CHUNKS.index(name)
                kind, c, bank_ = name[:2], n % 2, G[n % 2]
                if kind[0] == "o":
                    return
                act.wait_ge(b1.done.sem, b1.done.at(l, name))
                if kind in ("dq", "dk"):
                    hi(b1, l, name, (AQ if kind == "dq" else AK)[0][:, c, :], bank_[:, :])
                elif kind == "dv":
                    hi(b1, l, name, AV[0][:, :, c * P:(c + 1) * P],
                       bank_[:, :].rearrange("p (t n) -> p t n", t=4))
                elif kind in ("dz", "cz", "bz", "az"):
                    act.wait_ge(*own.last(1))
                    nc.scalar.activation(TH, bank_[:, :], ACT.Tanh, scale=0.5) \
                        .then_inc(b1.aux.sem, own.event(b1.aux, l, name))
                elif kind == "av":
                    act.wait_ge(*own.last(1))
                    nc.scalar.activation(CA[:, c, :], bank_[:, :], ACT.Tanh, scale=0.5) \
                        .then_inc(b1.aux.sem, own.event(b1.aux, l, name))
                elif kind == "bc":
                    act.wait_ge(*own.last(1))
                    nc.scalar.activation(CB[:, c, :], bank_[:, :], ACT.Copy) \
                        .then_inc(b1.aux.sem, own.event(b1.aux, l, name))
                elif kind == "cq":
                    act.wait_ge(b1.pre.sem, b1.pre.at(l, name))
                    hi(b1, l, name, AQ[0][:, c, :], PRE[:, c, :])
                elif name == "ck0":
                    act.wait_ge(b1.pre.sem, b1.pre.at(l, name))
                    for g in range(2):
                        for half in range(2):
                            hi(b1, l, f"ck{2 * g + half}", AK[0][half * HD:(half + 1) * HD, g, :],
                               PRE[g * HD:(g + 1) * HD, 0, :])
                elif name == "ck1":
                    hi(b1, l, "cv", AV[0][:, :, 0:P], bank_[:, :].rearrange("p (t n) -> p t n", t=4))
                if kind in ("bz", "az"):
                    i = [k for k, v in FILL.items() if v == name][0]
                    act.wait_ge(b1.pre.sem, b1.pre.at(l, "y" + name))
                    hi(b1, l, "y" + name, Y[0][:, (2 if kind == "bz" else 0) + c, :], PRE[:, (i + 1) % 2, :])
                if kind in ("dz", "cz"):
                    act.wait_ge(b1.free.sem, b1.free.at(l, name))

            begin("dq0")
            for k in range(KT):
                act.wait_ge(b1.pre.sem, b1.pre.at(l, f"n{k}"))
                hi(b1, l, f"n{k}", H[0][:, k, :], PRE[:, k % 2, :])
            for name in ("dq0", "dq1", "dk0", "dk1", "dv0", "dv1"):
                chunk(name, begun=name == "dq0")

            def softmax(i):
                w = P * len(b1_keys(i))
                exps(b1, l, str(i), w, 1.0, None if i < STEPS else P1["sink"] + (i - STEPS) // 2)
                if i == 1:
                    load_bias(2)
                if i == 3:
                    load_bias(3)
                if i == STEPS - 1:
                    load(ROPE[:, 0:2 * S], dram["rope1"], rope_in)

            softmax(0)
            chunk("dz0")
            chunk("dz1")
            for i in range(2 * STEPS):
                if i == STEPS:
                    for name in ("cq0", "cq1", "ck0", "ck1", "cz0"):
                        chunk(name)
                    softmax(i)
                    chunk("cz1")
                act.wait_ge(b1.tr.sem, b1.tr.at(l, str(i)))
                act.wait_ge(b1.pv.sem, b1.pv.at(l, str(i)) - 1)
                n = len(b1_keys(i))
                hi(b1, l, f"pt{i}a", PT1[0][:, 0:2, :], TB[0][:, :].rearrange("p (a n) -> p a n", a=2))
                hi(b1, l, f"pt{i}b", PT1[0][:, 2:n, :],
                   TB[1][:, 0:256 * (n - 2)].rearrange("p (a n) -> p a n", a=n - 2))
                if i % STEPS < STEPS - 1:
                    softmax(i + 1)
                if i == LN_STEP + 3:
                    begin(FILL[i])
                if i == LN_STEP + 4:
                    chunk(FILL[i - 1], begun=True)
                if i in FILL and i != LN_STEP + 3:
                    chunk(FILL[i])
                if i == LN_STEP + 2:
                    root(b1, l, "var", 2 * P)
                h, half = (i % STEPS) // 2, i % 2
                r = slice(HD * (h % 2), HD * (h % 2) + HD)
                act.wait_ge(b1.pre.sem, b1.pre.at(l, f"y{i}"))
                hi(b1, l, f"y{i}", Y[0][r, (6 if i < STEPS else 4) + h // 2, half * 256:(half + 1) * 256],
                   PRE[r, i % 2, 0:256])
                if i == LN_STEP + 3:
                    for c in range(2):
                        act.wait_ge(ln_in, 2 * l + (c + 1))
                        act.wait_ge(*own.last(1))
                        nc.scalar.activation(TMP[:, c, :], CA[:, c, :], ACT.Tanh, scale=0.5) \
                            .then_inc(b1.aux.sem, own.event(b1.aux, l, f"ln{c}"))
                    act.wait_ge(ln_out, l + 1)
            for k in range(1, 4):
                begin(f"o{k}0")
            act.wait_ge(*own.last(1))
            nc.scalar.activation(spare_a[:, :], ones[:, 0:1], ACT.Copy).then_inc(act_step, own.step())
        own.leave(DEPTH)

        root(bf, 0, "n", D)
        act.wait_ge(start, 1)
        load(CS2[:, :], dram["rope2"], par_in)
        load(IC[:, :, :], dram["counts"], par_in)
        with act.Fori(0, DEPTH) as l:
            own.enter(l, ACT_STEPS_2)
            act.wait_ge(b2.layer.sem, b2.layer.at(l, "end") - 1)
            load(PAR2[:, :], dram["par2"][bass.ds(l, 1)].rearrange("a p n -> p (a n)"), par_in)
            load(MC[:, :], dram["causal"], par_in)
            root(b2, l, "n", D)
            prep(2, l, 1, (b2.done, l, "kv0"), back=1)
            for k in range(KT):
                act.wait_ge(b2.pre.sem, b2.pre.at(l, f"n{k}"))
                hi(b2, l, f"n{k}", H[0][:, k, :], PRE[:, k % 2, :])
            prep(2, l, 2, (b2.done, l, "kv1"))
            act.wait_ge(b2.lru.sem, b2.lru.at(l, "sp"))
            act.wait_ge(*own.last(1))
            nc.scalar.activation(LS[:, 2:4], LS[:, 0:2], ACT.Exp, scale=-1.0) \
                .then_inc(b2.aux.sem, own.event(b2.aux, l, "sp"))

            def q_latent(k):
                act.wait_ge(b2.done.sem, b2.done.at(l, ("q00", "q01", "q2")[k]))
                col = P2["g_lat"] + k
                hi(b2, l, f"l{k}", lat(0, k), G[k % 2][:, :], scale=PAR2[:, col:col + 1])

            q_latent(0)
            root(b2, l, "kv", 2 * P)
            for k in (3, 4):
                act.wait_ge(b2.pre.sem, b2.pre.at(l, f"l{k}"))
                hi(b2, l, f"l{k}", lat(0, k), PRE[:, k % 2, :])
            q_latent(1)
            prep(2, l, 3, (b2.done, l, "q01"))
            q_latent(2)
            root(b2, l, "q", 3 * P)
            act.wait_ge(b2.pre.sem, b2.pre.at(l, "kr"))
            act.wait_ge(*own.last(1))
            nc.scalar.activation(K2[0][64:96, 0, :], PRE[64:96, 1, :], ACT.Copy).then_inc(act_step, own.step())
            hi(b2, l, "kr", K2[0][64:96, 1, :], PRE[64:96, 1, :])
            act.wait_ge(*own.last(1))
            nc.scalar.activation(spare_a[:, :], ones[:, 0:1], ACT.Copy).then_inc(act_step, own.step())
            with act.Fori(0, 2) as j:
                own.enter(j, ACT_STEPS_H)
                for jj in range(2):
                    uk = 3 + 3 * jj
                    if jj == 0:
                        prep(2, l, uk + 1, (b2.done, l, "q00", "h", j), step=6 * j, back=1)
                    else:
                        prep(2, l, uk + 1, (b2.done, l, "g03", "h", j), step=6 * j)

                    def softmax(s):
                        exps(b2, l, f"{jj}{s}", (256, 512)[s % 2], 96.0 ** -0.5, None, "h", j)

                    def q_part(a):
                        act.wait_ge(b2.pre.sem, b2.pre.at(l, f"q{jj}{a}", "h", j))
                        hi(b2, l, f"q{jj}{a}", Q2[0][0:96, :], PRE[0:96, a, :], "h", j)

                    q_part(0)
                    act.wait_ge(b2.done.sem, b2.done.at(l, f"k{jj}0", "h", j))
                    for a in range(2):
                        hi(b2, l, f"k{jj}{a}", K2[0][0:64, a, :], G[1][a * 64:(a + 1) * 64, :], "h", j)
                    act.wait_ge(b2.done.sem, b2.done.at(l, f"v{jj}0", "h", j))
                    hi(b2, l, f"v{jj}", V2[0][:, :, :], NB[:, :].rearrange("p (t n) -> p t n", t=4), "h", j)
                    softmax(0)
                    for s in range(4):
                        act.wait_ge(b2.tr.sem, b2.tr.at(l, f"{jj}{s}", "h", j))
                        act.wait_ge(b2.pv.sem, b2.pv.at(l, f"{jj}{s}", "h", j) - 1)
                        for n in range(1 + s % 2):
                            hi(b2, l, f"pt{jj}{s}" + "ab"[n], PT2[0][:, 2 * n:2 * n + 2, :],
                               TB[n][:, :].rearrange("p (a n) -> p a n", a=2), "h", j)
                        if s == 0:
                            q_part(1)
                            softmax(1)
                            prep(2, l, uk + 2, (b2.done, l, f"q{jj}1", "h", j), step=6 * j)
                        elif s < 3:
                            softmax(s + 1)
                        if s == 2:
                            prep(2, l, uk + 3, (b2.done, l, f"g{jj}1", "h", j), step=6 * j)
                        act.wait_ge(b2.done.sem, b2.done.at(l, f"g{jj}{s}", "h", j))
                        g, c = divmod(s, 2)
                        col = g * 8 + 2 * jj + c
                        act.wait_ge(*own.last(1))
                        nc.scalar.activation(GT[:, bass.ds(4 * j + col, 1), :].rearrange("p a n -> p (a n)"),
                                             G[c][:, :], ACT.Tanh, bias=HB[:, bass.ds(4 * j + (4 + col), 1)],
                                             scale=0.5) \
                            .then_inc(b2.aux.sem, own.event(b2.aux, l, f"g{jj}{s}", "h", j))
                        act.wait_ge(b2.pv.sem, b2.pv.at(l, f"{jj}{s}", "h", j))
                        a, half = divmod(s, 2)
                        r = slice(a * HD, (a + 1) * HD)
                        hi(b2, l, f"y{jj}{s}",
                           Y[0][r, bass.ds(2 * j + (2 + jj), 1), half * 256:(half + 1) * 256].rearrange(
                               "p a n -> p (a n)"), OB[r, 0:256], "h", j)
                act.wait_ge(*own.last(1))
                nc.scalar.activation(spare_a[:, :], ones[:, 0:1], ACT.Copy).then_inc(act_step, own.step())
            own.leave(2)
            prep(2, l, 16, (b2.done, l, "g13", "h", 1))
            for n in range(2):
                act.wait_ge(b2.pre.sem, b2.pre.at(l, f"uc{n}", "mid"))
                hi(b2, l, f"uc{n}", Y[0][:, 6 + n, :], L[:, n, 0, :], "mid")
                if n == 0:
                    prep(2, l, 17, (b2.done, l, "lr1", "mid"))
            prep(2, l, 18, (b2.done, l, "pl1", "mid"))
            for c in range(2):
                act.wait_ge(b2.sm.sem, b2.sm.at(l, f"a{c}"))
                act.wait_ge(*own.last(1))
                nc.scalar.activation(L[:, c, 1, :], TB[c][:, :], ACT.Tanh, bias=HB[:, c:c + 1], scale=0.5) \
                    .then_inc(b2.aux.sem, own.event(b2.aux, l, f"ra{c}", "mid"))
                act.wait_ge(b2.sm.sem, b2.sm.at(l, f"x{c}"))
                act.wait_ge(*own.last(1))
                nc.scalar.activation(L[:, c, 2, :], (OB, NB)[c][:, :], ACT.Tanh, bias=HB[:, 2 + c:3 + c], scale=0.5) \
                    .then_inc(b2.aux.sem, own.event(b2.aux, l, f"rx{c}", "mid"))
                if c == 0:
                    act.wait_ge(ls_ready, l + 1)
                act.wait_ge(*own.last(1))
                nc.scalar.activation(L[:, c, 3, :], L[:, c, 1, :], ACT.Tanh, bias=LS[:, 12 + c:13 + c],
                                     scale=LS[:, 12 + c:13 + c]) \
                    .then_inc(b2.aux.sem, own.event(b2.aux, l, f"lt{c}", "mid"))
                act.wait_ge(*own.last(1))
                nc.scalar.activation(L[:, c, 4, :], L[:, c, 1, :], ACT.Exp, bias=LS[:, 14 + c:15 + c],
                                     scale=LS[:, 14 + c:15 + c]) \
                    .then_inc(b2.aux.sem, own.event(b2.aux, l, f"la{c}", "mid"))
                act.wait_ge(*own.last(0))
                nc.scalar.activation(L[:, c, 1, :], L[:, c, 4, :], ACT.Square) \
                    .then_inc(b2.aux.sem, own.event(b2.aux, l, f"sq{c}", "mid"))
            for n in range(2):
                act.wait_ge(b2.pre.sem, b2.pre.at(l, f"pm{n}", "mid"))
                hi(b2, l, f"pm{n}", Y[0][:, n, :], PRE[:, n, :], "mid")
            for c in range(2):
                act.wait_ge(b2.lru.sem, b2.lru.at(l, f"c{c}"))
                act.wait_ge(*own.last(1))
                nc.scalar.activation(L[:, c, 1, :], L[:, c, 3, :], ACT.Sqrt) \
                    .then_inc(b2.aux.sem, own.event(b2.aux, l, f"rt{c}", "mid"))

            def gate_tanh(turn, seg, i, first, chunks=range(2)):
                for c in chunks:
                    act.wait_ge(b2.done.sem, b2.done.at(l, f"t{c}", seg, i))
                    act.wait_ge(*own.last(1))
                    nc.scalar.activation(PR[:, c, :], G[c][:, :], ACT.Tanh, scale=0.5,
                                         bias=HB[:, bass.ds(turn + (first + c), 1)]) \
                        .then_inc(b2.aux.sem, own.event(b2.aux, l, f"t{c}", seg, i))

            gate_tanh(0, "mid", 0, 20, (0,))
            prep(2, l, 19, (b2.sm, l, "p1"))
            for name, tile in (("lh0", 6), ("lh1", 7), ("py0", 0), ("py1", 1)):
                act.wait_ge(b2.pre.sem, b2.pre.at(l, name, "mid"))
                hi(b2, l, name, Y[0][:, tile, :], PRE[:, tile % 2, :], "mid")
            gate_tanh(0, "mid", 0, 20, (1,))
            act.wait_ge(*own.last(1))
            nc.scalar.activation(spare_a[:, :], ones[:, 0:1], ACT.Copy).then_inc(act_step, own.step())

            def merged(seg, i, tile):
                for c in range(2):
                    act.wait_ge(b2.pre.sem, b2.pre.at(l, f"b{c}", seg, i))
                    hi(b2, l, f"b{c}", MRG[0][:, bass.ds(tile + c, 1), :].rearrange("p a n -> p (a n)"),
                       PRE[:, c, :], seg, i, scale=0.5)

            with act.Fori(0, 3) as m:
                own.enter(m, ACT_STEPS_M)
                prep(2, l, 20, (b2.done, l, "t0", "m", m), step=2 * m, back=1)
                prep(2, l, 21, (b2.br, l, "1", "m", m), step=2 * m)
                merged("m", m, 2 * m)
                gate_tanh(2 * m, "m", m, 22)
                act.wait_ge(*own.last(1))
                nc.scalar.activation(spare_a[:, :], ones[:, 0:1], ACT.Copy).then_inc(act_step, own.step())
            own.leave(3)
            prep(2, l, 26, (b2.done, l, "t1", "m", 2))
            prep(2, l, 27, (b2.br, l, "1", "m3"))
            merged("m3", 0, 6)
            for k in range(KT):
                act.wait_ge(b2.free.sem, b2.free.at(l, f"o{k}", "out"))
                col = P2["g_ffn"] + k
                hi(b2, l, f"e{k}", H[0][:, k, :], X[:, k, :], "n2", scale=PAR2[:, col:col + 1])
                if k % 2 and k < KT - 1:
                    prep(2, l, 28 + k // 2, (b2.done, l, f"o{k}", "out"))
            act.wait_ge(*own.last(1))
            nc.scalar.activation(spare_a[:, :], ones[:, 0:1], ACT.Copy).then_inc(act_step, own.step())

            def up(k, step, seg, i, before):
                for n in range(KT):
                    if n == 0:
                        prep(2, l, k, before, step=step)
                    elif n % 2 == 0:
                        prep(2, l, k + n // 2, (b2.done, l, f"u{n - 1}", seg, i), step=step)
                    act.wait_ge(b2.done.sem, b2.done.at(l, f"u{n}", seg, i))
                    act.wait_ge(*own.last(1))
                    nc.scalar.activation(TMP[:, n % 2, :], G[n % 2][:, :], ACT.Relu) \
                        .then_inc(b2.aux.sem, own.event(b2.aux, l, f"u{n}", seg, i))
                    act.wait_ge(b2.pre.sem, b2.pre.at(l, f"u{n}", seg, i))
                    hi(b2, l, f"u{n}", Y[0][:, n, :], PRE[:, n % 2, :], seg, i)
                prep(2, l, k + 4, (b2.done, l, "u7", seg, i), step=step)

            def down(k, step, seg, i):
                for n in range(3):
                    prep(2, l, k + n, (b2.done, l, f"d{2 * n + 1}", seg, i), step=step)

            up(31, 0, "f0", 0, (b2.done, l, "o7", "out"))
            act.wait_ge(*own.last(1))
            nc.scalar.activation(spare_a[:, :], ones[:, 0:1], ACT.Copy).then_inc(act_step, own.step())
            with act.Fori(0, 3) as f:
                own.enter(f, ACT_STEPS_F)
                down(36, 8 * f, "f", f)
                up(39, 8 * f, "f", f, (b2.done, l, "d7", "f", f))
                act.wait_ge(*own.last(1))
                nc.scalar.activation(spare_a[:, :], ones[:, 0:1], ACT.Copy).then_inc(act_step, own.step())
            own.leave(3)
            down(60, 0, "f3", 0)
            act.wait_ge(*own.last(1))
            nc.scalar.activation(spare_a[:, :], ones[:, 0:1], ACT.Copy).then_inc(act_step, own.step())
        own.leave(DEPTH)
        root(bf, 1, "n", D)

    @block.vector
    def _(dve):
        own = Own(dve_step)

        def lo(b, l, name, out, in_, hi_, seg="", i=0, half=False, behind=1):
            dve.wait_ge(b.hi.sem, b.hi.at(l, name, seg, i))
            dve.wait_ge(*own.last(behind))
            if half:
                ins = nc.vector.scalar_tensor_tensor(out, in_, 0.5, hi_.bitcast(F32), ALU.mult, ALU.subtract)
            else:
                ins = nc.vector.tensor_tensor(out, in_, hi_.bitcast(F32), ALU.subtract)
            ins.then_inc(b.lo.sem, own.event(b.lo, l, name, seg, i))

        def mark(count, l, name, seg="", i=0):
            dve.wait_ge(*own.last(0))
            nc.vector.memset(spare_v[:, :], 0.0).then_inc(count.sem, own.event(count, l, name, seg, i))

        def diagonals(b, l, name, spread=True):
            dve.wait_ge(b.rt.sem, b.rt.at(l, name))
            dve.wait_ge(*own.last(1))
            nc.vector.reciprocal(NR[:, :], NR[:, :]).then_inc(dve_step, own.step())
            for t in range(4):
                dve.wait_ge(*own.last(1 if t else 0))
                ins = nc.vector.tensor_scalar(TMP[:, 0, t * P:(t + 1) * P], ident[:, :], NR[:, t:t + 1], None, ALU.mult)
                if t == 3:
                    ins.then_inc(b.dg.sem, own.event(b.dg, l, name))
                else:
                    ins.then_inc(dve_step, own.step())
            if spread:
                dve.wait_ge(b.bc.sem, b.bc.at(l, name))

        def spread_scale(b, l, name):
            dve.wait_ge(b.ss.sem, b.ss.at(l, name))
            dve.wait_ge(*own.last(1))
            nc.vector.tensor_scalar(NR[:, :], NB[:, 0:4], 1.0 / D, EPS, ALU.mult, ALU.add).then_inc(dve_step, own.step())
            dve.wait_ge(*own.last(0))
            nc.vector.reciprocal(NR[:, :], NR[:, :]).then_inc(dve_step, own.step())
            for t in range(4):
                dve.wait_ge(*own.last(1 if t else 0))
                ins = nc.vector.tensor_scalar(PR[:, 1, t * P:(t + 1) * P], ident[:, :], NR[:, t:t + 1], None, ALU.mult)
                if t == 3:
                    ins.then_inc(b.dg.sem, own.event(b.dg, l, name))
                else:
                    ins.then_inc(dve_step, own.step())

        def norm_to_h(b, l, name, first, gains, seg=""):
            diagonals(b, l, name)

            def rest(k):
                lo(b, l, f"{first}{k}", H[1][:, k, :], PRE[:, k % 2, :], H[0][:, k, :], seg)

            for k in range(KT):
                dve.wait_ge(*own.last(0))
                nc.vector.scalar_tensor_tensor(PRE[:, k % 2, :], X[:, k, :], gains[:, k:k + 1], NB[:, :],
                                               ALU.mult, ALU.mult) \
                    .then_inc(b.pre.sem, own.event(b.pre, l, f"{first}{k}", seg))
                if k:
                    rest(k - 1)
            rest(KT - 1)

        def squares(acc, src, first, ready=None):
            dve.wait_ge(*own.last(0))
            nc.vector.tensor_tensor(acc if first else PRE[:, 1, :], src, src, ALU.mult).then_inc(dve_step, own.step())
            if not first:
                dve.wait_ge(*own.last(0))
                ins = nc.vector.tensor_tensor(acc, acc, PRE[:, 1, :], ALU.add)
                if ready:
                    ins.then_inc(ready[0].sem, own.event(ready[0], ready[1], "n"))
                else:
                    ins.then_inc(dve_step, own.step())

        def row_max(b, l, name, w, masks, scale, exp_scale, seg="", i=0, sink=None):
            dve.wait_ge(b.sc.sem, b.sc.at(l, name, seg, i))
            dve.wait_ge(*own.last(0))
            nc.vector.memset(spare_v[:, :], 0.0).then_inc(dve_step, own.step())
            for q in range(2):
                nc.vector.tensor_tensor_reduce(PR[:, q, 0:w], SC[q][:, 0:w], masks[q], scale, -3e38, ALU.add,
                                               ALU.max, SM[:, q:q + 1]) \
                    .then_inc(dve_step, own.step())
            if sink is not None:
                dve.wait_ge(*own.last(0))
                nc.vector.tensor_scalar(SM[:, 0:2], SM[:, 0:2], PAR1[:, sink:sink + 1], None, ALU.max) \
                    .then_inc(dve_step, own.step())
            dve.wait_ge(*own.last(0))
            nc.vector.tensor_scalar(SM[:, 2:4], SM[:, 0:2], -exp_scale, None, ALU.mult) \
                .then_inc(b.red.sem, own.event(b.red, l, name, seg, i))

        def normalise(b, l, name, w, sink, seg="", i=0):
            dve.wait_ge(b.ex.sem, b.ex.at(l, name, seg, i))
            if sink is not None:
                dve.wait_ge(*own.last(1))
                nc.vector.tensor_tensor(SM[:, 4:6], SM[:, 4:6], SM[:, 8:10], ALU.add).then_inc(dve_step, own.step())
            dve.wait_ge(*own.last(0))
            nc.vector.reciprocal(SM[:, 6:8], SM[:, 4:6]).then_inc(dve_step, own.step())
            for q in range(2):
                dve.wait_ge(*own.last(q))
                ins = nc.vector.tensor_scalar(PR[:, q, 0:w], PR[:, q, 0:w], SM[:, 6 + q:7 + q], None, ALU.mult)
                if q:
                    ins.then_inc(b.pn.sem, own.event(b.pn, l, name, seg, i))
                else:
                    ins.then_inc(dve_step, own.step())

        for tile in (HA, CX):
            nc.vector.memset(tile[:, :, :], 0.0).then_inc(dve_step, own.step())
        dve.wait_ge(start, 1)
        for k in range(KT):
            if k % 2 == 0:
                dve.wait_ge(x_in[k // 2], 16)
            squares(ACC1[:, :], X[:, k, :], k == 0, (b1.acc, 0) if k == KT - 1 else None)
        dve.wait_ge(consts_in, 16 * N_CONST)

        with dve.Fori(0, DEPTH) as l:
            own.enter(l, DVE_STEPS_1)
            dve.wait_ge(par_in, 16 * l + 16)
            dve.wait_ge(*own.last(1))
            nc.vector.tensor_scalar(PAR1[:, P1["conv_a_w"]:P1["conv_a_w"] + 2 * CONV_A], PAR1[:,
                                    P1["conv_a_w"]:P1["conv_a_w"] + 2 * CONV_A], 0.5, None, ALU.mult) \
                .then_inc(dve_step, own.step())
            norm_to_h(b1, l, "n", "n", PAR1[:, P1["norm_g"]:P1["norm_g"] + KT])

            def par(name, k=0):
                return PAR1[:, P1[name] + k:P1[name] + k + 1]

            taps = iter([(j, c) for j in range(CONV_A) for c in range(2)])

            def conv_a(n):
                for _ in range(n):
                    j, c = next(taps)
                    src, w = HA[:, c, j:j + S], par("conv_a_w", c * CONV_A + j)
                    if j == 0:
                        dve.wait_ge(*own.last(1))
                        nc.vector.tensor_scalar(CA[:, c, :], src, w, par("conv_a_b", c), ALU.mult, ALU.add) \
                            .then_inc(dve_step, own.step())
                    else:
                        dve.wait_ge(*own.last(1))
                        nc.vector.scalar_tensor_tensor(CA[:, c, :], src, w, CA[:, c, :], ALU.mult, ALU.add) \
                            .then_inc(dve_step, own.step())

            def softmax_max(i):
                if i < STEPS:
                    h, half = i // 2, i % 2
                    if half == 0:
                        dve.wait_ge(bias_in[h % 2], 32 * l + 16 * (h // 2 + 1))
                        dve.wait_ge(*own.last(1))
                        nc.vector.scalar_tensor_tensor(BT[:, h % 2, :, :], BT[:, h % 2, :, :], 8.0, NM[:,
                                                       :].unsqueeze(1).broadcast_to([P, 14, GRID]), ALU.mult,
                                                       ALU.add) \
                            .then_inc(dve_step, own.step())
                    flat = BT[:, h % 2, :, :].rearrange("p a b -> p (a b)")
                    masks = [flat[:, (6 - 2 * qb) * GRID:(14 - 2 * qb) * GRID] for qb in (2 * half, 2 * half + 1)]
                    row_max(b1, l, str(i), S, masks, 0.125, 1.0)
                else:
                    half, lo_ = i % 2, b1_keys(i)[0] * P
                    masks = [MS[:, lo_ - P * qb + 256:lo_ - P * qb + 640] for qb in (2 * half, 2 * half + 1)]
                    row_max(b1, l, str(i), 3 * P, masks, 0.125, 1.0, sink=P1["sink"] + (i - STEPS) // 2)

            def softmax_rest(i):
                normalise(b1, l, str(i), P * len(b1_keys(i)), True if i >= STEPS else None)

            def rope(name, c):
                bank_ = G[c]
                dve.wait_ge(*own.last(1))
                nc.vector.tensor_tensor(TMP[:, 0, :], bank_[:, :], COS1, ALU.mult).then_inc(dve_step, own.step())
                for q in range(4):
                    to, of = slice((q ^ 1) * 32, (q ^ 1) * 32 + 32), slice(q * 32, q * 32 + 32)
                    dve.wait_ge(*own.last(1))
                    ins = nc.vector.tensor_tensor(TMP[to, 1, :], bank_[of, :], SIN1[of, :], ALU.mult)
                    if q == 3:
                        ins.then_inc(b1.free.sem, own.event(b1.free, l, name))
                    else:
                        ins.then_inc(dve_step, own.step())
                dve.wait_ge(*own.last(0))
                nc.vector.tensor_tensor(PRE[:, c, :], TMP[:, 0, :], TMP[:, 1, :], ALU.add) \
                    .then_inc(b1.pre.sem, own.event(b1.pre, l, name))

            def chunk(name):
                kind, c, bank_ = name[:2], B1_CHUNKS.index(name) % 2, G[B1_CHUNKS.index(name) % 2]
                if kind in ("av", "bc", "o0"):
                    return
                dve.wait_ge(b1.done.sem, b1.done.at(l, name))
                if kind in ("dq", "dk"):
                    t = AQ if kind == "dq" else AK
                    lo(b1, l, name, t[1][:, c, :], bank_[:, :], t[0][:, c, :])
                elif kind == "dv":
                    lo(b1, l, name, AV[1][:, :, c * P:(c + 1) * P],
                              bank_[:, :].rearrange("p (t n) -> p t n", t=4), AV[0][:, :, c * P:(c + 1) * P])
                elif kind in ("dz", "cz"):
                    dve.wait_ge(b1.aux.sem, b1.aux.at(l, name))
                    dve.wait_ge(*own.last(1))
                    nc.vector.scalar_tensor_tensor(ZB[:, c, :], TH, 1.0, bank_[:, :], ALU.add, ALU.mult) \
                        .then_inc(b1.free.sem, own.event(b1.free, l, name))
                elif kind == "au":
                    dve.wait_ge(b1.aux.sem, b1.aux.at(l, f"av{c}"))
                    dve.wait_ge(*own.last(1))
                    nc.vector.scalar_tensor_tensor(HA[:, c, PAD_A:PAD_A + S], CA[:, c, :], 1.0, bank_[:, :],
                                                   ALU.add, ALU.mult) \
                        .then_inc(b1.free.sem, own.event(b1.free, l, name))
                elif kind == "bx":
                    dve.wait_ge(b1.aux.sem, b1.aux.at(l, f"bc{c}"))
                    dve.wait_ge(*own.last(1))
                    nc.vector.tensor_tensor(CX[:, c, 1:1 + S], CB[:, c, :], bank_[:, :], ALU.mult) \
                        .then_inc(b1.free.sem, own.event(b1.free, l, name))
                    for j in range(3):
                        src, w = CX[:, c, j:j + S], par("conv_b_w", c * 3 + j)
                        if j == 0:
                            dve.wait_ge(*own.last(0))
                            nc.vector.tensor_scalar(CB[:, c, :], src, w, None, ALU.mult) \
                                .then_inc(dve_step, own.step())
                        else:
                            dve.wait_ge(*own.last(0))
                            nc.vector.scalar_tensor_tensor(CB[:, c, :], src, w, CB[:, c, :], ALU.mult, ALU.add) \
                                .then_inc(dve_step, own.step())
                elif kind == "bb":
                    dve.wait_ge(*own.last(1))
                    nc.vector.tensor_tensor(CB[:, c, :], CB[:, c, :], bank_[:, :], ALU.mult) \
                        .then_inc(b1.free.sem, own.event(b1.free, l, name))
                elif kind in ("bz", "az"):
                    i = [k for k, n in FILL.items() if n == name][0]
                    pre = PRE[:, (i + 1) % 2, :]
                    dve.wait_ge(b1.aux.sem, b1.aux.at(l, name))
                    dve.wait_ge(*own.last(0))
                    nc.vector.scalar_tensor_tensor(pre, TH, 1.0, bank_[:, :], ALU.add, ALU.mult) \
                        .then_inc(b1.free.sem, own.event(b1.free, l, name))
                    src, scale, tile = (CB, 0.5, 2 + c) if kind == "bz" else (CA, 0.25, c)
                    dve.wait_ge(*own.last(0))
                    nc.vector.scalar_tensor_tensor(pre, pre, scale, src[:, c, :], ALU.mult, ALU.mult) \
                        .then_inc(b1.pre.sem, own.event(b1.pre, l, "y" + name))
                    lo(b1, l, "y" + name, Y[1][:, tile, :], pre, Y[0][:, tile, :])
                elif kind == "cq":
                    dve.wait_ge(rope_in, 16 * l + 16)
                    rope(name, c)
                    lo(b1, l, name, AQ[1][:, c, :], PRE[:, c, :], AQ[0][:, c, :])
                elif name == "ck0":
                    rope(name, c)
                    dve.wait_ge(b1.hi.sem, b1.hi.at(l, "ck3"))
                    for g in range(2):
                        for half in range(2):
                            r = slice(g * HD, (g + 1) * HD)
                            lo(b1, l, f"ck{2 * g + half}", AK[1][half * HD:(half + 1) * HD, g, :],
                                      PRE[r, 0, :], AK[0][r, g, :])
                elif name == "ck1":
                    lo(b1, l, "cv", AV[1][:, :, 0:P], bank_[:, :].rearrange("p (t n) -> p t n", t=4),
                              AV[0][:, :, 0:P])

            def lo_y(i):
                h, half = (i % STEPS) // 2, i % 2
                r = slice(HD * (h % 2), HD * (h % 2) + HD)
                tile, cols = (6 if i < STEPS else 4) + h // 2, slice(half * 256, (half + 1) * 256)
                lo(b1, l, f"y{i}", Y[1][r, tile, cols], PRE[r, i % 2, 0:256], Y[0][r, tile, cols])

            for name in ("dq0", "dq1", "dk0", "dk1", "dv0", "dv1"):
                chunk(name)
            softmax_max(0)
            softmax_rest(0)
            chunk("dz0")
            chunk("dz1")
            for i in range(2 * STEPS):
                if i:
                    lo_y(i - 1)
                if i == STEPS:
                    for name in ("cq0", "cq1", "ck0", "ck1"):
                        chunk(name)
                    conv_a(TAPS["cz0"])
                    chunk("cz0")
                    softmax_max(i)
                    conv_a(2)
                    softmax_rest(i)
                    conv_a(TAPS["cz1"] - 2)
                    chunk("cz1")
                n = len(b1_keys(i))
                lo(b1, l, f"pt{i}a", PT1[1][:, 0:2, :], TB[0][:, :].rearrange("p (a n) -> p a n", a=2),
                          PT1[0][:, 0:2, :])
                lo(b1, l, f"pt{i}b", PT1[1][:, 2:n, :],
                          TB[1][:, 0:256 * (n - 2)].rearrange("p (a n) -> p a n", a=n - 2), PT1[0][:, 2:n, :])
                n_taps = TAPS.get(i, 0)
                if i % STEPS < STEPS - 1:
                    softmax_max(i + 1)
                    conv_a(n_taps // 4)
                    n_taps -= n_taps // 4
                    softmax_rest(i + 1)
                conv_a(n_taps)
                if i == LN_STEP:
                    mark(b1.acc, l, "mean")
                if i == LN_STEP + 4:
                    chunk(FILL[i - 1])
                if i in FILL and i != LN_STEP + 3:
                    chunk(FILL[i])
                if i == LN_STEP + 1:
                    dve.wait_ge(b1.ss.sem, b1.ss.at(l, "mean"))
                    for c in range(2):
                        dve.wait_ge(*own.last(1))
                        nc.vector.scalar_tensor_tensor(CA[:, c, :], NB[:, :], -1.0 / (2 * P), CA[:, c, :],
                                                       ALU.mult, ALU.add) \
                            .then_inc(dve_step, own.step())
                    dve.wait_ge(*own.last(1))
                    nc.vector.tensor_tensor(ACC1[:, :], CA[:, 0, :], CA[:, 0, :], ALU.mult) \
                        .then_inc(dve_step, own.step())
                    dve.wait_ge(*own.last(1))
                    nc.vector.tensor_tensor(PRE[:, 1, :], CA[:, 1, :], CA[:, 1, :], ALU.mult) \
                        .then_inc(dve_step, own.step())
                    dve.wait_ge(*own.last(0))
                    nc.vector.tensor_tensor(ACC1[:, :], ACC1[:, :], PRE[:, 1, :], ALU.add) \
                        .then_inc(b1.acc.sem, own.event(b1.acc, l, "var"))
                if i == LN_STEP + 2:
                    diagonals(b1, l, "var", spread=False)
                h, half = (i % STEPS) // 2, i % 2
                of = HD * (h % 2) if i < STEPS else HD * (h // 2)
                r = slice(HD * (h % 2), HD * (h % 2) + HD)
                dve.wait_ge(b1.pv.sem, b1.pv.at(l, str(i)))
                dve.wait_ge(*own.last(1))
                nc.vector.scalar_tensor_tensor(PRE[r, i % 2, 0:256], OB[of:of + HD, 0:256], 0.5, ZB[r, h // 2,
                                               half * 256:(half + 1) * 256], ALU.mult, ALU.mult) \
                    .then_inc(b1.pre.sem, own.event(b1.pre, l, f"y{i}"))
                if i == LN_STEP + 3:
                    dve.wait_ge(b1.bc.sem, b1.bc.at(l, "var"))
                    for c in range(2):
                        dve.wait_ge(*own.last(1))
                        nc.vector.tensor_tensor(CA[:, c, :], CA[:, c, :], NB[:, :], ALU.mult) \
                            .then_inc(dve_step, own.step())
                        dve.wait_ge(*own.last(0))
                        nc.vector.tensor_scalar(CA[:, c, :], CA[:, c, :], par("ln_g", c), par("ln_b", c),
                                                ALU.mult, ALU.add).then_inc(ln_in, own.reach(ln_in, 2 * l + (c + 1)))
                    for c in range(2):
                        dve.wait_ge(b1.aux.sem, b1.aux.at(l, f"ln{c}"))
                        dve.wait_ge(*own.last(1))
                        ins = nc.vector.scalar_tensor_tensor(CA[:, c, :], TMP[:, c, :], 1.0, CA[:, c, :],
                                                            ALU.add, ALU.mult)
                        if c:
                            ins.then_inc(ln_out, own.reach(ln_out, l + 1))
                        else:
                            ins.then_inc(dve_step, own.step())
            lo_y(2 * STEPS - 1)
            assert next(taps, None) is None
            mark(b1.layer, l, "end")
            for k in range(KT):
                name = f"o{k // 2}{k % 2}"
                dve.wait_ge(b1.done.sem, b1.done.at(l, name))
                dve.wait_ge(*own.last(0))
                nc.vector.tensor_tensor(X[:, k, :], X[:, k, :], G[k % 2][:, :], ALU.add) \
                    .then_inc(b1.free.sem, own.event(b1.free, l, name))
                squares(ACC1[:, :], X[:, k, :], k == 0, (b1.acc, l + 1) if k == KT - 1 else None)
                dve.wait_ge(*own.last(0))
                nc.vector.tensor_scalar(PRE[:, 0, :], X[:, k, :], PARF[:, k:k + 1], None, ALU.mult) \
                    .then_inc(dve_step, own.step())
                squares(ACCG, PRE[:, 0, :], k == 0)
            dve.wait_ge(*own.last(0))
            nc.vector.memset(spare_v[:, :], 0.0).then_inc(dve_step, own.step())
        own.leave(DEPTH)

        def final_norm(which):
            for k in range(KT):
                col = which * KT + k
                dve.wait_ge(*own.last(1))
                ins = nc.vector.scalar_tensor_tensor(X[:, k, :], X[:, k, :], PARF[:, col:col + 1], OB[:, :],
                                                     ALU.mult, ALU.mult)
                if which:
                    ins.then_inc(final.sem, own.event(final, 0, str(k)))
                else:
                    ins.then_inc(dve_step, own.step())

        diagonals(bf, 0, "n")
        dve.wait_ge(*own.last(0))
        nc.vector.tensor_tensor(ACC2, ACCG, OB[:, :], ALU.mult).then_inc(dve_step, own.step())
        dve.wait_ge(*own.last(0))
        nc.vector.tensor_tensor(ACC2, ACC2, OB[:, :], ALU.mult).then_inc(b2.acc.sem, own.event(b2.acc, 0, "n"))
        final_norm(0)

        with dve.Fori(0, DEPTH) as l:
            own.enter(l, DVE_STEPS_2)
            dve.wait_ge(par_in, 32 * l + 96)
            dve.wait_ge(*own.last(1))
            nc.vector.tensor_scalar(HB[:, 0:4], PAR2[:, P2["b_a"]:P2["b_a"] + 4], 0.5, None, ALU.mult) \
                .then_inc(dve_step, own.step())
            dve.wait_ge(*own.last(1))
            nc.vector.tensor_scalar(HB[:, 4:28], PAR2[:, P2["b_gate"]:P2["b_gate"] + 24], 0.5, None, ALU.mult) \
                .then_inc(dve_step, own.step())
            norm_to_h(b2, l, "n", "n", PAR2[:, P2["g_mix"]:P2["g_mix"] + KT])

            def par(name, k=0):
                return PAR2[:, P2[name] + k:P2[name] + k + 1]

            for n in range(2):
                dve.wait_ge(b2.done.sem, b2.done.at(l, f"kv{n}"))
                dve.wait_ge(*own.last(1))
                nc.vector.tensor_copy(GT[:, n, :], G[n][:, :]).then_inc(b2.free.sem, own.event(b2.free, l, f"kv{n}"))
            for n in range(2):
                squares(ACC2, GT[:, n, :], n == 0)
            mark(b2.acc, l, "kv")
            lam = PAR2[:, P2["lam"]:P2["lam"] + 2]
            dve.wait_ge(*own.last(1))
            nc.vector.scalar_tensor_tensor(LS[:, 0:2], lam, -1.0, lam, ALU.mult, ALU.max) \
                .then_inc(b2.lru.sem, own.event(b2.lru, l, "sp"))
            dve.wait_ge(b2.aux.sem, b2.aux.at(l, "sp"))
            dve.wait_ge(*own.last(1))
            nc.vector.tensor_scalar(LS[:, 4:6], LS[:, 2:4], 2.0, None, ALU.add).then_inc(dve_step, own.step())
            dve.wait_ge(*own.last(0))
            nc.vector.reciprocal(LS[:, 4:6], LS[:, 4:6]).then_inc(dve_step, own.step())
            dve.wait_ge(*own.last(0))
            nc.vector.tensor_tensor(LS[:, 4:6], LS[:, 4:6], LS[:, 2:4], ALU.mult).then_inc(dve_step, own.step())
            dve.wait_ge(*own.last(0))
            nc.vector.tensor_tensor(LS[:, 6:8], LS[:, 4:6], LS[:, 4:6], ALU.mult).then_inc(dve_step, own.step())
            dve.wait_ge(*own.last(1))
            nc.vector.memset(LS[:, 8:10], 1.0 / 17).then_inc(dve_step, own.step())
            for d in range(15, 0, -2):
                dve.wait_ge(*own.last(0))
                nc.vector.tensor_tensor(LS[:, 8:10], LS[:, 8:10], LS[:, 6:8], ALU.mult) \
                    .then_inc(dve_step, own.step())
                dve.wait_ge(*own.last(0))
                nc.vector.tensor_scalar(LS[:, 8:10], LS[:, 8:10], 1.0 / d, None, ALU.add) \
                    .then_inc(dve_step, own.step())
            dve.wait_ge(*own.last(0))
            nc.vector.tensor_tensor(LS[:, 8:10], LS[:, 8:10], LS[:, 4:6], ALU.mult).then_inc(dve_step, own.step())
            dve.wait_ge(*own.last(1))
            nc.vector.tensor_scalar(LS[:, 10:12], lam, -1.0, 0.0, ALU.mult, ALU.max).then_inc(dve_step, own.step())
            dve.wait_ge(*own.last(0))
            nc.vector.scalar_tensor_tensor(LS[:, 10:12], LS[:, 8:10], 2.0, LS[:, 10:12], ALU.mult, ALU.add) \
                .then_inc(dve_step, own.step())
            dve.wait_ge(*own.last(0))
            nc.vector.tensor_scalar(LS[:, 12:14], LS[:, 10:12], 4.0, None, ALU.mult).then_inc(dve_step, own.step())
            dve.wait_ge(*own.last(1))
            nc.vector.tensor_scalar(LS[:, 14:16], LS[:, 10:12], -4.0, None, ALU.mult) \
                .then_inc(ls_ready, own.reach(ls_ready, l + 1))

            def q_latent(k):
                dve.wait_ge(b2.hi.sem, b2.hi.at(l, f"l{k}"))
                dve.wait_ge(*own.last(1))
                nc.vector.tensor_copy(GT[:, 2 + k, :], G[k % 2][:, :]).then_inc(dve_step, own.step())
                dve.wait_ge(*own.last(0))
                nc.vector.scalar_tensor_tensor(lat(1, k), GT[:, 2 + k, :], par("g_lat", k), lat(0, k).bitcast(F32),
                                               ALU.mult, ALU.subtract) \
                    .then_inc(b2.lo.sem, own.event(b2.lo, l, f"l{k}"))
                squares(ACC2, GT[:, 2 + k, :], k == 0)
                if k == 2:
                    mark(b2.acc, l, "q")

            dve.wait_ge(b2.ss.sem, b2.ss.at(l, "kv"))
            q_latent(0)
            diagonals(b2, l, "kv")
            for k in (3, 4):
                dve.wait_ge(*own.last(1))
                nc.vector.scalar_tensor_tensor(PRE[:, k % 2, :], GT[:, k - 3, :], par("g_lat", k),
                                               NB[:, :], ALU.mult, ALU.mult) \
                    .then_inc(b2.pre.sem, own.event(b2.pre, l, f"l{k}"))
                lo(b2, l, f"l{k}", lat(1, k), PRE[:, k % 2, :], lat(0, k))
            q_latent(1)
            q_latent(2)
            dve.wait_ge(b2.done.sem, b2.done.at(l, "kr"))
            dve.wait_ge(*own.last(1))
            nc.vector.tensor_tensor(TMP[64:96, 0, :], G[1][64:96, :], CS2[64:96, :], ALU.mult) \
                .then_inc(dve_step, own.step())
            dve.wait_ge(*own.last(1))
            nc.vector.tensor_tensor(TMP[64:96, 1, :], G[1][96:128, :], CS2[96:128, :], ALU.mult) \
                .then_inc(b2.free.sem, own.event(b2.free, l, "kr"))
            dve.wait_ge(*own.last(0))
            nc.vector.tensor_tensor(PRE[64:96, 1, :], TMP[64:96, 0, :], TMP[64:96, 1, :], ALU.add) \
                .then_inc(b2.pre.sem, own.event(b2.pre, l, "kr"))
            diagonals(b2, l, "q")
            dve.wait_ge(*own.last(1))
            nc.vector.tensor_tensor(QS, CS2[:, :], NB[:, :], ALU.mult).then_inc(dve_step, own.step())
            dve.wait_ge(b2.hi.sem, b2.hi.at(l, "kr"))
            for a in range(2):
                dve.wait_ge(*own.last(1))
                ins = nc.vector.tensor_tensor(K2[1][64:96, a, :], PRE[64:96, 1, :], K2[0][64:96, a,
                                              :].bitcast(F32), ALU.subtract)
                if a:
                    ins.then_inc(b2.lo.sem, own.event(b2.lo, l, "kr"))
                else:
                    ins.then_inc(dve_step, own.step())
            dve.wait_ge(*own.last(1))
            nc.vector.memset(spare_v[:, :], 0.0).then_inc(dve_step, own.step())
            with dve.Fori(0, 2) as j:
                own.enter(j, DVE_STEPS_H)
                for jj in range(2):
                    def q_scale(a):
                        name = f"q{jj}{a}"
                        dve.wait_ge(b2.done.sem, b2.done.at(l, name, "h", j))
                        dve.wait_ge(*own.last(1))
                        nc.vector.tensor_tensor(PRE[0:64, a, :], G[a][0:64, :], QS[0:64, :], ALU.mult) \
                            .then_inc(dve_step, own.step())
                        dve.wait_ge(*own.last(1))
                        nc.vector.tensor_tensor(TMP[64:96, 0, :], G[a][64:96, :], QS[64:96, :], ALU.mult) \
                            .then_inc(dve_step, own.step())
                        dve.wait_ge(*own.last(1))
                        nc.vector.tensor_tensor(TMP[64:96, 1, :], G[a][96:128, :], QS[96:128, :], ALU.mult) \
                            .then_inc(b2.free.sem, own.event(b2.free, l, name, "h", j))
                        dve.wait_ge(*own.last(0))
                        nc.vector.tensor_tensor(PRE[64:96, a, :], TMP[64:96, 0, :], TMP[64:96, 1, :], ALU.add) \
                            .then_inc(b2.pre.sem, own.event(b2.pre, l, name, "h", j))

                    def q_lo(a):
                        lo(b2, l, f"q{jj}{a}", Q2[1][0:96, :], PRE[0:96, a, :], Q2[0][0:96, :], "h", j)

                    def softmax(s):
                        w = (256, 512)[s % 2]
                        masks = [MC[:, 384 - P * qb:384 - P * qb + w] for qb in (2 * (s % 2), 2 * (s % 2) + 1)]
                        row_max(b2, l, f"{jj}{s}", w, masks, 1.0, 96.0 ** -0.5, "h", j)
                        normalise(b2, l, f"{jj}{s}", w, None, "h", j)

                    def lo_y(s):
                        a, half = divmod(s, 2)
                        r = slice(a * HD, (a + 1) * HD)

                        def at(part):
                            return Y[part][r, bass.ds(2 * j + (2 + jj), 1), half * 256:(half + 1) * 256].rearrange(
                                "p a n -> p (a n)")

                        lo(b2, l, f"y{jj}{s}", at(1), OB[r, 0:256], at(0), "h", j)

                    q_scale(0)
                    q_lo(0)
                    for a in range(2):
                        lo(b2, l, f"k{jj}{a}", K2[1][0:64, a, :], G[1][a * 64:(a + 1) * 64, :],
                                  K2[0][0:64, a, :], "h", j)
                    lo(b2, l, f"v{jj}", V2[1][:, :, :], NB[:, :].rearrange("p (t n) -> p t n", t=4),
                              V2[0][:, :, :], "h", j)
                    softmax(0)
                    q_scale(1)
                    for s in range(4):
                        if s:
                            lo_y(s - 1)
                        for n in range(1 + s % 2):
                            lo(b2, l, f"pt{jj}{s}" + "ab"[n], PT2[1][:, 2 * n:2 * n + 2, :],
                                      TB[n][:, :].rearrange("p (a n) -> p a n", a=2),
                                      PT2[0][:, 2 * n:2 * n + 2, :], "h", j)
                        if s == 0:
                            q_lo(1)
                            softmax(1)
                        elif s < 3:
                            softmax(s + 1)
                    lo_y(3)
                dve.wait_ge(*own.last(1))
                nc.vector.memset(spare_v[:, :], 0.0).then_inc(dve_step, own.step())
            own.leave(2)

            for padded in (UP, SUMS):
                dve.wait_ge(*own.last(1))
                nc.vector.memset(padded[:, :, 0:POOLPAD], 0.0).then_inc(dve_step, own.step())

            def receive(name, tile):
                n = pools.index(name) % 2
                dve.wait_ge(b2.done.sem, b2.done.at(l, name, "mid"))
                dve.wait_ge(*own.last(1))
                nc.vector.tensor_copy(UP[:, tile, POOLPAD:], G[n][:, :]) \
                    .then_inc(b2.free.sem, own.event(b2.free, l, name, "mid"))

            for c in range(2):
                receive(f"lr{c}", c)
                for t in range(4):
                    src, w = UP[:, c, POOLPAD - 3 + t:POOLPAD - 3 + t + S], par("conv_w", 4 * c + t)
                    dve.wait_ge(*own.last(0))
                    if t == 0:
                        nc.vector.tensor_scalar(L[:, c, 0, :], src, w, par("conv_b", c), ALU.mult, ALU.add) \
                            .then_inc(dve_step, own.step())
                    elif t < 3:
                        nc.vector.scalar_tensor_tensor(L[:, c, 0, :], src, w, L[:, c, 0, :], ALU.mult, ALU.add) \
                            .then_inc(dve_step, own.step())
                    else:
                        nc.vector.scalar_tensor_tensor(L[:, c, 0, :], src, w, L[:, c, 0, :], ALU.mult, ALU.add) \
                            .then_inc(b2.pre.sem, own.event(b2.pre, l, f"uc{c}", "mid"))
                lo(b2, l, f"uc{c}", Y[1][:, 6 + c, :], L[:, c, 0, :], Y[0][:, 6 + c, :], "mid")
            size = S + POOLPAD
            A_, B_ = SUMS[:, 0, :], SUMS[:, 1, :]
            for c in range(2):
                receive(f"pl{c}", c)
                u = UP[:, c, :]

                def shifted(out, in_, by, rows=slice(0, P)):
                    dve.wait_ge(*own.last(0))
                    nc.vector.tensor_tensor(out[rows, POOLPAD:], in_[rows, POOLPAD:], in_[rows,
                                            POOLPAD - by:size - by], ALU.add) \
                        .then_inc(dve_step, own.step())

                shifted(A_, u, 1)
                shifted(B_, A_, 2)
                sums = [(A_, 2), (B_, 4)]
                if c:
                    shifted(A_, B_, 4)
                    shifted(B_, A_, 8, slice(64, P))
                    sums = [(A_, 8), (B_, 16)]
                for g, (sum_, w) in enumerate(sums):
                    r = slice(64 * g, 64 * g + 64)
                    dve.wait_ge(*own.last(1))
                    nc.vector.scalar_tensor_tensor(PRE[r, c, :], sum_[r, POOLPAD:], 1.0 / w, u[r,
                                                   POOLPAD:], ALU.mult, ALU.subtract) \
                        .then_inc(dve_step, own.step())
                    dve.wait_ge(*own.last(0))
                    nc.vector.tensor_tensor(PRE[r, c, 0:POOLPAD], sum_[r, POOLPAD:2 * POOLPAD], IC[r, c,
                                            :], ALU.mult) \
                        .then_inc(dve_step, own.step())
                    dve.wait_ge(*own.last(0))
                    ins = nc.vector.tensor_tensor(PRE[r, c, 0:POOLPAD], PRE[r, c, 0:POOLPAD], u[r,
                                                  POOLPAD:2 * POOLPAD], ALU.subtract)
                    if g:
                        ins.then_inc(b2.pre.sem, own.event(b2.pre, l, f"pm{c}", "mid"))
                    else:
                        ins.then_inc(dve_step, own.step())
            for c in range(2):
                dve.wait_ge(b2.aux.sem, b2.aux.at(l, f"sq{c}", "mid"))
                dve.wait_ge(*own.last(1))
                nc.vector.scalar_tensor_tensor(L[:, c, 3, :], L[:, c, 1, :], 1.0, L[:, c, 3, :], ALU.add, ALU.mult) \
                    .then_inc(b2.lru.sem, own.event(b2.lru, l, f"c{c}"))
                dve.wait_ge(*own.last(1))
                nc.vector.scalar_tensor_tensor(L[:, c, 2, :], L[:, c, 2, :], 1.0, L[:, c, 0, :], ALU.add, ALU.mult) \
                    .then_inc(dve_step, own.step())
            for c in range(2):
                lo(b2, l, f"pm{c}", Y[1][:, c, :], PRE[:, c, :], Y[0][:, c, :], "mid")
            for c in range(2):
                dve.wait_ge(b2.aux.sem, b2.aux.at(l, f"rt{c}", "mid"))
                dve.wait_ge(*own.last(1))
                nc.vector.scalar_tensor_tensor(L[:, c, 2, :], L[:, c, 2, :], 0.5, L[:, c, 1, :], ALU.mult, ALU.mult) \
                    .then_inc(dve_step, own.step())
                dve.wait_ge(*own.last(0))
                nc.vector.tensor_tensor_scan(PRE[:, c, :], L[:, c, 4, :], L[:, c, 2, :], 0.0, ALU.mult, ALU.add) \
                    .then_inc(b2.pre.sem, own.event(b2.pre, l, f"lh{c}", "mid"))
            for c in range(2):
                lo(b2, l, f"lh{c}", Y[1][:, 6 + c, :], PRE[:, c, :], Y[0][:, 6 + c, :], "mid")
            for c in range(2):
                dve.wait_ge(b2.sm.sem, b2.sm.at(l, f"p{c}"))
                dve.wait_ge(*own.last(1))
                nc.vector.tensor_scalar(PRE[:, c, :], SC[c][:, :], par("scale", c), None, ALU.mult) \
                    .then_inc(b2.pre.sem, own.event(b2.pre, l, f"py{c}", "mid"))
            for c in range(2):
                lo(b2, l, f"py{c}", Y[1][:, c, :], PRE[:, c, :], Y[0][:, c, :], "mid")
            dve.wait_ge(*own.last(1))
            nc.vector.memset(spare_v[:, :], 0.0).then_inc(dve_step, own.step())

            def merged(seg, i, gates_at, tile):
                for c in range(2):
                    A_, B_, C_ = ((SC[0], TB[0], SC[1]), (TB[1], OB, NB))[c]
                    dve.wait_ge(b2.br.sem, b2.br.at(l, str(c), seg, i))
                    dve.wait_ge(b2.aux.sem, gates_at(c))

                    def gate(g):
                        return GT[:, bass.ds(tile + (8 * g + c), 1), :].rearrange("p a n -> p (a n)")

                    dve.wait_ge(*own.last(1))
                    nc.vector.scalar_tensor_tensor(TMP[:, 0, :], gate(0), 1.0, A_[:, :], ALU.add, ALU.mult) \
                        .then_inc(dve_step, own.step())
                    dve.wait_ge(*own.last(1))
                    nc.vector.scalar_tensor_tensor(TMP[:, 1, :], gate(1), 1.0, B_[:, :], ALU.add, ALU.mult) \
                        .then_inc(dve_step, own.step())
                    dve.wait_ge(*own.last(0))
                    nc.vector.tensor_tensor(TMP[:, 0, :], TMP[:, 0, :], TMP[:, 1, :], ALU.add) \
                        .then_inc(dve_step, own.step())
                    dve.wait_ge(*own.last(0))
                    nc.vector.scalar_tensor_tensor(TMP[:, 1, :], PR[:, c, :], 1.0, C_[:, :], ALU.add, ALU.mult) \
                        .then_inc(b2.brf.sem, own.event(b2.brf, l, str(c), seg, i))
                    dve.wait_ge(*own.last(0))
                    nc.vector.tensor_tensor(PRE[:, c, :], TMP[:, 0, :], TMP[:, 1, :], ALU.add) \
                        .then_inc(b2.pre.sem, own.event(b2.pre, l, f"b{c}", seg, i))

                    def at(part):
                        return MRG[part][:, bass.ds(tile + c, 1), :].rearrange("p a n -> p (a n)")

                    lo(b2, l, f"b{c}", at(1), PRE[:, c, :], at(0), seg, i, half=True)

            with dve.Fori(0, 3) as m:
                own.enter(m, DVE_STEPS_M)
                merged("m", m, lambda c: b2.aux.at(l, f"t{c}", "m", m) - 2, 2 * m)
                dve.wait_ge(*own.last(1))
                nc.vector.memset(spare_v[:, :], 0.0).then_inc(dve_step, own.step())
            own.leave(3)
            merged("m3", 0, lambda c: b2.aux.at(l, f"t{c}", "m", 2), 6)
            for k in range(KT):
                dve.wait_ge(b2.done.sem, b2.done.at(l, f"o{k}", "out"))
                dve.wait_ge(*own.last(1))
                nc.vector.tensor_tensor(X[:, k, :], X[:, k, :], G[k % 2][:, :], ALU.add) \
                    .then_inc(b2.free.sem, own.event(b2.free, l, f"o{k}", "out"))
                dve.wait_ge(*own.last(0))
                square = PRE[:, 1, :] if k else ACC2
                nc.vector.tensor_tensor(square, X[:, k, :], X[:, k, :], ALU.mult).then_inc(dve_step, own.step())
                dve.wait_ge(b2.hi.sem, b2.hi.at(l, f"e{k}", "n2"))
                dve.wait_ge(*own.last(1))
                nc.vector.scalar_tensor_tensor(H[1][:, k, :], X[:, k, :], par("g_ffn", k), H[0][:, k, :].bitcast(F32),
                                               ALU.mult, ALU.subtract) \
                    .then_inc(b2.lo.sem, own.event(b2.lo, l, f"e{k}", "n2"))
                if k:
                    dve.wait_ge(*own.last(1))
                    nc.vector.tensor_tensor(ACC2, ACC2, PRE[:, 1, :], ALU.add).then_inc(dve_step, own.step())
            mark(b2.acc, l, "e")
            mark(b2.layer, l, "end")
            spread_scale(b2, l, "e")
            dve.wait_ge(*own.last(1))
            nc.vector.memset(spare_v[:, :], 0.0).then_inc(dve_step, own.step())

            def up(seg, i):
                for n in range(KT):
                    dve.wait_ge(b2.aux.sem, b2.aux.at(l, f"u{n}", seg, i))
                    dve.wait_ge(*own.last(1))
                    nc.vector.tensor_tensor(PRE[:, n % 2, :], TMP[:, n % 2, :], TMP[:, n % 2, :], ALU.mult) \
                        .then_inc(b2.pre.sem, own.event(b2.pre, l, f"u{n}", seg, i))
                    lo(b2, l, f"u{n}", Y[1][:, n, :], PRE[:, n % 2, :], Y[0][:, n, :], seg, i)

            def down(seg, i, ready=None):
                for n in range(KT):
                    dve.wait_ge(b2.done.sem, b2.done.at(l, f"d{n}", seg, i))
                    dve.wait_ge(*own.last(1))
                    nc.vector.tensor_tensor(PR[:, 1, :], G[n % 2][:, :], RB, ALU.mult) \
                        .then_inc(b2.free.sem, own.event(b2.free, l, f"d{n}", seg, i))
                    dve.wait_ge(*own.last(0))
                    nc.vector.tensor_tensor(X[:, n, :], X[:, n, :], PR[:, 1, :], ALU.add) \
                        .then_inc(dve_step, own.step())
                    squares(ACC2, X[:, n, :], n == 0, ready if n == KT - 1 else None)

            up("f0", 0)
            dve.wait_ge(b2.bc.sem, b2.bc.at(l, "e"))
            dve.wait_ge(*own.last(1))
            nc.vector.tensor_copy(RB, NB[:, :]).then_inc(dve_step, own.step())
            with dve.Fori(0, 3) as f:
                own.enter(f, DVE_STEPS_F)
                down("f", f)
                up("f", f)
                dve.wait_ge(*own.last(1))
                nc.vector.memset(spare_v[:, :], 0.0).then_inc(dve_step, own.step())
            own.leave(3)
            down("f3", 0, (b2.acc, l + 1))
            dve.wait_ge(*own.last(0))
            nc.vector.memset(spare_v[:, :], 0.0).then_inc(dve_step, own.step())
        own.leave(DEPTH)
        diagonals(bf, 1, "n")
        final_norm(1)


def tables():
    f = np.float32
    t = np.arange(S, dtype=f)
    inv = (f(10000.0) ** (-np.arange(0, HD, 2, dtype=f) / f(HD))).astype(f)
    ang = (t[None, :] * inv[:, None]).astype(f)
    cos, sin = np.cos(ang), np.sin(ang)
    rope1 = np.concatenate([np.concatenate([cos] * 4, 0), np.concatenate([sin, -sin] * 2, 0)], 1).astype(f)
    inv = (f(10000.0) ** (-np.arange(0, 32, 2, dtype=f) / f(32))).astype(f)
    ang = (t[None, :] * inv[:, None]).astype(f)
    cos, sin = np.cos(ang), np.sin(ang)
    rope2 = np.concatenate([np.ones((64, S), f), cos, cos, -sin, sin], 0).astype(f)
    q, k = np.arange(P)[:, None], np.arange(640)[None, :]
    window = np.where(np.abs(k - 256 - q) <= 128, 0.0, NEG).astype(f)
    causal = np.where(k - 384 <= q, 0.0, NEG).astype(f)
    c, kc = np.arange(GRID)[:, None], np.arange(GRID)[None, :]
    c0 = np.clip(c - 8, 0, GRID - 16)
    columns = np.where((kc >= c0) & (kc < c0 + 16), 0.0, NEG).astype(f)
    columns = np.concatenate([columns] * 2, 0)
    counts = np.zeros((P, 2, POOLPAD), f)
    for n, w in enumerate((2, 4, 8, 16)):
        counts[64 * (n % 2):64 * (n % 2) + 64, n // 2, :] = 1.0 / np.minimum(np.arange(POOLPAD) + 1, w)
    return {"rope1": rope1, "rope2": rope2, "window": window, "causal": causal, "columns": columns,
            "counts": counts, "ident": np.eye(P, dtype=f)}


def unit_of(w, col, width=256):
    kt = w.shape[0] // P
    out = np.zeros((P, KT, 256), np.float32)
    out[:, 0:kt, 0:width] = w[:, col:col + width].reshape(kt, P, width).transpose(1, 0, 2)
    return out.reshape(P, 2048)


def pack_stream(a):
    units = []
    for l in range(DEPTH):
        for u in B1_UNITS[:14]:
            units.append(unit_of(a["w_in"][l], B1_COLS[u]))
        for m in range(4):
            units.append(unit_of(a["w_out"][l], 256 * m))
    for l in range(DEPTH):
        w, q_up, kv_up = a["w_in_2"][l], a["w_q_up_2"][l], a["w_kv_up_2"][l]
        units.append(unit_of(w, 640))
        units.append(unit_of(w, 256))
        kr = w[:, 896:928]
        units.append(unit_of(np.concatenate([w[:, 512:640], np.zeros((D, 64), np.float32), kr,
                                             kr[:, 16:32], kr[:, 0:16]], 1), 0))
        for pair in range(4):
            q = []
            for h in (2 * pair, 2 * pair + 1):
                c = q_up[:, 96 * h:96 * h + 96]
                q += [c, c[:, 80:96], c[:, 64:80]]
            heads = [kv_up[:, P * h:P * h + P] for h in (2 * pair, 2 * pair + 1)]
            kv = np.concatenate([heads[0][:, 0:64], heads[1][:, 0:64], heads[0][:, 64:], heads[1][:, 64:]], 1)
            units.append(unit_of(np.concatenate([np.concatenate(q, 1), kv], 0), 0))
            for g in range(2):
                units.append(unit_of(w, 1184 + 1024 * g + 256 * pair))
        units.append(unit_of(w, 928))
        units.append(unit_of(w, 0))
        small = np.zeros((KT * P, P), np.float32)
        for n, name in enumerate(("w_pool_grp_2", "w_lru_a_2", "w_lru_x_2")):
            for g in range(4):
                at = (2 * n + g // 2) * P + 64 * (g % 2)
                small[at:at + 64, 64 * (g % 2):64 * (g % 2) + 64] = a[name][l][g]
        units.append(unit_of(small, 0, P))
        branches = np.concatenate([a["w_pool_proj_2"][l], a["w_mla_o_2"][l], a["w_lru_proj_2"][l]], 0)
        for m in range(4):
            units.append(unit_of(w, 1184 + 2048 + 256 * m))
            units.append(unit_of(branches, 256 * m))
        for m in range(4):
            units.append(unit_of(a["w_out_2"][l], 256 * m))
        for g in range(4):
            for m in range(4):
                units.append(unit_of(a["w_ff1_2"][l], 1024 * g + 256 * m))
            for m in range(4):
                units.append(unit_of(a["w_ff2_2"][l][1024 * g:1024 * (g + 1)], 256 * m))
    return np.stack(units)


def columns_of(x):
    return x.reshape(-1, P).T


def pack_params(a):
    par1, par2 = [], []
    for l in range(DEPTH):
        taps_a = a["conv_a_w"][l].reshape(CONV_A, 2, P).transpose(2, 1, 0).reshape(P, -1)
        taps_b = a["conv_b_w"][l].reshape(3, 2, P).transpose(2, 1, 0).reshape(P, -1)
        par1.append(np.concatenate([columns_of(a["norm_g"][l]), taps_a, columns_of(a["conv_a_b"][l]),
                                    columns_of(a["ln_a_g"][l]), columns_of(a["ln_a_b"][l]), taps_b,
                                    np.tile(a["swa_sink"][l][None, :], (P, 1))], 1))
        taps = a["conv_w_2"][l].reshape(4, 2, P).transpose(2, 1, 0).reshape(P, -1)
        par2.append(np.concatenate([columns_of(a["g_mix_2"][l]), columns_of(a["pool_scale_2"][l]),
                                    columns_of(a["g_q_2"][l]), columns_of(a["g_kv_2"][l]), taps,
                                    columns_of(a["conv_b_2"][l]), columns_of(a["b_lru_a_2"][l]),
                                    columns_of(a["b_lru_x_2"][l]), columns_of(a["lru_lambda_2"][l]),
                                    columns_of(a["b_gate_2"][l]), columns_of(a["g_ffn_2"][l])], 1))
    return np.stack(par1), np.stack(par2)


def slide_bias(rpb):
    flat = rpb.reshape(-1, 15, 31)
    wide = np.pad(flat, ((0, 0), (0, 0), (GRID - 16, GRID - 16)))
    out = np.stack([np.stack([wide[:, 1 - r:15 - r, GRID - 1 - cq:2 * GRID - 1 - cq] for cq in range(GRID)], 1)
                    for r in range(2)], 1)
    return out.reshape(-1, P, 14 * GRID)


def kernel(**inputs):
    import concourse.bacc as bacc
    from concourse.bass_utils import run_bass_kernel_spmd

    a = {k: np.asarray(v) for k, v in inputs.items()}
    arrays = dict(tables())
    arrays["x"] = np.ascontiguousarray(a["x"][0].T.reshape(KT, P, S).transpose(1, 0, 2))
    arrays["stream"] = pack_stream(a)
    arrays["par1"], arrays["par2"] = pack_params(a)
    arrays["finals"] = np.concatenate([columns_of(a["final_norm_g"]), columns_of(a["g_final_2"])], 1)
    arrays["bias"] = slide_bias(a["na_rpb"])
    nc = bacc.Bacc("TRN2", target_bir_lowering=False, num_devices=1)
    dram, feed = {}, {}
    for name, value in arrays.items():
        value = np.ascontiguousarray(value)
        feed[f"in_{name}"] = value
        dram[name] = nc.dram_tensor(f"in_{name}", value.shape, mybir.dt.from_np(value.dtype),
                                    kind="ExternalInput").ap()
    dram["out"] = nc.dram_tensor("out_0", (P, KT, S), F32, kind="ExternalOutput").ap()
    build(nc, dram)
    r = run_bass_kernel_spmd(nc, [feed], core_ids=[0])
    out = r.results[0]["out_0"]
    return np.ascontiguousarray(out.transpose(2, 1, 0).reshape(1, S, D))
```
